# Optimizing a Trainium2 kernel written in Bass

```python
import jax, jax.numpy as jnp
from jax import lax
import numpy as np

D_MODEL = 1024
BATCH = 1
SEQ = 256
DEPTH = 2

GRID_W = 64
CTX_LEN = 256
N_MIXERS = 4
Q_BLOCK = 128
ROPE_THETA = 10000.0
NORM_EPS = 1e-6
CONV_WIDTH = 31
CONV_PAD = CONV_WIDTH // 2
GQA_HEADS = 16
GQA_KV_HEADS = 4
GQA_GROUP = GQA_HEADS // GQA_KV_HEADS
GQA_HEAD_DIM = D_MODEL // GQA_HEADS
POOL_WINDOWS = (2, 4, 8, 16)
POOL_GROUP = D_MODEL // len(POOL_WINDOWS)
MLA_HEADS = 16
MLA_NOPE = 64
MLA_ROPE = 32
MLA_V = 64
MLA_QK = MLA_NOPE + MLA_ROPE
MLA_Q_LORA = 768
MLA_KV_LORA = 256
D_FF = 4 * D_MODEL
N_CONV = (DEPTH + 3) // N_MIXERS
N_GQA = (DEPTH + 2) // N_MIXERS
N_POOL = (DEPTH + 1) // N_MIXERS
N_MLA = DEPTH // N_MIXERS


def rms_norm(x, g):
    xf = x.astype(jnp.float32)
    y = xf * lax.rsqrt(jnp.mean(xf * xf, axis=-1, keepdims=True) + NORM_EPS)
    return (y * g.astype(jnp.float32)).astype(x.dtype)

def layer_norm(x, g, b):
    xf = x.astype(jnp.float32)
    mu = jnp.mean(xf, axis=-1, keepdims=True)
    var = jnp.mean(jnp.square(xf - mu), axis=-1, keepdims=True)
    y = (xf - mu) * lax.rsqrt(var + NORM_EPS)
    return (y * g.astype(jnp.float32) + b.astype(jnp.float32)).astype(x.dtype)

def modulate(h, shift, scale):
    return h * (1 + scale[..., None, :]) + shift[..., None, :]

def axial_tables(row, col, rot_dim):
    quarter = rot_dim // 4
    inv = ROPE_THETA ** (-jnp.arange(quarter, dtype=jnp.float32) / quarter)
    ang_r = row[:, None] * inv
    ang_c = col[:, None] * inv
    return (jnp.cos(ang_r), jnp.sin(ang_r), jnp.cos(ang_c), jnp.sin(ang_c))

def _rotate(v, cos, sin):
    a, b = jnp.split(v, 2, axis=-1)
    cos = cos.astype(v.dtype)
    sin = sin.astype(v.dtype)
    return jnp.concatenate([a * cos - b * sin, b * cos + a * sin], axis=-1)

def apply_axial_rope(x, tables):
    cr, sr, cc, sc = tables
    xr, xc = jnp.split(x, 2, axis=-1)
    return jnp.concatenate([_rotate(xr, cr, sr), _rotate(xc, cc, sc)], axis=-1)

def softmax_attend(q, k, v):
    s = jnp.einsum('bkgqd,bkld->bkgql', q, k).astype(jnp.float32) * (q.shape[-1] ** -0.5)
    p = jax.nn.softmax(s, axis=-1).astype(v.dtype)
    return jnp.einsum('bkgql,bkld->bkgqd', p, v)

def blocked_attend(q, k, v):
    b, kh, g, t, dq = q.shape
    nb = t // Q_BLOCK
    qb = q.reshape(b, kh, g, nb, Q_BLOCK, dq).transpose(3, 0, 1, 2, 4, 5)
    out = lax.map(lambda qq: softmax_attend(qq, k, v), qb)
    return out.transpose(1, 2, 3, 0, 4, 5).reshape(b, kh, g, t, v.shape[-1])

def merge_heads(o):
    b, kh, g, t, dv = o.shape
    return o.transpose(0, 3, 1, 2, 4).reshape(b, t, kh * g * dv)

def conv_module(h, w_pw1, w_dw, b_dw, ln_g, ln_b, w_pw2):
    u = h @ w_pw1
    a, gate = jnp.split(u, 2, axis=-1)
    u = a * jax.nn.sigmoid(gate)
    u = lax.conv_general_dilated(
        u, w_dw[:, None, :].astype(u.dtype), window_strides=(1,),
        padding=[(CONV_PAD, CONV_PAD)], dimension_numbers=('NWC', 'WIO', 'NWC'),
        feature_group_count=D_MODEL) + b_dw
    u = jax.nn.silu(layer_norm(u, ln_g, ln_b))
    return u @ w_pw2

def gqa_project(h, w_qkv, q_norm, k_norm):
    b, t, _ = h.shape
    nq = GQA_HEADS * GQA_HEAD_DIM
    nk = GQA_KV_HEADS * GQA_HEAD_DIM
    qkv = h @ w_qkv
    q = qkv[..., :nq].reshape(b, t, GQA_KV_HEADS, GQA_GROUP, GQA_HEAD_DIM).transpose(0, 2, 3, 1, 4)
    k = qkv[..., nq:nq + nk].reshape(b, t, GQA_KV_HEADS, GQA_HEAD_DIM).transpose(0, 2, 1, 3)
    v = qkv[..., nq + nk:].reshape(b, t, GQA_KV_HEADS, GQA_HEAD_DIM).transpose(0, 2, 1, 3)
    return rms_norm(q, q_norm), rms_norm(k, k_norm), v

def gqa_mixer(hl, hc, w_qkv, q_norm, k_norm, w_o, tables, with_ctx):
    ql, kl, vl = gqa_project(hl, w_qkv, q_norm, k_norm)
    qc, kc, vc = gqa_project(hc, w_qkv, q_norm, k_norm)
    ql = apply_axial_rope(ql, tables)
    kl = apply_axial_rope(kl, tables)
    k_all = jnp.concatenate([kc, kl], axis=2)
    v_all = jnp.concatenate([vc, vl], axis=2)
    ol = merge_heads(blocked_attend(ql, k_all, v_all)) @ w_o
    oc = merge_heads(softmax_attend(qc, kc, vc)) @ w_o if with_ctx else None
    return ol, oc

def pool_mixer(h, w_pool, scale):
    b, t, _ = h.shape
    hf = h.astype(jnp.float32)
    cs = jnp.concatenate([jnp.zeros((b, 1, D_MODEL), jnp.float32), jnp.cumsum(hf, axis=1)], axis=1)
    pos = jnp.arange(t)
    outs = []
    for g, w in enumerate(POOL_WINDOWS):
        lo = jnp.clip(pos - w // 2, 0, t)
        hi = jnp.clip(pos + w - w // 2, 0, t)
        csg = cs[..., g * POOL_GROUP:(g + 1) * POOL_GROUP]
        win = jnp.take(csg, hi, axis=1) - jnp.take(csg, lo, axis=1)
        cnt = (hi - lo).astype(jnp.float32)[:, None]
        outs.append(win / cnt - hf[..., g * POOL_GROUP:(g + 1) * POOL_GROUP])
    p = jnp.stack(outs, axis=2).astype(h.dtype)
    y = jnp.einsum('btgc,gcd->btgd', p, w_pool).reshape(b, t, D_MODEL)
    return y * scale

def mla_project(h, w_dq, q_lora_norm, w_uq, w_dkv, kv_lora_norm, w_ukv, q_norm, k_norm):
    b, t, _ = h.shape
    cq = rms_norm(h @ w_dq, q_lora_norm)
    q = (cq @ w_uq).reshape(b, t, MLA_HEADS, MLA_QK).transpose(0, 2, 1, 3)
    dkv = h @ w_dkv
    ckv = rms_norm(dkv[..., :MLA_KV_LORA], kv_lora_norm)
    k_rope = dkv[..., MLA_KV_LORA:]
    kv = (ckv @ w_ukv).reshape(b, t, MLA_HEADS, MLA_NOPE + MLA_V).transpose(0, 2, 1, 3)
    k_nope, v = kv[..., :MLA_NOPE], kv[..., MLA_NOPE:]
    k = jnp.concatenate([k_nope, jnp.broadcast_to(k_rope[:, None], (b, MLA_HEADS, t, MLA_ROPE))], axis=-1)
    return rms_norm(q, q_norm), rms_norm(k, k_norm), v

def rope_tail(x, tables):
    return jnp.concatenate([x[..., :MLA_NOPE], apply_axial_rope(x[..., MLA_NOPE:], tables)], axis=-1)

def mla_mixer(hl, hc, w_dq, q_lora_norm, w_uq, w_dkv, kv_lora_norm, w_ukv, q_norm, k_norm, w_o,
              tables, with_ctx):
    args = (w_dq, q_lora_norm, w_uq, w_dkv, kv_lora_norm, w_ukv, q_norm, k_norm)
    ql, kl, vl = mla_project(hl, *args)
    qc, kc, vc = mla_project(hc, *args)
    ql = rope_tail(ql, tables)[:, :, None]
    kl = rope_tail(kl, tables)
    k_all = jnp.concatenate([kc, kl], axis=2)
    v_all = jnp.concatenate([vc, vl], axis=2)
    ol = merge_heads(blocked_attend(ql, k_all, v_all)) @ w_o
    oc = merge_heads(softmax_attend(qc[:, :, None], kc, vc)) @ w_o if with_ctx else None
    return ol, oc

def sq_relu_mlp(h, w1, w2):
    return jnp.square(jax.nn.relu(h @ w1)) @ w2

def first_inputs(seed: int = 0) -> dict:
    key = jax.random.key(seed)
    ks = jax.random.split(key, 31)
    f32 = jnp.float32

    def nrm(k, shape, scale):
        return jax.random.normal(k, shape, f32) * scale

    def gain(k, shape):
        return 1.0 + 0.05 * jax.random.normal(k, shape, f32)

    d = D_MODEL
    return {
        'x': nrm(ks[0], (BATCH, SEQ, d), 1.0),
        'c': nrm(ks[1], (BATCH, d), 1.0),
        'ctx': nrm(ks[2], (BATCH, CTX_LEN, d), 1.0),
        'c_ctx': nrm(ks[3], (d,), 1.0),
        'norm1_g': gain(ks[4], (DEPTH, d)),
        'norm2_g': gain(ks[5], (DEPTH, d)),
        'w_mod': nrm(ks[6], (DEPTH, d, 6 * d), 0.5 * d ** -0.5),
        'b_mod': nrm(ks[7], (DEPTH, 6 * d), 0.02),
        'w_ff1': nrm(ks[8], (DEPTH, d, D_FF), d ** -0.5),
        'w_ff2': nrm(ks[9], (DEPTH, D_FF, d), D_FF ** -0.5),
        'conv_w_pw1': nrm(ks[10], (N_CONV, d, 2 * d), d ** -0.5),
        'conv_w_dw': nrm(ks[11], (N_CONV, CONV_WIDTH, d), CONV_WIDTH ** -0.5),
        'conv_b_dw': nrm(ks[12], (N_CONV, d), 0.02),
        'conv_ln_g': gain(ks[13], (N_CONV, d)),
        'conv_ln_b': nrm(ks[14], (N_CONV, d), 0.02),
        'conv_w_pw2': nrm(ks[15], (N_CONV, d, d), d ** -0.5),
        'gqa_w_qkv': nrm(ks[16], (N_GQA, d, (GQA_HEADS + 2 * GQA_KV_HEADS) * GQA_HEAD_DIM), d ** -0.5),
        'gqa_q_norm': gain(ks[17], (N_GQA, GQA_HEAD_DIM)),
        'gqa_k_norm': gain(ks[18], (N_GQA, GQA_HEAD_DIM)),
        'gqa_w_o': nrm(ks[19], (N_GQA, GQA_HEADS * GQA_HEAD_DIM, d), (GQA_HEADS * GQA_HEAD_DIM) ** -0.5),
        'pool_w': nrm(ks[20], (N_POOL, len(POOL_WINDOWS), POOL_GROUP, POOL_GROUP), POOL_GROUP ** -0.5),
        'pool_scale': gain(ks[21], (N_POOL, d)),
        'mla_w_dq': nrm(ks[22], (N_MLA, d, MLA_Q_LORA), d ** -0.5),
        'mla_q_lora_norm': gain(ks[23], (N_MLA, MLA_Q_LORA)),
        'mla_w_uq': nrm(ks[24], (N_MLA, MLA_Q_LORA, MLA_HEADS * MLA_QK), MLA_Q_LORA ** -0.5),
        'mla_w_dkv': nrm(ks[25], (N_MLA, d, MLA_KV_LORA + MLA_ROPE), d ** -0.5),
        'mla_kv_lora_norm': gain(ks[26], (N_MLA, MLA_KV_LORA)),
        'mla_w_ukv': nrm(ks[27], (N_MLA, MLA_KV_LORA, MLA_HEADS * (MLA_NOPE + MLA_V)), MLA_KV_LORA ** -0.5),
        'mla_q_norm': gain(ks[28], (N_MLA, MLA_QK)),
        'mla_k_norm': gain(ks[29], (N_MLA, MLA_QK)),
        'mla_w_o': nrm(ks[30], (N_MLA, MLA_HEADS * MLA_V, d), (MLA_HEADS * MLA_V) ** -0.5),
    }

def first_block(x, c, ctx, c_ctx, norm1_g, norm2_g, w_mod, b_mod, w_ff1, w_ff2,
              conv_w_pw1, conv_w_dw, conv_b_dw, conv_ln_g, conv_ln_b, conv_w_pw2,
              gqa_w_qkv, gqa_q_norm, gqa_k_norm, gqa_w_o, pool_w, pool_scale,
              mla_w_dq, mla_q_lora_norm, mla_w_uq, mla_w_dkv, mla_kv_lora_norm, mla_w_ukv,
              mla_q_norm, mla_k_norm, mla_w_o):
    seq = x.shape[1]
    rows = seq // GRID_W
    row_ids = jnp.repeat(jnp.arange(rows, dtype=jnp.float32), GRID_W)
    col_ids = jnp.tile(jnp.arange(GRID_W, dtype=jnp.float32), rows)
    tab_gqa = axial_tables(row_ids, col_ids, GQA_HEAD_DIM)
    tab_mla = axial_tables(row_ids, col_ids, MLA_ROPE)

    sc = jax.nn.silu(c)
    scc = jax.nn.silu(c_ctx)
    xl, xc = x, ctx
    for i in range(DEPTH):
        m = i % N_MIXERS
        j = i // N_MIXERS
        with_ctx = i < DEPTH - 1
        mod_l = jnp.split(sc @ w_mod[i] + b_mod[i], 6, axis=-1)
        mod_c = jnp.split(scc @ w_mod[i] + b_mod[i], 6, axis=-1)

        hl = modulate(rms_norm(xl, norm1_g[i]), mod_l[0], mod_l[1])
        hc = modulate(rms_norm(xc, norm1_g[i]), mod_c[0], mod_c[1])
        if m == 0:
            cargs = (conv_w_pw1[j], conv_w_dw[j], conv_b_dw[j], conv_ln_g[j], conv_ln_b[j], conv_w_pw2[j])
            ol = conv_module(hl, *cargs)
            oc = conv_module(hc, *cargs) if with_ctx else None
        elif m == 1:
            ol, oc = gqa_mixer(hl, hc, gqa_w_qkv[j], gqa_q_norm[j], gqa_k_norm[j], gqa_w_o[j],
                               tab_gqa, with_ctx)
        elif m == 2:
            ol = pool_mixer(hl, pool_w[j], pool_scale[j])
            oc = pool_mixer(hc, pool_w[j], pool_scale[j]) if with_ctx else None
        else:
            ol, oc = mla_mixer(hl, hc, mla_w_dq[j], mla_q_lora_norm[j], mla_w_uq[j], mla_w_dkv[j],
                               mla_kv_lora_norm[j], mla_w_ukv[j], mla_q_norm[j], mla_k_norm[j],
                               mla_w_o[j], tab_mla, with_ctx)
        xl = xl + mod_l[2][:, None, :] * ol
        if with_ctx:
            xc = xc + mod_c[2] * oc

        hl = modulate(rms_norm(xl, norm2_g[i]), mod_l[3], mod_l[4])
        xl = xl + mod_l[5][:, None, :] * sq_relu_mlp(hl, w_ff1[i], w_ff2[i])
        if with_ctx:
            hc = modulate(rms_norm(xc, norm2_g[i]), mod_c[3], mod_c[4])
            xc = xc + mod_c[5] * sq_relu_mlp(hc, w_ff1[i], w_ff2[i])
    return xl


MEM_LEN = 256
EPS = 1e-6
N_NORMS = 8
D_FF_2 = 2816
RW_HEADS = 8
RW_HEAD_DIM = 64
RW_WIDTH = RW_HEADS * RW_HEAD_DIM
RW_DECAY_RANK = 64
RW_AAA_RANK = 64
RW_GATE_RANK = 128
RW_LN_EPS = 64e-5
RW_SIZES = (RW_WIDTH, RW_WIDTH, RW_WIDTH, RW_DECAY_RANK, RW_AAA_RANK, RW_GATE_RANK)
RW_IN = 3 * RW_WIDTH + RW_DECAY_RANK + RW_AAA_RANK + RW_GATE_RANK
RT_HEADS = 4
RT_KEY_DIM = 128
RT_VAL_DIM = 128
RT_WIDTH = RT_HEADS * RT_VAL_DIM
RT_CHUNK = 128
RT_ROPE_BASE = 10000.0
RT_SIZES = (RT_HEADS * RT_KEY_DIM, RT_HEADS * RT_KEY_DIM, RT_WIDTH, RT_WIDTH)
RT_IN = 2 * RT_HEADS * RT_KEY_DIM + 2 * RT_WIDTH
EV_IN = RW_IN + RT_IN
EV_OUT = RW_WIDTH + RT_WIDTH
DSA_HEADS = 8
DSA_HEAD_DIM = 64
DSA_WIDTH = DSA_HEADS * DSA_HEAD_DIM
DSA_Q_RANK = 256
DSA_KV_RANK = 128
IDX_HEADS = 8
IDX_DIM = 64
TOPK_MAX = 256
DSA_SIZES = (DSA_Q_RANK, DSA_KV_RANK, IDX_DIM, IDX_HEADS)
DSA_IN = DSA_Q_RANK + DSA_KV_RANK + IDX_DIM + IDX_HEADS
SC_WIDTH = 512
SC_KERNEL = 3
SC_SIZES = (SC_WIDTH, SC_WIDTH, SC_WIDTH)
SC_IN = 3 * SC_WIDTH
OD_IN = DSA_IN + SC_IN
OD_OUT = DSA_WIDTH + SC_WIDTH
XA_HEADS = 4
XA_HEAD_DIM = 128
XA_WIDTH = XA_HEADS * XA_HEAD_DIM


F32 = jnp.float32

def split_cols(t, sizes):
    out, start = [], 0
    for s in sizes:
        out.append(t[..., start:start + s])
        start += s
    return out

def rms_norm_2(x, g, eps=EPS):
    xf = x.astype(F32)
    y = xf * lax.rsqrt(jnp.mean(xf * xf, axis=-1, keepdims=True) + eps)
    return (y * g.astype(F32)).astype(x.dtype)

def group_norm_heads(x, g, b, eps):
    xf = x.astype(F32)
    mu = jnp.mean(xf, axis=-1, keepdims=True)
    var = jnp.mean(jnp.square(xf - mu), axis=-1, keepdims=True)
    y = ((xf - mu) * lax.rsqrt(var + eps)).reshape(*x.shape[:-2], -1)
    return y * g.astype(F32) + b.astype(F32)

def token_shift(p):
    return jnp.pad(p, ((0, 0), (1, 0), (0, 0)))[:, :-1]

def swiglu(x, w_gate, w_up, w_down):
    return (jax.nn.silu(x @ w_gate) * (x @ w_up)) @ w_down

def rotary(x, positions):
    half = x.shape[-1] // 2
    inv_freq = RT_ROPE_BASE ** (-jnp.arange(half, dtype=F32) / half)
    ang = positions.astype(F32)[:, None] * inv_freq[None, :]
    cos = jnp.cos(ang)[None, :, None, :]
    sin = jnp.sin(ang)[None, :, None, :]
    x1, x2 = x[..., :half].astype(F32), x[..., half:].astype(F32)
    return jnp.concatenate([x1 * cos - x2 * sin, x1 * sin + x2 * cos], axis=-1).astype(x.dtype)

def rwkv7_mix(p, mu, w0, w2, a0, a2, g2, k_k, k_a, r_k, ln_g, ln_b):
    b_, s_, _ = p.shape
    p = p + (token_shift(p) - p) * mu
    r, k, v, xw, xa, xg = split_cols(p, RW_SIZES)
    w = -jax.nn.softplus(-(w0 + jnp.tanh(xw) @ w2)) - 0.5
    decay = jnp.exp(-jnp.exp(w.astype(F32)))
    a = jax.nn.sigmoid(a0 + xa @ a2)
    g = jax.nn.sigmoid(xg) @ g2
    heads = lambda t: t.reshape(b_, s_, RW_HEADS, RW_HEAD_DIM)
    kk = heads(k * k_k).astype(F32)
    kk = kk / jnp.maximum(jnp.sqrt(jnp.sum(kk * kk, axis=-1, keepdims=True)), 1e-12)
    k = k * (1 + (a - 1) * k_a)
    rh, kh, vh, ah = heads(r), heads(k), heads(v), heads(a).astype(F32)
    xs = tuple(jnp.moveaxis(t.astype(F32), 1, 0) for t in (rh, heads(decay), kh, vh, -kk, kk * ah))

    def step(state, inp):
        r_t, w_t, k_t, v_t, a_t, b_t = inp
        sa = jnp.einsum('bhvk,bhk->bhv', state, a_t)
        state = (state * w_t[:, :, None, :] + sa[..., None] * b_t[:, :, None, :]
                 + v_t[..., None] * k_t[:, :, None, :])
        return state, jnp.einsum('bhvk,bhk->bhv', state, r_t)

    state0 = jnp.zeros((b_, RW_HEADS, RW_HEAD_DIM, RW_HEAD_DIM), F32)
    _, y = lax.scan(step, state0, xs)
    y = group_norm_heads(jnp.moveaxis(y, 0, 1), ln_g, ln_b, RW_LN_EPS)
    bonus = jnp.sum(rh * kh * r_k, axis=-1, keepdims=True) * vh
    y = (y + bonus.reshape(b_, s_, RW_WIDTH).astype(F32)) * g.astype(F32)
    return y.astype(p.dtype)

def retention_mix(p, positions, gn_g, gn_b):
    b_, s_, _ = p.shape
    q, k, v, g = split_cols(p, RT_SIZES)
    q = rotary(q.reshape(b_, s_, RT_HEADS, RT_KEY_DIM), positions)
    k = rotary(k.reshape(b_, s_, RT_HEADS, RT_KEY_DIM), positions) * (RT_KEY_DIM ** -0.5)
    v = v.reshape(b_, s_, RT_HEADS, RT_VAL_DIM)
    n_chunks = s_ // RT_CHUNK
    chunk = lambda t: t.reshape(b_, n_chunks, RT_CHUNK, *t.shape[2:]).astype(F32)
    qc, kc, vc = chunk(q), chunk(k), chunk(v)
    log_gamma = jnp.log1p(-jnp.exp2(-5.0 - jnp.arange(RT_HEADS, dtype=F32)))
    idx = jnp.arange(RT_CHUNK, dtype=F32)
    rel = idx[:, None] - idx[None, :]
    decay_mask = jnp.where(rel[None] >= 0,
                           jnp.exp(jnp.maximum(rel, 0.0)[None] * log_gamma[:, None, None]), 0.0)
    scores = jnp.einsum('bnihd,bnjhd->bnhij', qc, kc) * decay_mask
    o_inner = jnp.einsum('bnhij,bnjhe->bnihe', scores, vc)
    zeta = jnp.exp((RT_CHUNK - 1 - idx)[None, :] * log_gamma[:, None])
    kv = jnp.einsum('bnjhd,hj,bnjhe->bnhde', kc, zeta, vc)
    chunk_gamma = jnp.exp(RT_CHUNK * log_gamma)[None, :, None, None]

    def step(state, kv_n):
        return state * chunk_gamma + kv_n, state

    state0 = jnp.zeros((b_, RT_HEADS, RT_KEY_DIM, RT_VAL_DIM), F32)
    _, r_prev = lax.scan(step, state0, jnp.moveaxis(kv, 1, 0))
    r_prev = jnp.moveaxis(r_prev, 0, 1)
    xi = jnp.exp((idx + 1)[:, None] * log_gamma[None, :])
    o_cross = jnp.einsum('bnihd,bnhde->bnihe', qc, r_prev) * xi[:, :, None]
    o = (o_inner + o_cross).reshape(b_, s_, RT_HEADS, RT_VAL_DIM)
    o = group_norm_heads(o, gn_g, gn_b, EPS)
    return (jax.nn.silu(g.astype(F32)) * o).astype(p.dtype)

def dsa_mix(p, q_norm_g, kv_norm_g, w_uq, w_uk, w_uv, w_qi):
    b_, s_, _ = p.shape
    c_q, c_kv, k_idx, w_idx = split_cols(p, DSA_SIZES)
    c_q = rms_norm_2(c_q, q_norm_g)
    c_kv = rms_norm_2(c_kv, kv_norm_g)
    q = jnp.einsum('btr,rhd->bthd', c_q, w_uq)
    q_lat = jnp.einsum('bthd,hdc->bthc', q, w_uk)
    q_idx = jnp.einsum('btr,rhd->bthd', c_q, w_qi)
    w_idx = w_idx * ((IDX_HEADS * IDX_DIM) ** -0.5)
    top_k = min(TOPK_MAX, s_ // 4)
    n_blocks = s_ // Q_BLOCK
    key_pos = jnp.arange(s_)

    def to_blocks(t):
        return jnp.moveaxis(t.reshape(b_, n_blocks, Q_BLOCK, *t.shape[2:]), 1, 0)

    def block(args):
        blk, ql, qi, wi = args
        q_pos = blk * Q_BLOCK + jnp.arange(Q_BLOCK)
        logits = jnp.einsum('bthd,bsd->bths', qi, k_idx)
        score = jnp.einsum('bth,bths->bts', wi, jax.nn.relu(logits)).astype(F32)
        causal = key_pos[None, :] <= q_pos[:, None]
        score = jnp.where(causal[None], score, -jnp.inf)
        top_val, top_idx = lax.top_k(score, top_k)
        valid = jnp.isfinite(top_val)
        sel = jax.vmap(lambda c, i: c[i])(c_kv, top_idx)
        s = jnp.einsum('bthc,btkc->bthk', ql, sel).astype(F32) * (DSA_HEAD_DIM ** -0.5)
        s = jnp.where(valid[:, :, None, :], s, -jnp.inf)
        prob = jax.nn.softmax(s, axis=-1).astype(sel.dtype)
        return jnp.einsum('bthk,btkc->bthc', prob, sel)

    o_lat = lax.map(block, (jnp.arange(n_blocks), to_blocks(q_lat), to_blocks(q_idx), to_blocks(w_idx)))
    o_lat = jnp.moveaxis(o_lat, 0, 1).reshape(b_, s_, DSA_HEADS, DSA_KV_RANK)
    o = jnp.einsum('bthc,hcd->bthd', o_lat, w_uv)
    return o.reshape(b_, s_, DSA_WIDTH).astype(p.dtype)

def short_conv_mix(p, conv_w, conv_b):
    h, gate_b, gate_c = split_cols(p, SC_SIZES)
    u = gate_c * h
    y = lax.conv_general_dilated(u, conv_w[:, None, :].astype(u.dtype), window_strides=(1,),
                                 padding=[(SC_KERNEL - 1, 0)],
                                 dimension_numbers=('NWC', 'WIO', 'NWC'),
                                 feature_group_count=SC_WIDTH) + conv_b
    return (gate_b * y).astype(p.dtype)

def memory_xattn(h, mem_n, wq, wk, wv, wo):
    b_, s_, _ = h.shape
    m_ = mem_n.shape[1]
    q = (h @ wq).reshape(b_, s_, XA_HEADS, XA_HEAD_DIM)
    k = (mem_n @ wk).reshape(b_, m_, XA_HEADS, XA_HEAD_DIM)
    v = (mem_n @ wv).reshape(b_, m_, XA_HEADS, XA_HEAD_DIM)
    s = jnp.einsum('bthd,bmhd->bhtm', q, k).astype(F32) * (XA_HEAD_DIM ** -0.5)
    prob = jax.nn.softmax(s, axis=-1).astype(v.dtype)
    o = jnp.einsum('bhtm,bmhd->bthd', prob, v).reshape(b_, s_, XA_WIDTH)
    return o @ wo

def second_inputs(seed: int = 0) -> dict:
    key = jax.random.key(seed)
    ks = iter(jax.random.split(key, 48))
    n_even = (DEPTH + 1) // 2
    n_odd = DEPTH // 2
    nrm = lambda shape, scale: jax.random.normal(next(ks), shape, F32) * scale
    gain = lambda shape: 1.0 + nrm(shape, 0.02)
    uni = lambda shape, lo, hi: jax.random.uniform(next(ks), shape, F32, lo, hi)
    return {
        'x': nrm((BATCH, SEQ, D_MODEL), 1.0),
        'mem': nrm((BATCH, MEM_LEN, D_MODEL), 1.0),
        'norm_g': gain((DEPTH, N_NORMS, D_MODEL)),
        'mem_norm_g': gain((D_MODEL,)),
        'ffn_w_gate': nrm((DEPTH, 2, D_MODEL, D_FF_2), D_MODEL ** -0.5),
        'ffn_w_up': nrm((DEPTH, 2, D_MODEL, D_FF_2), D_MODEL ** -0.5),
        'ffn_w_down': nrm((DEPTH, 2, D_FF_2, D_MODEL), D_FF_2 ** -0.5),
        'xa_wq': nrm((DEPTH, D_MODEL, XA_WIDTH), D_MODEL ** -0.5),
        'xa_wk': nrm((DEPTH, D_MODEL, XA_WIDTH), D_MODEL ** -0.5),
        'xa_wv': nrm((DEPTH, D_MODEL, XA_WIDTH), D_MODEL ** -0.5),
        'xa_wo': nrm((DEPTH, XA_WIDTH, D_MODEL), XA_WIDTH ** -0.5),
        'ev_w_in': nrm((n_even, D_MODEL, EV_IN), D_MODEL ** -0.5),
        'ev_w_out': nrm((n_even, EV_OUT, D_MODEL), EV_OUT ** -0.5),
        'rw_mu': uni((n_even, RW_IN), 0.0, 1.0),
        'rw_w0': uni((n_even, RW_WIDTH), -6.0, 1.0),
        'rw_w2': nrm((n_even, RW_DECAY_RANK, RW_WIDTH), 0.5 * RW_DECAY_RANK ** -0.5),
        'rw_a0': nrm((n_even, RW_WIDTH), 0.1),
        'rw_a2': nrm((n_even, RW_AAA_RANK, RW_WIDTH), 0.5 * RW_AAA_RANK ** -0.5),
        'rw_g2': nrm((n_even, RW_GATE_RANK, RW_WIDTH), RW_GATE_RANK ** -0.5),
        'rw_k_k': 0.85 + nrm((n_even, RW_WIDTH), 0.05),
        'rw_k_a': 1.0 + nrm((n_even, RW_WIDTH), 0.05),
        'rw_r_k': nrm((n_even, RW_HEADS, RW_HEAD_DIM), 0.1),
        'rw_ln_g': gain((n_even, RW_WIDTH)),
        'rw_ln_b': nrm((n_even, RW_WIDTH), 0.02),
        'rt_gn_g': gain((n_even, RT_WIDTH)),
        'rt_gn_b': nrm((n_even, RT_WIDTH), 0.02),
        'od_w_in': nrm((n_odd, D_MODEL, OD_IN), D_MODEL ** -0.5),
        'od_w_out': nrm((n_odd, OD_OUT, D_MODEL), OD_OUT ** -0.5),
        'dsa_q_norm_g': gain((n_odd, DSA_Q_RANK)),
        'dsa_kv_norm_g': gain((n_odd, DSA_KV_RANK)),
        'dsa_w_uq': nrm((n_odd, DSA_Q_RANK, DSA_HEADS, DSA_HEAD_DIM), DSA_Q_RANK ** -0.5),
        'dsa_w_uk': nrm((n_odd, DSA_HEADS, DSA_HEAD_DIM, DSA_KV_RANK), DSA_HEAD_DIM ** -0.5),
        'dsa_w_uv': nrm((n_odd, DSA_HEADS, DSA_KV_RANK, DSA_HEAD_DIM), DSA_KV_RANK ** -0.5),
        'dsa_w_qi': nrm((n_odd, DSA_Q_RANK, IDX_HEADS, IDX_DIM), DSA_Q_RANK ** -0.5),
        'sc_conv_w': nrm((n_odd, SC_KERNEL, SC_WIDTH), SC_KERNEL ** -0.5),
        'sc_conv_b': nrm((n_odd, SC_WIDTH), 0.02),
    }

def second_block(x, mem, norm_g, mem_norm_g, ffn_w_gate, ffn_w_up, ffn_w_down,
              xa_wq, xa_wk, xa_wv, xa_wo, ev_w_in, ev_w_out,
              rw_mu, rw_w0, rw_w2, rw_a0, rw_a2, rw_g2, rw_k_k, rw_k_a, rw_r_k, rw_ln_g, rw_ln_b,
              rt_gn_g, rt_gn_b, od_w_in, od_w_out,
              dsa_q_norm_g, dsa_kv_norm_g, dsa_w_uq, dsa_w_uk, dsa_w_uv, dsa_w_qi,
              sc_conv_w, sc_conv_b):
    mem_n = rms_norm_2(mem, mem_norm_g)
    positions = jnp.arange(x.shape[1])
    for l in range(DEPTH):
        ng = norm_g[l]
        h = swiglu(rms_norm_2(x, ng[0]), ffn_w_gate[l, 0], ffn_w_up[l, 0], ffn_w_down[l, 0])
        x = x + 0.5 * rms_norm_2(h, ng[1])
        h = rms_norm_2(x, ng[2])
        i = l // 2
        if l % 2 == 0:
            p = h @ ev_w_in[i]
            y_a = rwkv7_mix(p[..., :RW_IN], rw_mu[i], rw_w0[i], rw_w2[i], rw_a0[i], rw_a2[i],
                            rw_g2[i], rw_k_k[i], rw_k_a[i], rw_r_k[i], rw_ln_g[i], rw_ln_b[i])
            y_b = retention_mix(p[..., RW_IN:], positions, rt_gn_g[i], rt_gn_b[i])
            h = jnp.concatenate([y_a, y_b], axis=-1) @ ev_w_out[i]
        else:
            p = h @ od_w_in[i]
            y_c = dsa_mix(p[..., :DSA_IN], dsa_q_norm_g[i], dsa_kv_norm_g[i], dsa_w_uq[i],
                          dsa_w_uk[i], dsa_w_uv[i], dsa_w_qi[i])
            y_d = short_conv_mix(p[..., DSA_IN:], sc_conv_w[i], sc_conv_b[i])
            h = jnp.concatenate([y_c, y_d], axis=-1) @ od_w_out[i]
        x = x + rms_norm_2(h, ng[3])
        h = memory_xattn(rms_norm_2(x, ng[4]), mem_n, xa_wq[l], xa_wk[l], xa_wv[l], xa_wo[l])
        x = x + rms_norm_2(h, ng[5])
        h = swiglu(rms_norm_2(x, ng[6]), ffn_w_gate[l, 1], ffn_w_up[l, 1], ffn_w_down[l, 1])
        x = x + 0.5 * rms_norm_2(h, ng[7])
    return x


def setup_inputs(seed=0):
    out = dict(first_inputs(seed))
    for name, value in second_inputs(seed + 1).items():
        if name != "x":
            out[name + "_2"] = value
    return out


def reference(
    x, c, ctx, c_ctx, norm1_g, norm2_g, w_mod, b_mod, w_ff1, w_ff2, conv_w_pw1, conv_w_dw,
    conv_b_dw, conv_ln_g, conv_ln_b, conv_w_pw2, gqa_w_qkv, gqa_q_norm, gqa_k_norm, gqa_w_o,
    pool_w, pool_scale, mla_w_dq, mla_q_lora_norm, mla_w_uq, mla_w_dkv, mla_kv_lora_norm,
    mla_w_ukv, mla_q_norm, mla_k_norm, mla_w_o, mem_2, norm_g_2, mem_norm_g_2, ffn_w_gate_2,
    ffn_w_up_2, ffn_w_down_2, xa_wq_2, xa_wk_2, xa_wv_2, xa_wo_2, ev_w_in_2, ev_w_out_2,
    rw_mu_2, rw_w0_2, rw_w2_2, rw_a0_2, rw_a2_2, rw_g2_2, rw_k_k_2, rw_k_a_2, rw_r_k_2,
    rw_ln_g_2, rw_ln_b_2, rt_gn_g_2, rt_gn_b_2, od_w_in_2, od_w_out_2, dsa_q_norm_g_2,
    dsa_kv_norm_g_2, dsa_w_uq_2, dsa_w_uk_2, dsa_w_uv_2, dsa_w_qi_2, sc_conv_w_2, sc_conv_b_2,
):
    x = first_block(
        x, c, ctx, c_ctx, norm1_g, norm2_g, w_mod, b_mod, w_ff1, w_ff2, conv_w_pw1, conv_w_dw,
        conv_b_dw, conv_ln_g, conv_ln_b, conv_w_pw2, gqa_w_qkv, gqa_q_norm, gqa_k_norm, gqa_w_o,
        pool_w, pool_scale, mla_w_dq, mla_q_lora_norm, mla_w_uq, mla_w_dkv, mla_kv_lora_norm,
        mla_w_ukv, mla_q_norm, mla_k_norm, mla_w_o,
    )
    return second_block(
        x, mem_2, norm_g_2, mem_norm_g_2, ffn_w_gate_2, ffn_w_up_2, ffn_w_down_2, xa_wq_2,
        xa_wk_2, xa_wv_2, xa_wo_2, ev_w_in_2, ev_w_out_2, rw_mu_2, rw_w0_2, rw_w2_2, rw_a0_2,
        rw_a2_2, rw_g2_2, rw_k_k_2, rw_k_a_2, rw_r_k_2, rw_ln_g_2, rw_ln_b_2, rt_gn_g_2,
        rt_gn_b_2, od_w_in_2, od_w_out_2, dsa_q_norm_g_2, dsa_kv_norm_g_2, dsa_w_uq_2,
        dsa_w_uk_2, dsa_w_uv_2, dsa_w_qi_2, sc_conv_w_2, sc_conv_b_2,
    )


_drawn_inputs = setup_inputs


def setup_inputs(seed=0):
    import zlib

    import numpy as np

    out = dict(_drawn_inputs(seed))
    spreads = {}
    factors = {'conv_b_dw': 3.282,
     'conv_ln_b': 5.32,
     'gqa_q_norm': 8.0,
     'gqa_k_norm': 8.0,
     'rw_ln_g_2': 4.845,
     'rw_ln_b_2': 4.373,
     'rt_gn_g_2': 3.887,
     'rt_gn_b_2': 3.958,
     'dsa_q_norm_g_2': 6.167,
     'dsa_kv_norm_g_2': 8.0,
     'sc_conv_b_2': 48.675}
    for name, (base, spread) in spreads.items():
        noise = np.random.default_rng([zlib.crc32(name.encode()), seed]).standard_normal(out[name].shape)
        drawn = base * np.exp(spread * noise) if base else spread * noise
        out[name] = __import__('jax').numpy.asarray(drawn.astype(out[name].dtype))
    for name, factor in factors.items():
        out[name] = (out[name] * factor).astype(out[name].dtype)
    return out
```

```python
from contextlib import ExitStack, contextmanager

import numpy as np

import concourse.bass as bass
from concourse import mybir

F32 = mybir.dt.float32
ACT = mybir.ActivationFunctionType
ALU = mybir.AluOpType
AX = mybir.AxisListType.X

P = 128
T = 256
D = 1024
KT = D // P
RING = 12
FF1_TILES = 4096 // P
FF2_TILES = 2816 // P
TAPS = 31
PAD = TAPS // 2
SEG = T + 2 * PAD
RW_C = 64
RW_LEVELS = 6
TOPK = 64
NEG = -1.0e30
TAKEN = -3.0e38
EPS = 1e-6

VECTORS = (
    [("c", 16), ("b_mod", 96), ("norm1", 16), ("norm2", 16), ("dw", TAPS * KT), ("dw_b", KT), ("ln_g", KT),
     ("ln_b", KT), ("gqa_q", 1), ("gqa_k", 1), ("norm_g", 128), ("mem_g", KT), ("rw_mu", 14), ("w0", 4), ("a0", 4),
     ("k_k", 4), ("k_a", 4), ("r_k", 4), ("rw_g", 4), ("rw_b", 4), ("rt_g", 4), ("rt_b", 4), ("dsa_q", 2),
     ("dsa_kv", 1), ("sc_w", 12), ("sc_b", 4)])
CONSTS = [("ident", 128), ("ones", 128), ("blk", 128), ("gqa_rot", 128), ("rt_rot", 128), ("gqa_cos", 512),
          ("gqa_sin", 512), ("rt_cos", 256), ("rt_sin", 256), ("rt_decay", 1024), ("rw_mask", 512),
          ("rw_level", 128 * RW_LEVELS), ("causal", 384), ("eps", 4)]


def columns(table):
    at, n = {}, 0
    for name, width in table:
        at[name] = (n, width)
        n += width
    return at, n


VEC_AT, VEC_N = columns(VECTORS)
CON_AT, CON_N = columns(CONSTS)


def constant_arrays():
    f = np.float32
    p = np.arange(P)
    c = {"ident": np.eye(P, dtype=f), "ones": np.ones((P, P), f)}
    c["blk"] = (p[:, None] // 64 == p[None, :] // 64).astype(f)

    def rotation(half):
        m = np.zeros((P, P), f)
        for i in range(P):
            first = i % (2 * half) < half
            m[i + half if first else i - half, i] = -1.0 if first else 1.0
        return m

    c["gqa_rot"], c["rt_rot"] = rotation(16), rotation(64)
    pos = np.arange(T)
    inv = (f(10000.0) ** (-np.arange(16, dtype=f) / f(16))).astype(f)
    ang = np.zeros((64, T), f)
    for i in range(64):
        where = (pos // 64 if i < 32 else pos % 64).astype(f)
        ang[i] = where * inv[i % 16]
    ang = np.concatenate([ang, ang])
    c["gqa_cos"] = np.concatenate([np.ones((P, T), f), np.cos(ang)], 1)
    c["gqa_sin"] = np.concatenate([np.zeros((P, T), f), np.sin(ang)], 1)
    inv = (f(10000.0) ** (-np.arange(64, dtype=f) / f(64))).astype(f)
    ang = (pos.astype(f)[None, :] * inv[:, None]).astype(f)
    ang = np.concatenate([ang, ang])
    c["rt_cos"], c["rt_sin"] = np.cos(ang), np.sin(ang)
    rel = pos[None, :] - p[:, None]
    gammas = [np.log1p(-(2.0 ** (-5.0 - h))) for h in range(4)]
    c["rt_decay"] = np.concatenate(
        [np.where(rel >= 0, np.exp(np.maximum(rel, 0) * g), 0.0) * 128 ** -0.5 for g in gammas], 1)
    same = p[:, None] // RW_C == p[None, :] // RW_C
    strict = (same & (p[:, None] < p[None, :])).astype(f)
    upto = (same & (p[:, None] <= p[None, :])).astype(f)
    c["rw_mask"] = np.concatenate([strict, upto, strict, upto], 1)
    levels = []
    for n in range(RW_LEVELS):
        w = 1 << n
        levels.append((p[:, None] // (2 * w) == p[None, :] // (2 * w))
                      & (p[:, None] // w % 2 == 0) & (p[None, :] // w % 2 == 1))
    c["rw_level"] = np.concatenate(levels, 1)
    s = np.arange(T)
    c["causal"] = np.concatenate([np.where(s[None, :P] <= p[:, None], 0.0, NEG),
                                  np.where(s[None, :] <= P + p[:, None], 0.0, NEG)], 1)
    c["eps"] = np.tile(np.array([EPS, 64e-5, 0.0, 1.0]), (P, 1))
    return np.ascontiguousarray(np.concatenate([c[n].astype(f) for n, _ in CONSTS], 1))


def k_panels(w):
    n = w.shape[1] // P
    return w.reshape(KT, P, n, P).transpose(2, 1, 0, 3).reshape(n, P, D)


def row_panels(w):
    return w.reshape(-1, P, D)


def weight_stream(a):
    out = []

    def add(*panels):
        out.extend(np.asarray(x).reshape(-1, P, D) for x in panels)

    mod0, mod1 = k_panels(a["w_mod"][0]), k_panels(a["w_mod"][1])
    add(mod0[0:16])
    pw1 = k_panels(a["conv_w_pw1"][0])
    add(np.stack([pw1[:KT], pw1[KT:]], 1))
    add(mod0[16:], mod1)
    add(k_panels(a["conv_w_pw2"][0]))

    def mlp(layer):
        up, down = k_panels(a["w_ff1"][layer]), row_panels(a["w_ff2"][layer])
        add(up[0:1], np.stack([up[1:], down[:-1]], 1), down[-1:])

    mlp(0)
    mlp(0)
    qkv = a["gqa_w_qkv"][0]
    keys = qkv[:, 1024:1280].reshape(D, 4, 1, 64)
    add(k_panels(np.concatenate([keys, keys], 2).reshape(D, 512)))
    add(k_panels(qkv[:, 1280:1536]), k_panels(qkv[:, :1024]))
    add(k_panels(a["gqa_w_o"][0]))
    mlp(1)

    def ffn(layer, which):
        gate, up = (k_panels(a[n][layer, which]) for n in ("ffn_w_gate_2", "ffn_w_up_2"))
        down = row_panels(a["ffn_w_down_2"][layer, which])
        add(gate[0:1], up[0:1], np.stack([gate[1:], up[1:], down[:-1]], 1), down[-1:])

    def xattn(layer):
        add(k_panels(a["xa_wk_2"][layer]), k_panels(a["xa_wv_2"][layer]), k_panels(a["xa_wq_2"][layer]))
        add(row_panels(a["xa_wo_2"][layer]))

    ffn(0, 0)
    ev = k_panels(a["ev_w_in_2"][0])
    add(ev[14:], ev[:14])
    pair = np.concatenate([a["rw_w2_2"][0], a["rw_a2_2"][0]], 0)
    add(np.concatenate([pair, a["rw_g2_2"][0]], 1))
    add(k_panels(a["ev_w_out_2"][0]))
    xattn(0)
    ffn(0, 1)
    ffn(1, 0)
    od = a["od_w_in_2"][0]
    k_idx = od[:, 384:448]
    none = np.zeros((D, 120), np.float32)
    add(k_panels(np.concatenate([od[:, :384], k_idx, k_idx, od[:, 448:456], none, od[:, 456:]], 1)))
    q_rows = lambda w: w[0].reshape(2, P, 512).transpose(1, 0, 2).reshape(P, D)
    uk = a["dsa_w_uk_2"][0].reshape(4, P, P).transpose(1, 0, 2).reshape(P, 512)
    uv = a["dsa_w_uv_2"][0].transpose(1, 0, 2).reshape(P, 512)
    add(q_rows(a["dsa_w_uq_2"]), q_rows(a["dsa_w_qi_2"]), np.concatenate([uk, uv], 1))
    add(k_panels(a["od_w_out_2"][0]))
    xattn(1)
    ffn(1, 1)
    return np.concatenate(out)


def cols(v):
    return np.asarray(v, np.float32).reshape(-1, P).T


def vector_columns(a):
    two = lambda v: np.concatenate([v[0], v[0]])
    v = {
        "c": np.stack([cols(a["c_ctx"]), cols(a["c"])], 2).reshape(P, 16),
        "b_mod": cols(a["b_mod"]), "norm1": cols(a["norm1_g"]), "norm2": cols(a["norm2_g"]),
        "dw": cols(a["conv_w_dw"]), "dw_b": cols(a["conv_b_dw"]), "ln_g": cols(a["conv_ln_g"]),
        "ln_b": cols(a["conv_ln_b"]), "gqa_q": cols(two(a["gqa_q_norm"])), "gqa_k": cols(two(a["gqa_k_norm"])),
        "norm_g": cols(a["norm_g_2"]), "mem_g": cols(a["mem_norm_g_2"]), "rw_mu": cols(a["rw_mu_2"]),
        "w0": cols(a["rw_w0_2"]), "a0": cols(a["rw_a0_2"]), "k_k": cols(a["rw_k_k_2"]), "k_a": cols(a["rw_k_a_2"]),
        "r_k": cols(a["rw_r_k_2"]), "rw_g": cols(a["rw_ln_g_2"]), "rw_b": cols(a["rw_ln_b_2"]),
        "rt_g": cols(a["rt_gn_g_2"]), "rt_b": cols(a["rt_gn_b_2"]), "dsa_q": cols(a["dsa_q_norm_g_2"]),
        "dsa_kv": cols(a["dsa_kv_norm_g_2"]), "sc_w": cols(a["sc_conv_w_2"]), "sc_b": cols(a["sc_conv_b_2"]),
    }
    return np.ascontiguousarray(np.concatenate([v[n] for n, _ in VECTORS], 1))


def feature_major(x):
    return np.ascontiguousarray(np.asarray(x).reshape(T, KT, P).transpose(2, 1, 0))


class Steps:

    def __init__(self, key, eng, plan):
        self.key, self.eng, self.plan, self.n = key, eng, plan, 0

    def step(self, ins, name=None):
        self.n += 1
        if name is not None:
            self.plan[self.key, name] = self.n

    def base(self, name):
        self.plan[self.key, name] = self.n

    @contextmanager
    def loop(self, turns):
        start = self.n
        with self.eng.Fori(0, turns) as i:
            yield i
        self.n = start + (self.n - start) * turns


def build(nc, const, vec, xs, mem, weights, out, plan, upto=99):
    with ExitStack() as ctx:
        def sb(name, *shape):
            return ctx.enter_context(nc.sbuf_tensor(name, [P, *shape], F32))

        def sem(name):
            return ctx.enter_context(nc.semaphore(name))

        ring = sb("ring", RING, D)
        con = sb("con", CON_N)
        vecs = sb("vecs", VEC_N)
        X = sb("X", KT, 2 * T)
        H = sb("H", KT, 2 * T)
        RS = sb("RS", 2, 2 * T)
        MOD = sb("MOD", 96, 2)
        GS = sb("GS", 4, KT, 2)
        SC = sb("SC", 16)
        small = sb("small", 64)
        arena = sb("arena", 25600)
        ps = ctx.enter_context(nc.psum_tensor("ps", [P, 8, 512], F32))

        full = [sem(f"panel_full{s}") for s in range(RING)]
        panels_used = sem("panels_used")
        pe_done, act_done, dve_done, pool_done = (sem(f"{k}_done") for k in ("pe", "act", "dve", "pool"))
        sems = {"pe": pe_done, "act": act_done, "dve": dve_done, "pool": pool_done, "panel": panels_used}

        def at(key, name):
            return plan.get((key, name), 1)

        def after(key, name):
            return sems[key], at(key, name)

        inputs_in = [sem(f"{n}_in") for n in ("con", "vec", "x", "mem")]
        out_stored = sem("out_stored")

        def c(name, *shape):
            at, w = CON_AT[name]
            ap = con[:, at:at + w]
            return ap

        def v(name, i=0, n=1):
            at, w = VEC_AT[name]
            return vecs[:, at + i:at + i + n]

        def area(at, *shape):
            n = int(np.prod(shape))
            assert at + n <= 25600, (at, shape)
            ap = arena[:, at:at + n]
            if len(shape) == 2:
                ap = ap.rearrange("p (a b) -> p a b", a=shape[0])
            if len(shape) == 3:
                ap = ap.rearrange("p (a b c) -> p a b c", a=shape[0], b=shape[1])
            return ap

        ident, ones, blk = c("ident"), c("ones"), c("blk")
        eps6, eps_rw = c("eps")[:, 0:1], c("eps")[:, 1:2]
        LAT = slice(T, 2 * T)
        ACC = lambda k: ps[:, 4 + k // 2, (k % 2) * T:(k % 2 + 1) * T]

        U = area(0, KT, 2, SEG)
        CV = area(4608, KT, 2 * T)
        SG = area(8704, 2, 2 * T)
        HS = area(25600 - 2048, 2, 2 * T)
        HT = area(25600 - 1024, 2, 2 * T)
        KQ = area(0, 8, 2 * T)
        GV = area(4096, 4, 2 * P)
        GO = area(5120, KT, T)
        SQ = area(7168, 2, 2 * T)
        ROT = area(8192, 2, 2 * T)
        PR = area(10240, 3, 2 * T)
        PT = area(11776, 2, 2 * T)
        SBI = area(12800, 2, T)
        AS = area(13312, 64, 4)

        Y = area(0, KT, T)
        MEMN = X[:, :, 0:T]
        TMP = H[:, :, 0:T]
        HG = sb("HG", 4, KT)
        XK, XV, XQ, XO = area(0, 4, T), area(1024, 2, 512), area(2048, 4, T), area(3072, 4, T)
        RQK, RROT = area(2048, 4, 512), area(4096, 2, 512)
        RV, RG, RO, RP = area(5120, 2, 512), area(6144, 4, T), area(7168, 4, T), area(8192, 2, 512)
        GSQ, GRR = area(9216, 2, 512), area(10240, 2, 512)
        RAW, P2 = area(14848, 2, 2, 260), area(11264, 14, T)
        LW, LC, EP, EN, EX = (area(16384 + 1024 * n, 1024) for n in range(5))
        AA, KK, KP, RESET = (area(21504 + 1024 * n, 1024) for n in range(4))
        RWG, BON = H[:, 0:4, 0:T], H[:, 4:8, 0:T]
        AR = area(2048, 4, 2, T)
        BF, KF = area(4096, 4, T), area(5120, 4, T)
        BC, KC = area(6144, 4, T), area(7168, 4, T)
        AT, BT, KTM, VT = area(8192, 2, 512), area(9216, 2, 512), area(10240, 2, 512), area(14848, 2, 512)
        PC = small[:, 16:32].rearrange("p (m c) -> p m c", m=4)
        MR, MA = area(16384, 16, 2, P), area(20480, 8, 2, P)
        TI, TT, XB = area(22528, 8, P), area(23552, 8, P), area(24576, 8, P)
        AL, W1, TV, TAT = area(11264, 8, P), area(12288, 512), area(12800, 2, 512), area(13824, 4, T)
        SK, SKP = area(6144, 4, 4, 64), area(7168, 4, 64)
        UB, YR = area(4096, 2, 8, 64), area(5120, 4, T)
        WSQ, WRR = area(20480, 2, 512), area(22528, 2, 512)
        CQ, CKV, KI, WI = area(2048, 2, T), area(2560, T), area(2816, T), area(3072, 2, 8)
        SU, GB = area(3104, 4, 260), area(4160, 4, T)
        DQ, QI, QL, CKT = area(5184, 4, T), area(6208, 4, T), area(7232, 8, T), area(9280, 2, P)
        RL, SCO, WK, BI, OL = area(9536, 2, T), area(13568, 2, T), area(14080, 2, T), area(14592, 2, T), area(15104, 8, T)
        TOP = small[:, 32:48].rearrange("p (t e) -> p t e", t=2)
        SHH = area(17152, 4, T)
        SQD = area(18176, 3, T)

        lo_of = lambda h: 64 * (h % 2)
        RW_UNITS = [(t, h) for t in range(2) for h in range(8)]
        GQA_UNITS = [(h, t, 4) for h in range(16) for t in range(2)]
        XA_UNITS = [(h, t, 2) for h in range(4) for t in range(2)]
        DSA_UNITS = [(h, t, t + 1) for h in range(8) for t in range(2)]

        block = ctx.enter_context(nc.Block())

        @block.sync
        def _(sp):
            total = plan.get(("panel", "total"), RING)
            for n in range(min(RING, total)):
                sp.dma_start(ring[:, n, :], weights[n]).then_inc(full[n], 16)
            turns = total // RING
            if turns > 1:
                with sp.Fori(1, turns) as i:
                    for s in range(RING):
                        sp.wait_ge(panels_used, RING * i + (s + 1 - RING))
                        sp.dma_start(ring[:, s, :], weights[RING * i + s]).then_inc(full[s], 16)
            for n in range(max(turns, 1) * RING, total):
                sp.wait_ge(panels_used, n + 1 - RING)
                sp.dma_start(ring[:, n % RING, :], weights[n]).then_inc(full[n % RING], 16)
            sp.wait_ge(panels_used, total)

        @block.tensor
        def _(pe):
            s = Steps("pe", pe, plan)
            panels = [0]

            def panel(i=None, back=0):
                n = panels[0]
                panels[0] += 1
                slot, value = n % RING, 16 * (n // RING + 1)
                pe.wait_ge(full[slot], value if i is None else 16 * i + value)
                return ring[:, slot, :]

            def used(ins, name=None):
                ins.then_inc(panels_used, 1)
                if name is not None:
                    plan["panel", name] = panels[0]

            def turns(n):
                panels[0] += (n - 1) * RING

            def feature_tile(dst, rhs, w, per_k=None, first=True, name=None):
                for k in range(KT):
                    if per_k:
                        pe.wait_ge(sems[per_k[0]], at(per_k[0], per_k[1] + f"{k}"))
                    ins = pe.matmul(dst, w[:, k * P:(k + 1) * P], rhs(k), start=(k == 0), stop=(k == KT - 1))
                used(ins, name)

            def column_sums(bank, src, tiles, name, what=ones, wait=None):
                for k in range(tiles):
                    if wait:
                        pe.wait_ge(sems[wait[0]], at(wait[0], wait[1] + f"{k}"))
                    ins = pe.matmul(bank, what, src(k), start=(k == 0), stop=(k == tiles - 1))
                s.step(ins.then_inc(pe_done, 1), name)

            def hidden_loop(tag, tiles, kinds, width, rhs, last_free):
                p0 = panels[0]
                plan["panel", tag] = p0
                d0 = at("dve", tag)
                per = kinds + 1

                def up(t, c, i=None):
                    if i is not None or t >= 2:
                        pe.wait_ge(sems["dve"], d0 + t - 1 if i is None else d0 + t - 1 + i * (RING // per))
                    for q in range(kinds):
                        w = panel(i)
                        for k in range(KT):
                            if i is None and t == 0 and q == 0:
                                pe.wait_ge(sems[last_free[0]], at(last_free[0], f"{last_free[1]}h{k}"))
                            ins = pe.matmul(ps[:, t % 2, q * T:(q + 1) * T], w[:, k * P:(k + 1) * P], rhs(k),
                                            start=(k == 0 and q == 0), stop=(k == KT - 1), skip_group_check=True)
                        used(ins)

                def down(t, i=None):
                    pe.wait_ge(sems["dve"], d0 + t + 1 if i is None else d0 + t + 1 + i * (RING // per))
                    w = panel(i)
                    for k in range(KT):
                        ins = pe.matmul(ACC(k), w[:, k * P:(k + 1) * P], HT[:, t % 2, 0:T],
                                        start=(i is None and t == 0 and k % 2 == 0),
                                        stop=(t == tiles - 1), skip_group_check=True)
                    used(ins, tag + ".last" if i is None and t == tiles - 1 else None)

                body = RING // per
                n = (tiles - 2) // body
                up(0, 0)
                up(1, 1)
                pe.wait_ge(dve_done, at("dve", tag + ".acc_free"))
                down(0)
                with pe.Fori(0, n) as i:
                    for b in range(body):
                        up(2 + b, b, i)
                        down(1 + b, i)
                turns(n)
                for t in range(2 + n * body, tiles):
                    up(t, 0)
                    down(t - 1)
                down(tiles - 1)

            for q in range(2):
                pe.wait_ge(inputs_in[q], 16)

            mod_out = lambda m: ps[:, 7, 2 * m:2 * m + 2]

            def mod_tile(dst, i=None, name=None):
                w = panel(i)
                for k in range(KT):
                    ins = pe.matmul(dst, w[:, k * P:(k + 1) * P], SC[:, 2 * k:2 * k + 2],
                                    start=(k == 0), stop=(k == KT - 1), skip_group_check=True)
                used(ins, name)

            def norm_sums(tag, t0, width):
                column_sums(ps[:, 2, 0:width], lambda k: H[:, k, t0:t0 + width], KT, tag + "sum",
                            wait=("act", tag + "sq"))

            pe.wait_ge(act_done, at("act", "silu_c"))
            for m in range(16):
                mod_tile(mod_out(m), name=f"mod{m}")
            norm_sums("n0", 0, 2 * T)

            for j in range(KT):
                if j >= 2:
                    pe.wait_ge(dve_done, at("dve", f"glu{j - 2}"))
                else:
                    pe.wait_ge(act_done, at("act", "n0rms"))
                for q in range(2):
                    feature_tile(ps[:, 2 * (j % 2) + q, :], lambda k: H[:, k, :], panel(),
                                 ("act", "n0h") if j == 0 and q == 0 else None, name=f"pw1_{j}_{q}")
            with pe.Fori(0, 6) as i:
                for b in range(RING):
                    mod_tile(ps[:, 7, bass.ds(24 * i + (32 + 2 * b), 2)], i)
            turns(6)
            for m in range(88, 96):
                mod_tile(mod_out(m), name="mod_all")
            column_sums(ps[:, 0, :], lambda k: CV[:, k, :], KT, "ln_mean", wait=("dve", "conv"))
            column_sums(ps[:, 2, :], lambda k: H[:, k, :], KT, "ln_var", wait=("act", "ln_sq"))
            for j in range(KT):
                if j >= 2:
                    pe.wait_ge(dve_done, at("dve", f"pw2_{j - 2}"))
                feature_tile(ps[:, j % 2, :], lambda k: H[:, k, :], panel(), ("act", "ln_h") if j == 0 else None,
                             name=f"pw2_{j}")
            if upto < 1:
                plan["panel", "total"] = panels[0]
                return
            norm_sums("n1", 0, 2 * T)
            hidden_loop("mlp0c", FF1_TILES, 1, T, lambda k: H[:, k, 0:T], ("act", "n1"))
            hidden_loop("mlp0l", FF1_TILES, 1, T, lambda k: H[:, k, LAT], ("act", "n1"))
            if upto < 2:
                plan["panel", "total"] = panels[0]
                return

            norm_sums("n2", 0, 2 * T)
            for u in range(4):
                if u >= 2:
                    pe.wait_ge(act_done, at("act", f"kq_raw{u - 2}"))
                else:
                    pe.wait_ge(act_done, at("act", "n2rms"))
                feature_tile(ps[:, u % 2, :], lambda k: H[:, k, :], panel(), ("act", "n2h") if u == 0 else None,
                             name=f"kq{u}")
            for q in range(2):
                w = panel()
                pe.wait_ge(act_done, at("act", "kq_raw3")) if q else pe.wait_ge(act_done, at("act", "kq_raw2"))
                for t in range(4):
                    for k in range(KT):
                        ins = pe.matmul(ps[:, 4 + q, t * P:(t + 1) * P], H[:, k, t * P:(t + 1) * P],
                                        w[:, k * P:(k + 1) * P], start=(k == 0 and t == 0), stop=(k == KT - 1),
                                        skip_group_check=True)
                used(ins, f"gv{q}")
                plan["panel", "gqa_w"] = panels[0]
            for u in range(4, 8):
                pe.wait_ge(act_done, at("act", f"kq_raw{u - 2}"))
                for q in range(2):
                    w = panel()
                    for k in range(KT):
                        ins = pe.matmul(ps[:, u % 2, q * T:(q + 1) * T], w[:, k * P:(k + 1) * P], H[:, k, LAT],
                                        start=(k == 0 and q == 0), stop=(k == KT - 1), skip_group_check=True)
                    used(ins, f"kq{u}")
            for u in range(8):
                pe.wait_ge(act_done, at("act", f"kq_sq{u}"))
                if u >= 2:
                    pe.wait_ge(act_done, at("act", f"kq_rms{u - 2}"))
                s.step(pe.matmul(ps[:, 2 + u % 2, :], blk, SQ[:, u % 2, :], start=True, stop=True).then_inc(pe_done, 1), f"kq_sum{u}")
            for u in range(8):
                pe.wait_ge(dve_done, at("dve", f"kq_norm{u}"))
                if u >= 2:
                    pe.wait_ge(dve_done, at("dve", f"kq_sin{u - 2}"))
                else:
                    pe.wait_ge(act_done, at("act", f"kq_raw{u + 6}"))
                s.step(pe.matmul(ps[:, u % 2, :], c("gqa_rot"), KQ[:, u, :], start=True, stop=True).then_inc(pe_done, 1), f"kq_rot{u}")

            def attention(tag, units, L, score, value, out_of):
                for u in range(len(units) + 2):
                    if u < len(units):
                        if u >= 4:
                            pe.wait_ge(*(after("dve", f"{tag}_bias{u - 4}") if tag == "dsa" else after("act", f"{tag}_exp{u - 4}")))
                        a, b = score(u)
                        s.step(pe.matmul(ps[:, u % 4, 0:units[u][2] * P], a, b, start=True, stop=True).then_inc(pe_done, 1), f"{tag}_s{u}")
                    if u >= 2:
                        w = u - 2
                        pe.wait_ge(dve_done, at("dve", f"{tag}_p{w}"))
                        if w >= 2:
                            pe.wait_ge(act_done, at("act", f"{tag}_pt{w - 2}"))
                        nl = units[w][2]
                        for l in range(nl):
                            ins = pe.transpose(ps[:, 4 + w % 2, l * P:(l + 1) * P],
                                               PR[:, w % 3, l * P:(l + 1) * P], ident)
                        s.step(ins.then_inc(pe_done, 1), f"{tag}_t{w}")
                        if w >= 4 and w % 2 == 0:
                            pe.wait_ge(dve_done, at("dve", f"{tag}_o{w - 3}"))
                        pe.wait_ge(act_done, at("act", f"{tag}_pt{w}"))
                        for l in range(nl):
                            ins = pe.matmul(out_of(w), value(w, l), PT[:, w % 2, l * P:(l + 1) * P],
                                            start=(l == 0), stop=(l == nl - 1), skip_group_check=True)
                        s.step(ins.then_inc(pe_done, 1), f"{tag}_pv{w}")

            gqa_units = [(h, t, 4) for h in range(16) for t in range(2)]

            def gqa_score(u):
                h, t, _ = gqa_units[u]
                lo = 64 * (h % 2)
                q = KQ[lo:lo + 64, 4 + h // 4, (h // 2 % 2) * T + t * P:(h // 2 % 2) * T + t * P + P]
                return q, KQ[lo:lo + 64, h // 4, :]

            def gqa_value(u, l):
                h = gqa_units[u][0]
                g = h // 4
                return GV[:, l, g * 64:(g + 1) * 64]

            def gqa_out(u):
                h, t, _ = gqa_units[u]
                lo = 64 * (h % 2)
                return ps[lo:lo + 64, 6 + h % 2, t * P:(t + 1) * P]

            pe.wait_ge(dve_done, at("dve", "kq_done"))
            pe.wait_ge(act_done, at("act", "gv1"))
            attention("gqa", gqa_units, 4 * P, gqa_score, gqa_value, gqa_out)
            for j in range(KT):
                if j >= 2:
                    pe.wait_ge(dve_done, at("dve", f"wo_{j - 2}"))
                else:
                    pe.wait_ge(dve_done, at("dve", "gqa_o31"))
                feature_tile(ps[:, j % 2, 0:T], lambda k: GO[:, k, :], panel(), name=f"wo_{j}")
            norm_sums("n3", T, T)
            hidden_loop("mlp1", FF1_TILES, 1, T, lambda k: H[:, k, LAT], ("act", "n3"))
            if upto < 3:
                plan["panel", "total"] = panels[0]
                return

            HL = lambda k: H[:, k, LAT]

            def row_products(tag, tiles, src, wait):
                for r in range(tiles):
                    w = panel()
                    pe.wait_ge(sems[wait[0]], at(wait[0], wait[1](r)))
                    for k in range(KT):
                        ins = pe.matmul(ACC(k), w[:, k * P:(k + 1) * P], src(r), start=(r == 0 and k % 2 == 0),
                                        stop=(r == tiles - 1), skip_group_check=True)
                    used(ins, f"{tag}_out{r}")

            def out_tiles(tag, wait):
                for j in range(KT):
                    w = panel()
                    for k in range(KT):
                        if j == 0:
                            pe.wait_ge(*after(*wait(k)))
                        ins = pe.matmul(ACC(j), w[:, k * P:(k + 1) * P], Y[:, k, :], start=(k == 0 and j % 2 == 0),
                                        stop=(k == KT - 1), skip_group_check=True)
                    used(ins, f"{tag}_out{j}")

            def sums_post(tag):
                column_sums(ps[:, 2, 0:T], HL, KT, tag + "sum", wait=("act", tag + "sq"))

            def pair(bank, name, per_k=None):
                for q in range(2):
                    w = panel()
                    for k in range(KT):
                        if per_k and q == 0:
                            pe.wait_ge(sems[per_k[0]], at(per_k[0], f"{per_k[1]}{k}"))
                        ins = pe.matmul(ps[:, bank, q * T:(q + 1) * T], w[:, k * P:(k + 1) * P], HL(k),
                                        start=(k == 0 and q == 0), stop=(k == KT - 1), skip_group_check=True)
                    used(ins, name)

            def token_major(bank, src, name):
                w = panel()
                for t in range(2):
                    for k in range(KT):
                        ins = pe.matmul(ps[:, bank, t * P:(t + 1) * P], src(k, t), w[:, k * P:(k + 1) * P],
                                        start=(k == 0 and t == 0), stop=(k == KT - 1), skip_group_check=True)
                used(ins, name)

            lat_tile = lambda k, t: H[:, k, T + t * P:T + (t + 1) * P]

            def ffn(tag):
                sums_post(tag + "a")
                hidden_loop(tag, FF2_TILES, 2, T, HL, ("dve", tag + "a"))
                sums_post(tag + "b")

            def xattn(tag):
                for h in range(4):
                    if h >= 2:
                        pe.wait_ge(act_done, at("act", f"{tag}_k{h - 2}"))
                    w = panel()
                    for k in range(KT):
                        ins = pe.matmul(ps[:, h % 2, 0:T], w[:, k * P:(k + 1) * P], MEMN[:, k, :], start=(k == 0),
                                        stop=(k == KT - 1))
                    used(ins, f"{tag}_k{h}")
                for q in range(4):
                    pe.wait_ge(act_done, at("act", f"{tag}_k{q}" if q < 2 else f"{tag}_v{q - 2}")) if q >= 2 else pe.wait_ge(act_done, at("act", f"{tag}_k{q + 2}"))
                    token_major(q % 2, lambda k, t: MEMN[:, k, t * P:(t + 1) * P], f"{tag}_v{q}")
                sums_post(tag + "a")
                for h in range(4):
                    pe.wait_ge(act_done, at("act", f"{tag}_v{h + 2}" if h < 2 else f"{tag}_q{h - 2}"))
                    feature_tile(ps[:, h % 2, 0:T], HL, panel(), ("dve", tag + "ah") if h == 0 else None, name=f"{tag}_q{h}")
                pe.wait_ge(act_done, at("act", f"{tag}_q3"))
                attention(tag, XA_UNITS, 2 * P,
                          lambda u: (XQ[:, u // 2, (u % 2) * P:(u % 2 + 1) * P], XK[:, u // 2, :]),
                          lambda u, l: XV[:, l, (u // 2) * P:(u // 2 + 1) * P],
                          lambda u: ps[:, 6 + u // 2 % 2, (u % 2) * P:(u % 2 + 1) * P])
                row_products(tag, 4, lambda r: XO[:, r, :], ("dve", lambda r: f"{tag}_o7"))
                sums_post(tag + "b")

            def group_norm(tag, buf, what, sq, ready):
                for q in range(2):
                    pe.wait_ge(*after(*ready(q)))
                    s.step(pe.matmul(ps[:, q, :], what, buf[:, 2 * q:2 * q + 2, :], start=True, stop=True).then_inc(pe_done, 1), f"{tag}_mean{q}")
                for q in range(2):
                    pe.wait_ge(act_done, at("act", f"{tag}_sq{q}"))
                    s.step(pe.matmul(ps[:, 2 + q, :], what, sq[:, q, :], start=True, stop=True).then_inc(pe_done, 1), f"{tag}_var{q}")

            column_sums(ps[:, 2, 0:T], lambda k: H[:, k, 0:T], KT, "memsum", wait=("act", "memsq"))
            ffn("f0")

            if upto < 4:
                plan["panel", "total"] = panels[0]
                return
            sums_post("m0a")
            for u in range(4):
                if u >= 2:
                    pe.wait_ge(act_done, at("act", f"rt_raw{u - 2}"))
                pair(u % 2, f"rt_qk{u}", ("dve", "m0ah") if u == 0 else None)
            for q in range(4):
                if q >= 2:
                    pe.wait_ge(act_done, at("act", f"rt_v{q - 2}"))
                else:
                    pe.wait_ge(dve_done, at("dve", "m0_acc_free"))
                token_major(4 + q % 2, lat_tile, f"rt_v{q}")
            for u in range(2):
                pe.wait_ge(act_done, at("act", f"rt_raw{u + 2}"))
                pair(u % 2, f"rt_g{u}")
            for u in range(7):
                pe.wait_ge(act_done, at("act", f"rt_g{u}" if u < 2 else f"rw_raw{u - 2}"))
                pair(u % 2, f"rw_p{u}")
            for u in range(4):
                if u < 2:
                    pe.wait_ge(act_done, at("act", "m0arms"))
                else:
                    pe.wait_ge(dve_done, at("dve", f"rt_sin{u - 2}"))
                s.step(pe.matmul(ps[:, 2 + u % 2, :], c("rt_rot"), RQK[:, u, :], start=True, stop=True).then_inc(pe_done, 1), f"rt_rot{u}")
            for h in range(4):
                q, k = RQK[:, h // 2, (h % 2) * T:(h % 2 + 1) * T], RQK[:, 2 + h // 2, (h % 2) * T:(h % 2 + 1) * T]
                if h == 0:
                    pe.wait_ge(pool_done, at("pool", "rt_cos3"))
                    pe.wait_ge(act_done, at("act", "rt_v3"))
                elif h >= 2:
                    pe.wait_ge(dve_done, at("dve", f"rt_p{h - 2}"))
                pe.matmul(ps[:, 4 + h % 2, 0:T], k[:, 0:P], q, start=True, stop=True, skip_group_check=True)
                s.step(pe.matmul(ps[:, 4 + h % 2, T:T + P], k[:, P:T], q[:, P:T], start=False, stop=True,
                                 skip_group_check=True).then_inc(pe_done, 1), f"rt_s{h}")
            for h in range(4):
                pe.wait_ge(dve_done, at("dve", f"rt_p{h}"))
                if h >= 2:
                    pe.wait_ge(act_done, at("act", f"rt_o{h - 2}"))
                pe.matmul(ps[:, 6 + h % 2, 0:T], RV[:, 0, h * P:(h + 1) * P], RP[:, h % 2, 0:T], start=True, stop=False,
                          skip_group_check=True)
                s.step(pe.matmul(ps[:, 6 + h % 2, P:T], RV[:, 1, h * P:(h + 1) * P], RP[:, h % 2, T:T + P], start=False,
                                 stop=True, skip_group_check=True).then_inc(pe_done, 1), f"rt_pv{h}")
            pe.wait_ge(act_done, at("act", "rw_raw6"))
            pe.wait_ge(dve_done, at("dve", "rt_sin3"))
            group_norm("rt", RO, ones, GSQ, lambda q: ("act", f"rt_o{2 * q + 1}"))

            w = panel()
            pe.wait_ge(act_done, at("act", "rw_tanh"))
            pe.wait_ge(dve_done, at("dve", "rt_gn"))
            for m in range(4):
                for rows, bank, out_cols in ((slice(0, 64), 0, m), (slice(64, P), 2, m)):
                    pe.matmul(ps[:, bank + m // 2, (m % 2) * T:(m % 2 + 1) * T], w[rows, m * P:(m + 1) * P],
                              P2[rows, 12, :], start=(m % 2 == 0), stop=True, skip_group_check=True)
            for m in range(4):
                ins = pe.matmul(ps[:, 4 + m // 2, (m % 2) * T:(m % 2 + 1) * T], w[:, 512 + m * P:512 + (m + 1) * P],
                                P2[:, 13, :], start=(m % 2 == 0), stop=True, skip_group_check=True)
            used(ins, "rw_low")
            for q in range(2):
                pe.wait_ge(dve_done, at("dve", "rw_kk2"))
                s.step(pe.matmul(ps[:, 6 + q, :], blk, EX[:, q * 512:(q + 1) * 512], start=True, stop=True).then_inc(pe_done, 1), f"rw_kksum{q}")
            for q in range(2):
                pe.wait_ge(act_done, at("act", "rw_g"))
                pe.wait_ge(dve_done, at("dve", "rw_rk"))
                s.step(pe.matmul(ps[:, 4 + q, :], blk, LW[:, q * 512:(q + 1) * 512], start=True, stop=True).then_inc(pe_done, 1), f"rw_bon{q}")
            n = 0
            for name, src, ready in (("v", P2[:, 8:12, :], "rw_p2"), ("a", AR[:, :, 0, :], "rw_ahat"),
                                     ("b", BC, "rw_bc"), ("k", KC, "rw_kc")):
                pe.wait_ge(dve_done, at("dve", ready))
                for t in range(2):
                    if n == 0:
                        pe.wait_ge(act_done, at("act", "rw_sig"))
                    if n >= 2:
                        pe.wait_ge(act_done, at("act", f"rw_tm{n - 2}"))
                    for m in range(4):
                        ins = pe.transpose(ps[:, n % 2, m * P:(m + 1) * P], src[:, m, t * P:(t + 1) * P], ident)
                    s.step(ins.then_inc(pe_done, 1), f"rw_tm{n}")
                    n += 1
            pe.wait_ge(act_done, at("act", "rw_tm7"))
            pe.wait_ge(dve_done, at("dve", "rw_bonus"))
            pe.wait_ge(dve_done, at("dve", "rw_kkn"))
            for t in range(2):
                for h in range(8):
                    u, m, lo = t * 8 + h, h // 2, lo_of(h)
                    bank = 4 + h % 4
                    if u >= 4:
                        pe.wait_ge(dve_done, at("dve", f"rw_mm{u - 4}"))
                    ar = AR[lo:lo + 64, m, :, t * P:(t + 1) * P]
                    pe.matmul(ps[:, bank, 0:T].rearrange("p (x t) -> p x t", x=2), BF[lo:lo + 64, m, t * P:(t + 1) * P], ar,
                              start=True, stop=True, skip_group_check=True)
                    s.step(pe.matmul(ps[:, bank, T:2 * T].rearrange("p (x t) -> p x t", x=2),
                                     KF[lo:lo + 64, m, t * P:(t + 1) * P], ar, start=False, stop=True,
                                     skip_group_check=True).then_inc(pe_done, 1), f"rw_mm{u}")
                for n in range(RW_LEVELS):
                    for q in range(2):
                        pe.wait_ge(pool_done, at("pool", f"rw_al{t}_{n}_{q}"))
                        if n:
                            pe.wait_ge(dve_done, at("dve", f"rw_t{t}_{n - 1}_{q}"))
                        elif q == 0:
                            pe.wait_ge(dve_done, at("dve", f"rw_mm{t * 8 + 7}"))
                        for h in range(4 * q, 4 * q + 4):
                            ins = pe.matmul(ps[:, 3 * q, (h % 4) * P:(h % 4 + 1) * P], AL[:, h, :],
                                            TI[:, h, :] if n else ident, start=True, stop=True, skip_group_check=True)
                        s.step(ins.then_inc(pe_done, 1), f"rw_x{t}_{n}_{q}")
                    if n == 0:
                        continue
                    for q in range(2):
                        pe.wait_ge(act_done, at("act", f"rw_x{t}_{n}_{q}"))
                        if n < RW_LEVELS - 1:
                            for h in range(4 * q, 4 * q + 4):
                                ins = pe.matmul(ps[:, 3 * q + 1, (h % 4) * P:(h % 4 + 1) * P], TT[:, h, :], XB[:, h, :],
                                                start=True, stop=True, skip_group_check=True)
                            s.step(ins.then_inc(pe_done, 1), f"rw_dt{t}_{n}_{q}")
                        for h in range(4 * q, 4 * q + 4):
                            ins = pe.matmul(ps[:, 3 * q + 2, (h % 4) * P:(h % 4 + 1) * P], XB[:, h, :], TT[:, h, :],
                                            start=True, stop=True, skip_group_check=True)
                        s.step(ins.then_inc(pe_done, 1), f"rw_dtt{t}_{n}_{q}")
                for h in range(8):
                    ins = pe.matmul(ps[:, 6, h * 64:(h + 1) * 64], MA[:, h, 1, :], VT[:, t, h * 64:(h + 1) * 64],
                                    start=True, stop=True, skip_group_check=True)
                s.step(ins.then_inc(pe_done, 1), f"rw_w1_{t}")
                pe.wait_ge(act_done, at("act", f"rw_w1_{t}"))
                pe.wait_ge(dve_done, at("dve", f"rw_t{t}_{RW_LEVELS - 1}_1"))
                for h in range(8):
                    ins = pe.matmul(ps[:, 7, h * 64:(h + 1) * 64], TT[:, h, :], W1[:, h * 64:(h + 1) * 64],
                                    start=True, stop=True, skip_group_check=True)
                s.step(ins.then_inc(pe_done, 1), f"rw_tv{t}")
                for h in range(8):
                    lo = lo_of(h)
                    ins = pe.matmul(ps[lo:lo + 64, 1, (h // 2) * P:(h // 2 + 1) * P], AT[:, t, h * 64:(h + 1) * 64],
                                    TT[:, h, :], start=True, stop=True, skip_group_check=True)
                s.step(ins.then_inc(pe_done, 1), f"rw_ta{t}")
                pe.wait_ge(act_done, at("act", f"rw_tv{t}"))
            for ch in range(4):
                t, lo = ch // 2, 64 * (ch % 2)
                if ch:
                    pe.wait_ge(act_done, at("act", "rw_ta1"))
                    pe.wait_ge(dve_done, at("dve", f"rw_s{ch}"))
                    for h in range(8):
                        kl = lo_of(h)
                        ins = pe.matmul(ps[lo:lo + 64, 2 + h % 2, (h // 2) * 64:(h // 2 + 1) * 64],
                                        TAT[kl:kl + 64, h // 2, ch * 64:(ch + 1) * 64], SK[kl:kl + 64, ch, h // 2, :],
                                        start=True, stop=True, skip_group_check=True)
                    s.step(ins.then_inc(pe_done, 1), f"rw_u{ch}")
                pe.wait_ge(dve_done, at("dve", f"rw_u{ch}"))
                if ch < 3:
                    for h in range(8):
                        kl = lo_of(h)
                        dst = ps[kl:kl + 64, 4 + ch % 2, (h // 2) * 64:(h // 2 + 1) * 64]
                        pe.matmul(dst, BT[lo:lo + 64, t, h * 64:(h + 1) * 64], UB[lo:lo + 64, t, h, :], start=True,
                                  stop=False, skip_group_check=True)
                        ins = pe.matmul(dst, KTM[lo:lo + 64, t, h * 64:(h + 1) * 64], VT[lo:lo + 64, t, h * 64:(h + 1) * 64],
                                        start=False, stop=True, skip_group_check=True)
                    s.step(ins.then_inc(pe_done, 1), f"rw_s{ch + 1}")
                if ch % 2 == 0:
                    continue
                if t:
                    pe.wait_ge(dve_done, at("dve", "rw_y0"))
                for h in range(8):
                    u, m, kl = t * 8 + h, h // 2, lo_of(h)
                    bank = 6 + h % 2
                    dst = lambda a, b: ps[kl:kl + 64, bank, m * P + a:m * P + b]
                    pe.matmul(dst(0, P), VT[:, t, h * 64:(h + 1) * 64], MR[:, u, 1, :], start=True, stop=False,
                              skip_group_check=True)
                    ins = pe.matmul(dst(0, P), UB[:, t, h, :], MR[:, u, 0, :], start=False, stop=(t == 0),
                                    skip_group_check=True)
                    for cc in (2 * t, 2 * t + 1):
                        if cc:
                            a = 64 * (cc % 2)
                            ins = pe.matmul(dst(a, a + 64), SK[kl:kl + 64, cc, m, :],
                                            AR[kl:kl + 64, m, 1, cc * 64:(cc + 1) * 64], start=False, stop=True,
                                            skip_group_check=True)
                s.step(ins.then_inc(pe_done, 1), f"rw_y{t}")
            pe.wait_ge(dve_done, at("dve", "rw_u3"))
            group_norm("rw", YR, blk, WSQ, lambda q: ("dve", "rw_y1"))
            out_tiles("m0", lambda k: ("dve", f"yb{k - 4}" if k >= 4 else f"ya{k}"))
            sums_post("m0b")
            if upto < 5:
                plan["panel", "total"] = panels[0]
                return
            xattn("x0")
            ffn("f1")
            ffn("f2")

            sums_post("m1a")
            banks = lambda n: n % 2
            n = 0
            for n in range(2):
                w = panel()
                for k in range(KT):
                    if n == 0:
                        pe.wait_ge(dve_done, at("dve", f"m1ah{k}"))
                    ins = pe.matmul(ps[:, 0, n * T:(n + 1) * T], w[:, k * P:(k + 1) * P], HL(k),
                                    start=(k == 0 and n == 0), stop=(k == KT - 1), skip_group_check=True)
                used(ins, "ds_cq")
            for n, name in ((0, "ds_ckv"), (1, "ds_ki")):
                w = panel()
                for k in range(KT):
                    ins = pe.matmul(ps[:, 1, n * T:(n + 1) * T], w[:, k * P:(k + 1) * P], HL(k),
                                    start=(k == 0 and n == 0), stop=(k == KT - 1), skip_group_check=True)
                used(ins, name)
            w = panel()
            pe.wait_ge(act_done, at("act", "m1arms"))
            for t in range(2):
                for k in range(KT):
                    ins = pe.matmul(ps[:, 3, t * 8:(t + 1) * 8], lat_tile(k, t), w[:, k * P:k * P + 8],
                                    start=(k == 0 and t == 0), stop=(k == KT - 1), skip_group_check=True)
            used(ins, "ds_w")
            pe.wait_ge(dve_done, at("dve", "m1_acc_free"))
            for u in range(6):
                if u >= 2:
                    pe.wait_ge(act_done, at("act", f"sc_raw{u - 2}"))
                pair(4 + u % 2, f"sc_p{u}")
            for q in range(2):
                pe.wait_ge(act_done, at("act", f"ds_sq{q}"))
                ins = pe.matmul(ps[:, 2, 0:T], ones, SQD[:, q, :], start=(q == 0), stop=(q == 1), skip_group_check=True)
            s.step(ins.then_inc(pe_done, 1), "ds_cqsum")
            pe.wait_ge(act_done, at("act", "ds_sq2"))
            pe.wait_ge(act_done, at("act", "ds_w"))
            s.step(pe.matmul(ps[:, 3, 0:T], ones, SQD[:, 2, :], start=True, stop=True).then_inc(pe_done, 1), "ds_kvsum")
            for name, dst in (("ds_q", 0), ("ds_qi", 6)):
                w = panel()
                pe.wait_ge(dve_done, at("dve", "ds_cqn"))
                pe.wait_ge(act_done, at("act", "ds_ki"))
                for m in range(4):
                    for r in range(2):
                        ins = pe.matmul(ps[:, dst + m // 2, (m % 2) * T:(m % 2 + 1) * T],
                                        w[:, r * 512 + m * P:r * 512 + (m + 1) * P], CQ[:, r, :],
                                        start=(r == 0 and m % 2 == 0), stop=(r == 1), skip_group_check=True)
                used(ins, name)
            pe.wait_ge(dve_done, at("dve", "ds_ckvn"))
            pe.wait_ge(act_done, at("act", "sc_raw5"))
            for t in range(2):
                ins = pe.transpose(ps[:, 4, t * P:(t + 1) * P], CKV[:, t * P:(t + 1) * P], ident)
            s.step(ins.then_inc(pe_done, 1), "ds_ckt")
            pe.wait_ge(act_done, at("act", "ds_qi"))
            for u in range(16):
                h, t = u // 2, u % 2
                lo = lo_of(h)
                if u >= 4:
                    pe.wait_ge(act_done, at("act", f"ds_rl{u - 4}"))
                bank = 4 + (h % 2) * 2 + t
                if u == 0:
                    pe.wait_ge(act_done, at("act", "ds_ckt"))
                s.step(pe.matmul(ps[:, bank, 0:(t + 1) * P], QI[lo:lo + 64, h // 2, t * P:(t + 1) * P],
                                 KI[lo:lo + 64, 0:(t + 1) * P], start=True, stop=True).then_inc(pe_done, 1), f"ds_l{u}")
            uk = panel()
            pe.wait_ge(act_done, at("act", "ds_q"))
            for h in range(8):
                lo = lo_of(h)
                if h < 2:
                    pe.wait_ge(dve_done, at("dve", "ds_ckvn"))
                else:
                    pe.wait_ge(act_done, at("act", f"ds_ql{h - 2}"))
                s.step(pe.matmul(ps[:, 2 + h % 2, 0:T], uk[lo:lo + 64, (h // 2) * P:(h // 2 + 1) * P],
                                 DQ[lo:lo + 64, h // 2, :], start=True, stop=True).then_inc(pe_done, 1), f"ds_ql{h}")
            pe.wait_ge(act_done, at("act", "ds_ql7"))
            attention("dsa", DSA_UNITS, None,
                      lambda u: (QL[:, u // 2, (u % 2) * P:(u % 2 + 1) * P], CKV[:, 0:(u % 2 + 1) * P]),
                      lambda u, l: CKT[:, l, :],
                      lambda u: ps[:, 6 + u // 2 % 2, (u % 2) * P:(u % 2 + 1) * P])
            pe.wait_ge(dve_done, at("dve", "dsa_o15"))
            for h in range(8):
                lo = lo_of(h)
                ins = pe.matmul(ps[lo:lo + 64, h // 4, (h // 2 % 2) * T:(h // 2 % 2 + 1) * T],
                                uk[:, 512 + h * 64:512 + (h + 1) * 64], OL[:, h, :], start=True, stop=True,
                                skip_group_check=True)
            used(ins, "ds_uv")
            out_tiles("m1", lambda k: ("dve", f"yd{k - 4}") if k >= 4 else ("act", f"yc{k // 2}"))
            sums_post("m1b")
            xattn("x1")
            ffn("f3")
            plan["panel", "total"] = panels[0]

        @block.scalar
        def _(act):
            s = Steps("act", act, plan)
            act.dma_start(con[:, :], const).then_inc(inputs_in[0], 16)
            act.dma_start(vecs[:, :], vec).then_inc(inputs_in[1], 16)
            act.dma_start(X[:, :, :], xs).then_inc(inputs_in[2], 16)

            def squares(tag, src, dst, tiles, wait=None):
                for k in range(tiles):
                    if wait:
                        act.wait_ge(sems[wait[0]], at(wait[0], wait[1].format(k)))
                    s.step(act.activation(dst(k), src(k), ACT.Square).then_inc(act_done, 1), f"{tag}sq{k}")

            def rms(tag, width, n, eps=eps6):
                act.wait_ge(pe_done, at("pe", tag + "sum"))
                s.step(act.activation(RS[:, 0, 0:width], ps[:, 2, 0:width], ACT.Sqrt, bias=eps, scale=1.0 / n).then_inc(act_done, 1),
                       tag + "rms")

            def mod_norm(tag, layer, which, segs, wait, last_panel):
                t0, t1 = min(segs) * T, (max(segs) + 1) * T
                act.wait_ge(panels_used, at("panel", last_panel)) if last_panel else None
                squares(tag, lambda k: X[:, k, t0:t1], lambda k: H[:, k, t0:t1], KT, wait)
                rms(tag, t1 - t0, D)
                for k in range(KT):
                    for g in segs:
                        act.wait_ge(dve_done, at("dve", f"{tag}g{k}_{g}"))
                        m = layer * 48 + 24 * which + k
                        ins = act.activation(H[:, k, g * T:(g + 1) * T], H[:, k, g * T:(g + 1) * T], ACT.Identity,
                                             bias=MOD[:, m, g:g + 1])
                        s.step(ins.then_inc(act_done, 1), f"{tag}h{k}" if g == segs[-1] else None)

            def hidden_act(tag, tiles, kinds, func):
                s.base(tag)
                p0, d0 = at("panel", tag), at("dve", tag)
                per = kinds + 1
                body = RING // per

                def tile_(t, i=None):
                    turn = 0 if i is None else i
                    value = p0 + (kinds if t == 0 else per * t + kinds - 1)
                    act.wait_ge(panels_used, value if i is None else value + i * RING)
                    if i is not None or t >= 2:
                        act.wait_ge(sems["dve"], d0 + t - 1 if i is None else d0 + t - 1 + i * body)
                    s.step(act.activation(HS[:, t % 2, 0:T], ps[:, t % 2, 0:T], func).then_inc(act_done, 1))

                n = (tiles - 2) // body
                tile_(0)
                tile_(1)
                with s.loop(n) as i:
                    for b in range(body):
                        tile_(2 + b, i)
                for t in range(2 + n * body, tiles):
                    tile_(t)

            act.wait_ge(inputs_in[1], 16)
            s.step(act.activation(SC[:, :], v("c", 0, 16), ACT.Silu).then_inc(act_done, 1), "silu_c")
            act.wait_ge(inputs_in[0], 16)
            act.wait_ge(inputs_in[2], 16)
            mod_norm("n0", 0, 0, (0, 1), None, None)
            for j in range(KT):
                act.wait_ge(panels_used, at("panel", f"pw1_{j}_1"))
                if j >= 2:
                    act.wait_ge(dve_done, at("dve", f"glu{j - 2}"))
                s.step(act.activation(SG[:, j % 2, :], ps[:, 2 * (j % 2) + 1, :], ACT.Sigmoid).then_inc(act_done, 1), f"sig{j}")
            act.wait_ge(panels_used, at("panel", "pw1_7_1"))
            squares("ln_", lambda k: CV[:, k, :], lambda k: H[:, k, :], KT, ("dve", "ln_c{}"))
            act.wait_ge(pe_done, at("pe", "ln_var"))
            s.step(act.activation(RS[:, 0, :], ps[:, 2, :], ACT.Sqrt, bias=eps6, scale=1.0 / D).then_inc(act_done, 1), "ln_rms")
            for k in range(KT):
                act.wait_ge(dve_done, at("dve", f"ln_n{k}"))
                s.step(act.activation(H[:, k, :], CV[:, k, :], ACT.Silu, bias=v("ln_b", k), scale=v("ln_g", k)).then_inc(act_done, 1),
                       f"ln_h{k}")
            if upto < 1:
                return
            mod_norm("n1", 0, 1, (0, 1), ("dve", "pw2_{}"), "pw2_7")
            hidden_act("mlp0c", FF1_TILES, 1, ACT.Relu)
            hidden_act("mlp0l", FF1_TILES, 1, ACT.Relu)
            if upto < 2:
                return
            mod_norm("n2", 1, 0, (0, 1), ("dve", "mlp0l_x{}"), "mlp0l.last")
            for u in range(8):
                act.wait_ge(panels_used, at("panel", f"kq{u}"))
                s.step(act.copy(KQ[:, u, :], ps[:, u % 2, :]).then_inc(act_done, 1), f"kq_raw{u}")
                if u == 3:
                    for q in range(2):
                        act.wait_ge(panels_used, at("panel", f"gv{q}"))
                        s.step(act.copy(GV[:, :, q * P:(q + 1) * P], ps[:, 4 + q, :].rearrange("p (t c) -> p t c", t=4)).then_inc(act_done, 1),
                               f"gv{q}")

            def kq_rms(u):
                act.wait_ge(pe_done, at("pe", f"kq_sum{u}"))
                if u >= 2:
                    act.wait_ge(dve_done, at("dve", f"kq_norm{u - 2}"))
                s.step(act.activation(ROT[:, u % 2, :], ps[:, 2 + u % 2, :], ACT.Sqrt, bias=eps6, scale=1.0 / 64).then_inc(act_done, 1),
                       f"kq_rms{u}")

            for u in range(8):
                if u >= 2:
                    act.wait_ge(pe_done, at("pe", f"kq_sum{u - 2}"))
                else:
                    act.wait_ge(act_done, s.n)
                s.step(act.activation(SQ[:, u % 2, :], KQ[:, u, :], ACT.Square).then_inc(act_done, 1), f"kq_sq{u}")
                if u >= 1:
                    kq_rms(u - 1)
            kq_rms(7)

            def attention(tag, units, scale):
                for u in range(len(units) + 1):
                    if u < len(units):
                        L = units[u][2] * P
                        act.wait_ge(dve_done, at("dve", f"{tag}_max{u}"))
                        if u >= 3:
                            act.wait_ge(pe_done, at("pe", f"{tag}_t{u - 3}"))
                        src = SBI[:, u % 2, 0:L] if tag == "dsa" else ps[:, u % 4, 0:L]
                        s.step(act.activation(PR[:, u % 3, 0:L], src, ACT.Exp, bias=AS[:, u % 64, 0:1], scale=scale,
                                              accum_out=AS[:, u % 64, 1:2]).then_inc(act_done, 1), f"{tag}_exp{u}")
                    if u >= 2:
                        pt(tag, units, u - 2)
                pt(tag, units, len(units) - 1)

            def pt(tag, units, w):
                L = units[w][2] * P
                act.wait_ge(pe_done, at("pe", f"{tag}_t{w}"))
                if w >= 2:
                    act.wait_ge(pe_done, at("pe", f"{tag}_pv{w - 2}"))
                s.step(act.copy(PT[:, w % 2, 0:L], ps[:, 4 + w % 2, 0:L]).then_inc(act_done, 1), f"{tag}_pt{w}")

            gqa_units = [(h, t, 4) for h in range(16) for t in range(2)]
            attention("gqa", gqa_units, 64 ** -0.5)
            mod_norm("n3", 1, 1, (1,), ("dve", "wo_{}"), "wo_7")
            hidden_act("mlp1", FF1_TILES, 1, ACT.Relu)
            if upto < 3:
                return

            HL = lambda k: H[:, k, LAT]
            XL = lambda k: X[:, k, LAT]

            def plain_norm(tag, wait, last_panel):
                if last_panel:
                    act.wait_ge(panels_used, at("panel", last_panel))
                squares(tag + "a", XL, HL, KT, wait)
                rms(tag + "a", T, D)

            def post_norm(tag, last_panel):
                act.wait_ge(panels_used, at("panel", last_panel))
                squares(tag + "b", ACC, HL, KT)
                rms(tag + "b", T, D)

            def evacuate(name, key, dst, src, func=ACT.Copy, **kw):
                act.wait_ge(sems[key], at(key, name))
                s.step(act.activation(dst, src, func, **kw).then_inc(act_done, 1), name)

            def ffn(tag, wait, last_panel):
                plain_norm(tag, wait, last_panel)
                hidden_act(tag, FF2_TILES, 2, ACT.Silu)
                post_norm(tag, tag + ".last")

            def xattn(tag, wait, last_panel):
                for h in range(4):
                    evacuate(f"{tag}_k{h}", "panel", XK[:, h, :], ps[:, h % 2, 0:T])
                for q in range(4):
                    evacuate(f"{tag}_v{q}", "panel", XV[:, :, q * P:(q + 1) * P],
                             ps[:, q % 2, 0:T].rearrange("p (t c) -> p t c", t=2))
                plain_norm(tag, wait, last_panel)
                for h in range(4):
                    evacuate(f"{tag}_q{h}", "panel", XQ[:, h, :], ps[:, h % 2, 0:T])
                attention(tag, XA_UNITS, P ** -0.5)
                post_norm(tag, f"{tag}_out3")

            def group_norm(tag, buf, sq, rr, n, eps):
                for q in range(2):
                    act.wait_ge(dve_done, at("dve", f"{tag}_cen{q}"))
                    s.step(act.activation(sq[:, q, :], buf[:, 2 * q:2 * q + 2, :], ACT.Square).then_inc(act_done, 1), f"{tag}_sq{q}")
                for q in range(2):
                    act.wait_ge(pe_done, at("pe", f"{tag}_var{q}"))
                    s.step(act.activation(rr[:, q, :], ps[:, 2 + q, :], ACT.Sqrt, bias=eps, scale=1.0 / n).then_inc(act_done, 1), f"{tag}_rms{q}")

            act.wait_ge(dve_done, at("dve", "n2g7_1"))
            act.dma_start(MEMN, mem).then_inc(inputs_in[3], 16)
            act.wait_ge(inputs_in[3], 16)
            act.wait_ge(panels_used, at("panel", "gqa_w"))
            squares("mem", lambda k: MEMN[:, k, :], lambda k: H[:, k, 0:T], KT)
            rms("mem", T, D)
            act.wait_ge(dve_done, at("dve", "mem_n"))
            ffn("f0", ("dve", "mlp1_x{}"), "mlp1.last")
            if upto < 4:
                return
            plain_norm("m0", ("pool", "f0_x{}"), None)
            for u in range(4):
                evacuate(f"rt_qk{u}", "panel", RQK[:, u, :], ps[:, u % 2, :])
                plan["act", f"rt_raw{u}"] = s.n
            for q in range(4):
                evacuate(f"rt_v{q}", "panel", RV[:, :, q * P:(q + 1) * P],
                         ps[:, 4 + q % 2, 0:T].rearrange("p (t c) -> p t c", t=2))
            for u in range(2):
                evacuate(f"rt_g{u}", "panel", RG[:, 2 * u:2 * u + 2, :], ps[:, u % 2, :].rearrange("p (m t) -> p m t", m=2),
                         ACT.Silu)
            act.wait_ge(pool_done, at("pool", "raw_pad"))
            for u in range(7):
                act.wait_ge(panels_used, at("panel", f"rw_p{u}"))
                if u >= 2:
                    act.wait_ge(dve_done, at("dve", f"rw_shift{u - 2}"))
                s.step(act.copy(RAW[:, u % 2, :, 1:T + 1], ps[:, u % 2, :].rearrange("p (m t) -> p m t", m=2)).then_inc(act_done, 1), f"rw_raw{u}")
            for h in range(4):
                evacuate(f"rt_pv{h}", "pe", RO[:, h, :], ps[:, 6 + h % 2, 0:T])
                plan["act", f"rt_o{h}"] = s.n
            act.wait_ge(dve_done, at("dve", "rw_shift6"))
            s.step(act.activation(P2[0:64, 12, :], P2[0:64, 12, :], ACT.Tanh).then_inc(act_done, 1))
            s.step(act.activation(P2[:, 13, :], P2[:, 13, :], ACT.Sigmoid).then_inc(act_done, 1), "rw_tanh")
            group_norm("rt", RO, GSQ, GRR, P, eps6)
            act.wait_ge(panels_used, at("panel", "rw_low"))
            for m in range(4):
                s.step(act.activation(LW[:, m * T:(m + 1) * T], ps[:, m // 2, (m % 2) * T:(m % 2 + 1) * T], ACT.Sigmoid,
                                      bias=v("w0", m)).then_inc(act_done, 1))
                s.step(act.activation(AA[:, m * T:(m + 1) * T], ps[:, 2 + m // 2, (m % 2) * T:(m % 2 + 1) * T],
                                      ACT.Sigmoid, bias=v("a0", m)).then_inc(act_done, 1), "rw_sig")
            for q in range(2):
                s.step(act.copy(RWG[:, 2 * q:2 * q + 2, :], ps[:, 4 + q, :].rearrange("p (m t) -> p m t", m=2)).then_inc(act_done, 1), "rw_g")
            for q in range(2):
                act.wait_ge(pe_done, at("pe", f"rw_kksum{q}"))
                s.step(act.activation(EX[:, q * 512:(q + 1) * 512], ps[:, 6 + q, :], ACT.Sqrt).then_inc(act_done, 1), f"rw_kkroot")
            act.wait_ge(dve_done, at("dve", "rw_scan"))
            s.step(act.activation(EP, LC, ACT.Exp).then_inc(act_done, 1), "rw_ep")
            s.step(act.activation(EN, LC, ACT.Exp, scale=-1.0).then_inc(act_done, 1), "rw_en")
            act.wait_ge(dve_done, at("dve", "rw_excl"))
            s.step(act.activation(EX, EX, ACT.Exp).then_inc(act_done, 1), "rw_ex")
            n = 0
            for dst in (VT, AT, BT, KTM):
                for t in range(2):
                    evacuate(f"rw_tm{n}", "pe", dst[:, t, :], ps[:, n % 2, :])
                    n += 1
            for t in range(2):
                for n in range(1, RW_LEVELS):
                    for q in range(2):
                        act.wait_ge(pe_done, at("pe", f"rw_x{t}_{n}_{q}"))
                        s.step(act.copy(XB[:, 4 * q:4 * q + 4, :], ps[:, 3 * q, :].rearrange("p (h t) -> p h t", h=4)).then_inc(act_done, 1),
                               f"rw_x{t}_{n}_{q}")
                evacuate(f"rw_w1_{t}", "pe", W1, ps[:, 6, :])
                evacuate(f"rw_tv{t}", "pe", TV[:, t, :], ps[:, 7, :])
                evacuate(f"rw_ta{t}", "pe", TAT[:, :, t * P:(t + 1) * P], ps[:, 1, :].rearrange("p (m t) -> p m t", m=4))
            group_norm("rw", YR, WSQ, WRR, 64, eps_rw)
            act.wait_ge(panels_used, at("panel", "m0_out7"))
            squares("m0b", ACC, HL, KT)
            rms("m0b", T, D)
            if upto < 5:
                return
            xattn("x0", ("pool", "m0_x{}"), None)
            ffn("f1", ("pool", "x0_x{}"), None)
            ffn("f2", ("pool", "f1_x{}"), None)
            plain_norm("m1", ("pool", "f2_x{}"), None)
            act.wait_ge(panels_used, at("panel", "ds_cq"))
            s.step(act.copy(CQ, ps[:, 0, :].rearrange("p (m t) -> p m t", m=2)).then_inc(act_done, 1), "ds_cq")
            act.wait_ge(panels_used, at("panel", "ds_ki"))
            s.step(act.copy(CKV, ps[:, 1, 0:T]).then_inc(act_done, 1), "ds_ckv")
            s.step(act.copy(KI, ps[:, 1, T:2 * T]).then_inc(act_done, 1), "ds_ki")
            act.wait_ge(panels_used, at("panel", "ds_w"))
            s.step(act.activation(WI, ps[:, 3, 0:16].rearrange("p (t h) -> p t h", t=2), ACT.Copy, scale=512 ** -0.5).then_inc(act_done, 1), "ds_w")
            act.wait_ge(act_done, s.n)
            for q in range(2):
                s.step(act.activation(SQD[:, q, :], CQ[:, q, :], ACT.Square).then_inc(act_done, 1), f"ds_sq{q}")
            s.step(act.activation(SQD[:, 2, :], CKV, ACT.Square).then_inc(act_done, 1), "ds_sq2")
            for u in range(6):
                dst = (SHH[:, 2 * u:2 * u + 2, :] if u < 2 else GB[:, 2 * u - 4:2 * u - 2, :] if u < 4 else
                       SU[:, 2 * u - 8:2 * u - 6, 2:T + 2])
                act.wait_ge(panels_used, at("panel", f"sc_p{u}"))
                if u == 4:
                    act.wait_ge(pool_done, at("pool", "su_pad"))
                s.step(act.copy(dst, ps[:, 4 + u % 2, :].rearrange("p (m t) -> p m t", m=2)).then_inc(act_done, 1), f"sc_raw{u}")
            act.wait_ge(pe_done, at("pe", "ds_cqsum"))
            s.step(act.activation(RS[:, 0, 0:T], ps[:, 2, 0:T], ACT.Sqrt, bias=eps6, scale=1.0 / 256).then_inc(act_done, 1), "ds_cqrms")
            act.wait_ge(pe_done, at("pe", "ds_kvsum"))
            s.step(act.activation(RS[:, 1, 0:T], ps[:, 3, 0:T], ACT.Sqrt, bias=eps6, scale=1.0 / 128).then_inc(act_done, 1), "ds_kvrms")
            act.wait_ge(panels_used, at("panel", "ds_q"))
            for q in range(2):
                s.step(act.copy(DQ[:, 2 * q:2 * q + 2, :], ps[:, q, :].rearrange("p (m t) -> p m t", m=2)).then_inc(act_done, 1), "ds_q")
            act.wait_ge(panels_used, at("panel", "ds_qi"))
            for q in range(2):
                s.step(act.copy(QI[:, 2 * q:2 * q + 2, :], ps[:, 6 + q, :].rearrange("p (m t) -> p m t", m=2)).then_inc(act_done, 1), "ds_qi")
            evacuate("ds_ckt", "pe", CKT, ps[:, 4, 0:T].rearrange("p (l c) -> p l c", l=2))
            for u in range(16):
                h, t = u // 2, u % 2
                act.wait_ge(pe_done, at("pe", f"ds_l{u}"))
                if u >= 2:
                    act.wait_ge(dve_done, at("dve", f"ds_sc{u - 2}"))
                s.step(act.activation(RL[:, u % 2, 0:(t + 1) * P], ps[:, 4 + (h % 2) * 2 + t, 0:(t + 1) * P], ACT.Relu).then_inc(act_done, 1), f"ds_rl{u}")
            for h in range(8):
                evacuate(f"ds_ql{h}", "pe", QL[:, h, :], ps[:, 2 + h % 2, 0:T])
            attention("dsa", DSA_UNITS, 64 ** -0.5)
            act.wait_ge(panels_used, at("panel", "ds_uv"))
            for q in range(2):
                s.step(act.copy(Y[:, 2 * q:2 * q + 2, :], ps[:, q, :].rearrange("p (m t) -> p m t", m=2)).then_inc(act_done, 1), f"yc{q}")
            post_norm("m1", "m1_out7")
            xattn("x1", ("pool", "m1_x{}"), None)
            ffn("f3", ("pool", "x1_x{}"), None)
            act.wait_ge(pool_done, at("pool", "f3_x7"))
            act.dma_start(out, X[:, :, LAT]).then_inc(out_stored, 16)
            act.wait_ge(out_stored, 16)

        @block.vector
        def _(dve):
            s = Steps("dve", dve, plan)
            mod = lambda layer, which, k, g: MOD[:, layer * 48 + which * 8 + k, g:g + 1]

            def gain_shift(n, layer, gain, which):
                sc = MOD[:, layer * 48 + which * 8:layer * 48 + which * 8 + 8, :]
                s.step(dve.scalar_tensor_tensor(out=GS[:, n, :, :], in0=sc, scalar=1.0,
                                                in1=gain.unsqueeze(2).to_broadcast([P, KT, 2]),
                                                op0=ALU.add, op1=ALU.mult).then_inc(dve_done, 1))

            def invert(tag, width):
                dve.wait_ge(act_done, at("act", tag + "rms"))
                s.step(dve.reciprocal(RS[:, 0, 0:width], RS[:, 0, 0:width]).then_inc(dve_done, 1), tag + "inv")
                dve.wait_ge(dve_done, s.n)

            def mod_norm(tag, n, segs):
                t0 = min(segs) * T
                invert(tag, len(segs) * T)
                for k in range(KT):
                    for g in segs:
                        s.step(dve.scalar_tensor_tensor(
                            out=H[:, k, g * T:(g + 1) * T], in0=X[:, k, g * T:(g + 1) * T],
                            scalar=GS[:, n, k, g:g + 1], in1=RS[:, 0, g * T - t0:(g + 1) * T - t0],
                            op0=ALU.mult, op1=ALU.mult).then_inc(dve_done, 1), f"{tag}g{k}_{g}")

            def hidden_dve(tag, tiles, kinds, squared):
                s.base(tag)
                a0, p0 = at("act", tag), at("panel", tag)
                per = kinds + 1
                body = RING // per

                def tile_(t, i=None):
                    act_value = a0 + t + 1
                    used = p0 + per * (t - 1) + kinds
                    dve.wait_ge(sems["act"], act_value if i is None else act_value + i * body)
                    if i is not None or t >= 2:
                        dve.wait_ge(panels_used, used if i is None else used + i * RING)
                    if squared:
                        ins = dve.tensor_tensor(HT[:, t % 2, 0:T], HS[:, t % 2, 0:T], ps[:, t % 2, 0:T], ALU.mult)
                    else:
                        ins = dve.tensor_tensor(HT[:, t % 2, 0:T], HS[:, t % 2, 0:T], ps[:, t % 2, T:2 * T], ALU.mult)
                    s.step(ins.then_inc(dve_done, 1))

                n = (tiles - 2) // body
                tile_(0)
                tile_(1)
                with s.loop(n) as i:
                    for b in range(body):
                        tile_(2 + b, i)
                for t in range(2 + n * body, tiles):
                    tile_(t)

            def gated_add(src, gate, k, g, name):
                s.step(dve.scalar_tensor_tensor(out=X[:, k, g * T:(g + 1) * T], in0=src, scalar=gate,
                                                in1=X[:, k, g * T:(g + 1) * T], op0=ALU.mult, op1=ALU.add).then_inc(dve_done, 1), name)

            dve.wait_ge(inputs_in[1], 16)
            dve.wait_ge(panels_used, at("panel", "mod15"))
            s.step(dve.tensor_tensor(MOD[:, 0:16, :], ps[:, 7, 0:32].rearrange("p (m g) -> p m g", g=2),
                                     v("b_mod", 0, 16).unsqueeze(2).to_broadcast([P, 16, 2]), ALU.add).then_inc(dve_done, 1), "mod_first")
            dve.wait_ge(dve_done, s.n)
            gain_shift(0, 0, v("norm1", 0, 8), 1)
            dve.wait_ge(inputs_in[2], 16)
            mod_norm("n0", 0, (0, 1))
            dve.wait_ge(pool_done, at("pool", "pad"))
            for j in range(KT):
                dve.wait_ge(act_done, at("act", f"sig{j}"))
                s.step(dve.tensor_tensor(U[:, j, :, PAD:PAD + T],
                                         ps[:, 2 * (j % 2), :].rearrange("p (g t) -> p g t", g=2),
                                         SG[:, j % 2, :].rearrange("p (g t) -> p g t", g=2), ALU.mult).then_inc(dve_done, 1), f"glu{j}")
            cv = lambda j: CV[:, j, :].rearrange("p (g t) -> p g t", g=2)
            for j0 in range(0, KT, 2):
                for tap in range(TAPS):
                    for j in (j0, j0 + 1):
                        src = U[:, j, :, tap:tap + T]
                        w = v("dw", tap * KT + j)
                        dve.wait_ge(dve_done, s.n - 1)
                        if tap == 0:
                            ins = dve.tensor_scalar(cv(j), src, w, v("dw_b", j), ALU.mult, ALU.add)
                        else:
                            ins = dve.scalar_tensor_tensor(out=cv(j), in0=src, scalar=w, in1=cv(j),
                                                           op0=ALU.mult, op1=ALU.add)
                        s.step(ins.then_inc(dve_done, 1), f"conv{j}" if tap == TAPS - 1 else None)
            dve.wait_ge(pe_done, at("pe", "ln_mean"))
            s.step(dve.tensor_scalar(RS[:, 1, :], ps[:, 0, :], 1.0 / D, None, ALU.mult).then_inc(dve_done, 1))
            dve.wait_ge(dve_done, s.n)
            for k in range(KT):
                s.step(dve.tensor_tensor(CV[:, k, :], CV[:, k, :], RS[:, 1, :], ALU.subtract).then_inc(dve_done, 1), f"ln_c{k}")
            dve.wait_ge(act_done, at("act", "ln_rms"))
            s.step(dve.reciprocal(RS[:, 0, :], RS[:, 0, :]).then_inc(dve_done, 1))
            dve.wait_ge(dve_done, s.n)
            for k in range(KT):
                s.step(dve.tensor_tensor(CV[:, k, :], CV[:, k, :], RS[:, 0, :], ALU.mult).then_inc(dve_done, 1), f"ln_n{k}")
            dve.wait_ge(panels_used, at("panel", "mod_all"))
            s.step(dve.tensor_tensor(MOD[:, 16:96, :], ps[:, 7, 32:192].rearrange("p (m g) -> p m g", g=2),
                                     v("b_mod", 16, 80).unsqueeze(2).to_broadcast([P, 80, 2]), ALU.add).then_inc(dve_done, 1), "mod_rest")
            dve.wait_ge(dve_done, s.n)
            gain_shift(1, 0, v("norm2", 0, 8), 4)
            gain_shift(2, 1, v("norm1", 8, 8), 1)
            gain_shift(3, 1, v("norm2", 8, 8), 4)
            for j in range(KT):
                dve.wait_ge(panels_used, at("panel", f"pw2_{j}"))
                gated_add(ps[:, j % 2, 0:T], mod(0, 2, j, 0), j, 0, None)
                gated_add(ps[:, j % 2, T:2 * T], mod(0, 2, j, 1), j, 1, f"pw2_{j}")
            if upto < 1:
                return
            mod_norm("n1", 1, (0, 1))
            s.base("mlp0c.acc_free")
            hidden_dve("mlp0c", FF1_TILES, 1, True)
            dve.wait_ge(panels_used, at("panel", "mlp0c.last"))
            for k in range(KT):
                gated_add(ACC(k), mod(0, 5, k, 0), k, 0, f"mlp0c_x{k}")
            s.base("mlp0l.acc_free")
            hidden_dve("mlp0l", FF1_TILES, 1, True)
            dve.wait_ge(panels_used, at("panel", "mlp0l.last"))
            for k in range(KT):
                gated_add(ACC(k), mod(0, 5, k, 1), k, 1, f"mlp0l_x{k}")
            if upto < 2:
                return
            mod_norm("n2", 2, (0, 1))
            for u in range(8):
                dve.wait_ge(act_done, at("act", f"kq_rms{u}"))
                s.step(dve.reciprocal(ROT[:, u % 2, :], ROT[:, u % 2, :]).then_inc(dve_done, 1))
                dve.wait_ge(dve_done, s.n)
                s.step(dve.scalar_tensor_tensor(out=KQ[:, u, :], in0=KQ[:, u, :], scalar=v("gqa_k" if u < 4 else "gqa_q"),
                                                in1=ROT[:, u % 2, :], op0=ALU.mult, op1=ALU.mult).then_inc(dve_done, 1), f"kq_norm{u}")
            for u in range(8):
                dve.wait_ge(pe_done, at("pe", f"kq_rot{u}"))
                if u >= 2:
                    dve.wait_ge(pool_done, at("pool", f"kq_cos{u - 2}"))
                dve.wait_ge(dve_done, s.n)
                for half in range(2):
                    sin = c("gqa_sin")[:, half * T:(half + 1) * T] if u < 4 else c("gqa_sin")[:, T:2 * T]
                    ins = dve.tensor_tensor(ROT[:, u % 2, half * T:(half + 1) * T], ps[:, u % 2, half * T:(half + 1) * T],
                                            sin, ALU.mult)
                    s.step(ins.then_inc(dve_done, 1), f"kq_sin{u}" if half else None)
            dve.wait_ge(pool_done, at("pool", "kq_cos7"))
            s.base("kq_done0")
            s.step(dve.memset(small[:, 0:1], 0.0).then_inc(dve_done, 1), "kq_done")

            def attention(tag, units, scale, out_src, out_dst, bias=None):
                for u in range(len(units) + 3):
                    if u < len(units):
                        L = units[u][2] * P
                        dve.wait_ge(pe_done, at("pe", f"{tag}_s{u}"))
                        if bias is not None:
                            if u >= 2:
                                dve.wait_ge(act_done, at("act", f"{tag}_exp{u - 2}"))
                            s.step(dve.tensor_tensor(SBI[:, u % 2, 0:L], ps[:, u % 4, 0:L], bias(u), ALU.add).then_inc(dve_done, 1), f"{tag}_bias{u}")
                            dve.wait_ge(dve_done, s.n)
                            src = SBI[:, u % 2, 0:L]
                        else:
                            src = ps[:, u % 4, 0:L]
                        s.step(dve.reduce_max(AS[:, u % 64, 2:3], src, AX).then_inc(dve_done, 1))
                        dve.wait_ge(dve_done, s.n)
                        s.step(dve.tensor_scalar(AS[:, u % 64, 0:1], AS[:, u % 64, 2:3], -scale, None, ALU.mult).then_inc(dve_done, 1),
                               f"{tag}_max{u}")
                    if 1 <= u <= len(units):
                        w = u - 1
                        L = units[w][2] * P
                        dve.wait_ge(act_done, at("act", f"{tag}_exp{w}"))
                        s.step(dve.reciprocal(AS[:, w % 64, 3:4], AS[:, w % 64, 1:2]).then_inc(dve_done, 1))
                        dve.wait_ge(dve_done, s.n)
                        s.step(dve.tensor_scalar(PR[:, w % 3, 0:L], PR[:, w % 3, 0:L], AS[:, w % 64, 3:4], None,
                                                 ALU.mult).then_inc(dve_done, 1), f"{tag}_p{w}")
                    w = u - 3
                    if w >= 0 and w % 2:
                        dve.wait_ge(pe_done, at("pe", f"{tag}_pv{w}"))
                        s.step(dve.tensor_copy(out_dst(w), out_src(w)).then_inc(dve_done, 1), f"{tag}_o{w}")

            gqa_units = [(h, t, 4) for h in range(16) for t in range(2)]

            def gqa_part(buf, w, where):
                h, t, _ = gqa_units[w]
                lo = 64 * (h % 2)
                return GO[lo:lo + 64, h // 2, :] if where else ps[lo:lo + 64, 6 + h % 2, 0:T]

            attention("gqa", gqa_units, 64 ** -0.5, lambda w: gqa_part(0, w, 0), lambda w: gqa_part(0, w, 1))
            for j in range(KT):
                dve.wait_ge(panels_used, at("panel", f"wo_{j}"))
                gated_add(ps[:, j % 2, 0:T], mod(1, 2, j, 1), j, 1, f"wo_{j}")
            mod_norm("n3", 3, (1,))
            s.base("mlp1.acc_free")
            hidden_dve("mlp1", FF1_TILES, 1, True)
            dve.wait_ge(panels_used, at("panel", "mlp1.last"))
            for k in range(KT):
                gated_add(ACC(k), mod(1, 5, k, 1), k, 1, f"mlp1_x{k}")
            if upto < 3:
                return

            def plain_norm(tag, which):
                invert(tag + "a", T)
                for k in range(KT):
                    s.step(dve.scalar_tensor_tensor(out=H[:, k, LAT], in0=X[:, k, LAT], scalar=v("norm_g", which * 8 + k),
                                                    in1=RS[:, 0, 0:T], op0=ALU.mult, op1=ALU.mult).then_inc(dve_done, 1), f"{tag}ah{k}")

            def post_norm(tag, gain):
                invert(tag + "b", T)
                for k in range(KT):
                    s.step(dve.scalar_tensor_tensor(out=TMP[:, k, :], in0=ACC(k), scalar=gain(k), in1=RS[:, 0, 0:T],
                                                    op0=ALU.mult, op1=ALU.mult).then_inc(dve_done, 1), f"{tag}_t{k}")

            def ffn(tag, layer, first, half):
                plain_norm(tag, layer * 8 + first)
                s.base(tag + ".acc_free")
                hidden_dve(tag, FF2_TILES, 2, False)
                post_norm(tag, lambda k: HG[:, half, k:k + 1])

            def xattn(tag, layer):
                plain_norm(tag, layer * 8 + 4)
                attention(tag, XA_UNITS, P ** -0.5, lambda w: ps[:, 6 + w // 2 % 2, 0:T], lambda w: XO[:, w // 2, :])
                post_norm(tag, lambda k: v("norm_g", (layer * 8 + 5) * 8 + k))

            def group_norm(tag, buf, rr, n, gain, shift):
                for q in range(2):
                    dve.wait_ge(pe_done, at("pe", f"{tag}_mean{q}"))
                    pairs = buf[:, 2 * q:2 * q + 2, :]
                    s.step(dve.scalar_tensor_tensor(out=pairs, in0=ps[:, q, :].rearrange("p (m t) -> p m t", m=2),
                                                    scalar=-1.0 / n, in1=pairs, op0=ALU.mult, op1=ALU.add).then_inc(dve_done, 1), f"{tag}_cen{q}")
                for q in range(2):
                    dve.wait_ge(act_done, at("act", f"{tag}_rms{q}"))
                    pairs = buf[:, 2 * q:2 * q + 2, :]
                    s.step(dve.reciprocal(rr[:, q, :], rr[:, q, :]).then_inc(dve_done, 1))
                    dve.wait_ge(dve_done, s.n)
                    s.step(dve.tensor_tensor(pairs, pairs, rr[:, q, :].rearrange("p (m t) -> p m t", m=2), ALU.mult).then_inc(dve_done, 1))
                    dve.wait_ge(dve_done, s.n)
                    for m in (2 * q, 2 * q + 1):
                        s.step(dve.tensor_scalar(buf[:, m, :], buf[:, m, :], v(gain, m), v(shift, m), ALU.mult, ALU.add).then_inc(dve_done, 1))
                dve.wait_ge(dve_done, s.n)

            for n, which in enumerate((1, 7, 9, 15)):
                s.step(dve.tensor_scalar(HG[:, n, :], v("norm_g", which * 8, 8), 0.5, None, ALU.mult).then_inc(dve_done, 1))
            invert("mem", T)
            for k in range(KT):
                s.step(dve.scalar_tensor_tensor(out=MEMN[:, k, :], in0=MEMN[:, k, :], scalar=v("mem_g", k),
                                                in1=RS[:, 0, 0:T], op0=ALU.mult, op1=ALU.mult).then_inc(dve_done, 1), "mem_n")
            ffn("f0", 0, 0, 0)
            if upto < 4:
                return
            plain_norm("m0", 2)
            s.base("m0_acc_free")
            for u in range(7):
                dve.wait_ge(act_done, at("act", f"rw_raw{u}"))
                now = RAW[:, u % 2, :, 1:T + 1]
                s.step(dve.tensor_tensor(P2[:, 2 * u:2 * u + 2, :], RAW[:, u % 2, :, 0:T], now, ALU.subtract).then_inc(dve_done, 1))
                dve.wait_ge(dve_done, s.n)
                for m in range(2):
                    p2 = P2[:, 2 * u + m, :]
                    s.step(dve.scalar_tensor_tensor(out=p2, in0=p2, scalar=v("rw_mu", 2 * u + m), in1=now[:, m, :],
                                                    op0=ALU.mult, op1=ALU.add).then_inc(dve_done, 1), f"rw_shift{u}")
            plan["dve", "rw_p2"] = s.n
            for u in range(4):
                dve.wait_ge(pe_done, at("pe", f"rt_rot{u}"))
                if u >= 2:
                    dve.wait_ge(pool_done, at("pool", f"rt_cos{u - 2}"))
                s.step(dve.tensor_tensor(RROT[:, u % 2, :].rearrange("p (m t) -> p m t", m=2),
                                         ps[:, 2 + u % 2, :].rearrange("p (m t) -> p m t", m=2),
                                         c("rt_sin").unsqueeze(1).to_broadcast([P, 2, T]), ALU.mult).then_inc(dve_done, 1), f"rt_sin{u}")
            for h in range(4):
                dve.wait_ge(pe_done, at("pe", f"rt_s{h}"))
                if h >= 2:
                    dve.wait_ge(pe_done, at("pe", f"rt_pv{h - 2}"))
                decay = c("rt_decay")[:, h * T:(h + 1) * T]
                s.step(dve.tensor_tensor(RP[:, h % 2, 0:T], ps[:, 4 + h % 2, 0:T], decay, ALU.mult).then_inc(dve_done, 1))
                s.step(dve.tensor_tensor(RP[:, h % 2, T:T + P], ps[:, 4 + h % 2, T:T + P], decay[:, 0:P], ALU.mult).then_inc(dve_done, 1), f"rt_p{h}")
            group_norm("rt", RO, GRR, P, "rt_g", "rt_b")
            dve.wait_ge(act_done, at("act", "rt_g1"))
            for m in range(4):
                s.step(dve.tensor_tensor(Y[:, 4 + m, :], RO[:, m, :], RG[:, m, :], ALU.mult).then_inc(dve_done, 1), f"yb{m}")
            plan["dve", "rt_gn"] = s.n
            dve.wait_ge(dve_done, s.n)
            r4, k4, v4 = P2[:, 0:4, :], P2[:, 4:8, :], P2[:, 8:12, :]
            four = lambda ap: ap.rearrange("p (m t) -> p m t", m=4)
            for m in range(4):
                s.step(dve.tensor_scalar(KK[:, m * T:(m + 1) * T], P2[:, 4 + m, :], v("k_k", m), None, ALU.mult).then_inc(dve_done, 1))
            dve.wait_ge(dve_done, s.n)
            s.step(dve.tensor_tensor(EX, KK, KK, ALU.mult).then_inc(dve_done, 1), "rw_kk2")
            dve.wait_ge(act_done, at("act", "rw_sig"))
            for m in range(4):
                s.step(dve.tensor_scalar(KP[:, m * T:(m + 1) * T], AA[:, m * T:(m + 1) * T], 1.0, v("k_a", m),
                                         ALU.subtract, ALU.mult).then_inc(dve_done, 1))
            dve.wait_ge(dve_done, s.n)
            s.step(dve.scalar_tensor_tensor(out=four(KP), in0=four(KP), scalar=1.0, in1=k4, op0=ALU.add, op1=ALU.mult).then_inc(dve_done, 1))
            s.step(dve.tensor_scalar(EN, LW, -float(np.exp(-0.5)), None, ALU.mult).then_inc(dve_done, 1))
            dve.wait_ge(pool_done, at("pool", "reset"))
            dve.wait_ge(dve_done, s.n)
            s.step(dve.tensor_tensor_scan(LC, RESET, EN, 0.0, ALU.mult, ALU.add).then_inc(dve_done, 1), "rw_scan0")
            dve.wait_ge(dve_done, s.n)
            s.step(dve.tensor_tensor(four(LW), r4, four(KP), ALU.mult).then_inc(dve_done, 1))
            dve.wait_ge(dve_done, s.n)
            for m in range(4):
                s.step(dve.tensor_scalar(LW[:, m * T:(m + 1) * T], LW[:, m * T:(m + 1) * T], v("r_k", m), None, ALU.mult).then_inc(dve_done, 1), "rw_rk")
            dve.wait_ge(act_done, at("act", "rw_kkroot"))
            s.step(dve.tensor_scalar(EX, EX, 1e-12, None, ALU.max).then_inc(dve_done, 1))
            dve.wait_ge(dve_done, s.n)
            s.step(dve.reciprocal(EX, EX).then_inc(dve_done, 1))
            dve.wait_ge(dve_done, s.n)
            s.step(dve.tensor_tensor(KK, KK, EX, ALU.mult).then_inc(dve_done, 1), "rw_kkn")
            dve.wait_ge(dve_done, s.n)
            s.step(dve.tensor_tensor(EX, LC, EN, ALU.subtract).then_inc(dve_done, 1), "rw_excl")
            plan["dve", "rw_scan"] = s.n
            s.step(dve.tensor_tensor(AA, AA, KK, ALU.mult).then_inc(dve_done, 1))
            for q in range(2):
                dve.wait_ge(pe_done, at("pe", f"rw_bon{q}"))
                s.step(dve.tensor_tensor(BON[:, 2 * q:2 * q + 2, :], ps[:, 4 + q, :].rearrange("p (m t) -> p m t", m=2),
                                         P2[:, 8 + 2 * q:10 + 2 * q, :], ALU.mult).then_inc(dve_done, 1), "rw_bonus")
            dve.wait_ge(act_done, at("act", "rw_ep"))
            dve.wait_ge(pe_done, at("pe", "rt_mean1"))
            s.step(dve.tensor_tensor(AR[:, :, 1, :], r4, four(EP), ALU.mult).then_inc(dve_done, 1), "rw_rhat")
            s.step(dve.tensor_copy(PC, four(EP).rearrange("p m (c t) -> p m c t", c=4)[:, :, :, RW_C - 1]).then_inc(dve_done, 1), "rw_pc")
            dve.wait_ge(act_done, at("act", "rw_en"))
            dve.wait_ge(dve_done, s.n)
            s.step(dve.tensor_tensor(BF, four(AA), four(EN), ALU.mult).then_inc(dve_done, 1))
            s.step(dve.tensor_tensor(KF, four(KP), four(EN), ALU.mult).then_inc(dve_done, 1))
            dve.wait_ge(act_done, at("act", "rw_ex"))
            s.step(dve.scalar_tensor_tensor(out=AR[:, :, 0, :], in0=four(KK), scalar=-1.0, in1=four(EX), op0=ALU.mult,
                                            op1=ALU.mult).then_inc(dve_done, 1), "rw_ahat")
            dve.wait_ge(dve_done, s.n)
            for src, dst, name in ((BF, BC, "rw_bc"), (KF, KC, "rw_kc")):
                for m in range(4):
                    s.step(dve.tensor_tensor(dst[:, m, :].rearrange("p (c t) -> p c t", c=4),
                                             src[:, m, :].rearrange("p (c t) -> p c t", c=4),
                                             PC[:, m, :].unsqueeze(2).to_broadcast([P, 4, RW_C]), ALU.mult).then_inc(dve_done, 1), name)
            masks = c("rw_mask").rearrange("p (x y t) -> p x y t", x=2, y=2)
            for t in range(2):
                for h in range(8):
                    u = t * 8 + h
                    dve.wait_ge(pe_done, at("pe", f"rw_mm{u}"))
                    if h == 0 and t:
                        dve.wait_ge(pe_done, at("pe", "rw_w1_0"))
                        dve.wait_ge(pool_done, at("pool", f"rw_al0_{RW_LEVELS - 1}_1"))
                    got = ps[:, 4 + h % 4, :].rearrange("p (x y t) -> p x y t", x=2, y=2)
                    s.step(dve.tensor_tensor(MA[:, h, :, :], got[:, :, 0, :], masks[:, :, 0, :], ALU.mult).then_inc(dve_done, 1), f"rw_ma{u}")
                    s.step(dve.tensor_tensor(MR[:, u, :, :], got[:, :, 1, :], masks[:, :, 1, :], ALU.mult).then_inc(dve_done, 1), f"rw_mm{u}")
                for n in range(RW_LEVELS):
                    for q in range(2):
                        hs = slice(4 * q, 4 * q + 4)
                        eye = ident.unsqueeze(1).to_broadcast([P, 4, P])
                        bank = lambda b: ps[:, 3 * q + b, :].rearrange("p (h t) -> p h t", h=4)
                        if n == 0:
                            dve.wait_ge(pe_done, at("pe", f"rw_x{t}_{n}_{q}"))
                            if t and q == 0:
                                dve.wait_ge(pe_done, at("pe", "rw_ta0"))
                            s.step(dve.tensor_tensor(TI[:, hs, :], bank(0), eye, ALU.add).then_inc(dve_done, 1))
                            s.step(dve.tensor_tensor(TT[:, hs, :], AL[:, hs, :], eye, ALU.add).then_inc(dve_done, 1), f"rw_t{t}_{n}_{q}")
                            continue
                        if n < RW_LEVELS - 1:
                            dve.wait_ge(pe_done, at("pe", f"rw_dt{t}_{n}_{q}"))
                            dve.wait_ge(dve_done, s.n)
                            s.step(dve.tensor_tensor(TI[:, hs, :], TI[:, hs, :], bank(1), ALU.add).then_inc(dve_done, 1))
                        dve.wait_ge(pe_done, at("pe", f"rw_dtt{t}_{n}_{q}"))
                        dve.wait_ge(dve_done, s.n)
                        s.step(dve.tensor_tensor(TT[:, hs, :], TT[:, hs, :], bank(2), ALU.add).then_inc(dve_done, 1), f"rw_t{t}_{n}_{q}")
            s.step(dve.memset(SK[:, 0, :, :], 0.0).then_inc(dve_done, 1))
            for ch in range(4):
                t, lo = ch // 2, 64 * (ch % 2)
                rows = slice(lo, lo + 64)
                ub, tv = (ap.rearrange("p (m x) v -> p x m v", x=2) for ap in
                          (UB[rows, t, :, :], TV[rows, t, :].rearrange("p (h v) -> p h v", h=8)))
                if ch == 0:
                    dve.wait_ge(act_done, at("act", "rw_ta1"))
                    s.step(dve.tensor_copy(ub[:, 0, :, :], tv[:, 0, :, :]).then_inc(dve_done, 1))
                    s.step(dve.tensor_copy(ub[:, 1, :, :], tv[:, 1, :, :]).then_inc(dve_done, 1), "rw_u0")
                else:
                    dve.wait_ge(pe_done, at("pe", f"rw_u{ch}"))
                    for x in range(2):
                        s.step(dve.tensor_tensor(ub[:, x, :, :], ps[rows, 2 + x, 0:T].rearrange("p (m v) -> p m v", m=4),
                                                 tv[:, x, :, :], ALU.add).then_inc(dve_done, 1), f"rw_u{ch}")
                if ch < 3:
                    dve.wait_ge(dve_done, s.n)
                    s.step(dve.tensor_tensor(SKP, SK[:, ch, :, :], PC[:, :, ch:ch + 1].to_broadcast([P, 4, 64]), ALU.mult).then_inc(dve_done, 1))
                    dve.wait_ge(pe_done, at("pe", f"rw_s{ch + 1}"))
                    dve.wait_ge(dve_done, s.n)
                    s.step(dve.tensor_tensor(SK[:, ch + 1, :, :], ps[:, 4 + ch % 2, 0:T].rearrange("p (m v) -> p m v", m=4),
                                             SKP, ALU.add).then_inc(dve_done, 1), f"rw_s{ch + 1}")
                if ch % 2:
                    dve.wait_ge(pe_done, at("pe", f"rw_y{t}"))
                    for x in range(2):
                        half = slice(64 * x, 64 * x + 64)
                        s.step(dve.tensor_copy(YR[half, :, t * P:(t + 1) * P],
                                               ps[half, 6 + x, :].rearrange("p (m t) -> p m t", m=4)).then_inc(dve_done, 1), f"rw_y{t}")
            dve.wait_ge(dve_done, s.n)
            group_norm("rw", YR, WRR, 64, "rw_g", "rw_b")
            dve.wait_ge(act_done, at("act", "rw_g"))
            s.step(dve.tensor_tensor(YR, YR, BON, ALU.add).then_inc(dve_done, 1))
            dve.wait_ge(dve_done, s.n)
            for m in range(4):
                s.step(dve.tensor_tensor(Y[:, m, :], YR[:, m, :], RWG[:, m, :], ALU.mult).then_inc(dve_done, 1), f"ya{m}")
            dve.wait_ge(dve_done, s.n)
            post_norm("m0", lambda k: v("norm_g", 3 * 8 + k))
            if upto < 5:
                return
            xattn("x0", 0)
            ffn("f1", 0, 6, 1)
            ffn("f2", 1, 0, 2)
            plain_norm("m1", 10)
            s.base("m1_acc_free")
            dve.wait_ge(act_done, at("act", "ds_kvrms"))
            s.step(dve.reciprocal(RS[:, :, 0:T], RS[:, :, 0:T]).then_inc(dve_done, 1))
            dve.wait_ge(dve_done, s.n)
            for q in range(2):
                s.step(dve.scalar_tensor_tensor(out=CQ[:, q, :], in0=CQ[:, q, :], scalar=v("dsa_q", q), in1=RS[:, 0, 0:T],
                                                op0=ALU.mult, op1=ALU.mult).then_inc(dve_done, 1), "ds_cqn")
            s.step(dve.scalar_tensor_tensor(out=CKV, in0=CKV, scalar=v("dsa_kv"), in1=RS[:, 1, 0:T], op0=ALU.mult,
                                            op1=ALU.mult).then_inc(dve_done, 1), "ds_ckvn")
            for u in range(16):
                h, t = u // 2, u % 2
                L = (t + 1) * P
                dve.wait_ge(act_done, at("act", f"ds_rl{u}"))
                if h == 0:
                    ins = dve.tensor_scalar(SCO[:, t, 0:L], RL[:, u % 2, 0:L], WI[:, t, h:h + 1], None, ALU.mult)
                else:
                    dve.wait_ge(dve_done, s.n - 1)
                    ins = dve.scalar_tensor_tensor(out=SCO[:, t, 0:L], in0=RL[:, u % 2, 0:L], scalar=WI[:, t, h:h + 1],
                                                   in1=SCO[:, t, 0:L], op0=ALU.mult, op1=ALU.add)
                s.step(ins.then_inc(dve_done, 1), f"ds_sc{u}")
            dve.wait_ge(dve_done, s.n)
            mask = [c("causal")[:, 0:P], c("causal")[:, P:3 * P]]
            for t in range(2):
                L = (t + 1) * P
                s.step(dve.tensor_tensor(WK[:, t, 0:L], SCO[:, t, 0:L], mask[t], ALU.add).then_inc(dve_done, 1))
            for n in range(TOPK // 8):
                for t in range(2):
                    dve.wait_ge(dve_done, s.n - 1)
                    s.step(dve.max(TOP[:, t, :], WK[:, t, 0:(t + 1) * P]).then_inc(dve_done, 1))
                for t in range(2):
                    dve.wait_ge(dve_done, s.n - 1)
                    row = WK[:, t, 0:(t + 1) * P]
                    s.step(dve.match_replace(row, TOP[:, t, :], row, TAKEN).then_inc(dve_done, 1))
            dve.wait_ge(dve_done, s.n)
            for t in range(2):
                L = (t + 1) * P
                s.step(dve.tensor_scalar(BI[:, t, 0:L], WK[:, t, 0:L], TAKEN, NEG, ALU.not_equal, ALU.mult).then_inc(dve_done, 1))
                dve.wait_ge(dve_done, s.n)
                s.step(dve.tensor_tensor(BI[:, t, 0:L], BI[:, t, 0:L], mask[t], ALU.add).then_inc(dve_done, 1))
            dve.wait_ge(dve_done, s.n)
            attention("dsa", DSA_UNITS, 64 ** -0.5, lambda w: ps[:, 6 + w // 2 % 2, 0:T], lambda w: OL[:, w // 2, :],
                      bias=lambda u: BI[:, u % 2, 0:(u % 2 + 1) * P])
            dve.wait_ge(act_done, at("act", "sc_raw5"))
            s.step(dve.tensor_tensor(SU[:, :, 2:T + 2], SU[:, :, 2:T + 2], SHH, ALU.mult).then_inc(dve_done, 1))
            dve.wait_ge(dve_done, s.n)
            for m in range(4):
                y = Y[:, 4 + m, :]
                s.step(dve.tensor_scalar(y, SU[:, m, 0:T], v("sc_w", m), v("sc_b", m), ALU.mult, ALU.add).then_inc(dve_done, 1))
                for tap in (1, 2):
                    dve.wait_ge(dve_done, s.n)
                    s.step(dve.scalar_tensor_tensor(out=y, in0=SU[:, m, tap:tap + T], scalar=v("sc_w", 4 * tap + m), in1=y,
                                                    op0=ALU.mult, op1=ALU.add).then_inc(dve_done, 1))
                dve.wait_ge(dve_done, s.n)
                s.step(dve.tensor_tensor(y, y, GB[:, m, :], ALU.mult).then_inc(dve_done, 1), f"yd{m}")
            post_norm("m1", lambda k: v("norm_g", 11 * 8 + k))
            xattn("x1", 1)
            ffn("f3", 1, 6, 3)

        @block.gpsimd
        def _(pool):
            s = Steps("pool", pool, plan)
            s.step(pool.memset(U[:, :, :, :], 0.0).then_inc(pool_done, 1), "pad")
            pool.wait_ge(inputs_in[0], 16)
            if upto < 2:
                return
            for u in range(8):
                pool.wait_ge(pe_done, at("pe", f"kq_rot{u}"))
                for half in range(2):
                    cos = c("gqa_cos")[:, half * T:(half + 1) * T] if u < 4 else c("gqa_cos")[:, T:2 * T]
                    q = KQ[:, u, half * T:(half + 1) * T]
                    s.step(pool.tensor_tensor(q, q, cos, ALU.mult).then_inc(pool_done, 1))
                pool.wait_ge(dve_done, at("dve", f"kq_sin{u}"))
                pool.wait_ge(pool_done, s.n)
                s.step(pool.tensor_tensor(KQ[:, u, :], KQ[:, u, :], ROT[:, u % 2, :], ALU.add).then_inc(pool_done, 1), f"kq_cos{u}")
            if upto < 3:
                return

            def add_x(tag):
                for k in range(KT):
                    pool.wait_ge(dve_done, at("dve", f"{tag}_t{k}"))
                    s.step(pool.tensor_tensor(X[:, k, LAT], X[:, k, LAT], TMP[:, k, :], ALU.add).then_inc(pool_done, 1), f"{tag}_x{k}")

            add_x("f0")
            if upto < 4:
                return
            s.step(pool.memset(RAW[:, :, :, :], 0.0).then_inc(pool_done, 1), "raw_pad")
            s.step(pool.memset(RESET, 1.0).then_inc(pool_done, 1))
            pool.wait_ge(pool_done, s.n)
            s.step(pool.memset(RESET.rearrange("p (c t) -> p c t", t=RW_C)[:, :, 0:1], 0.0).then_inc(pool_done, 1), "reset")
            for u in range(4):
                pool.wait_ge(pe_done, at("pe", f"rt_rot{u}"))
                qk = RQK[:, u, :].rearrange("p (m t) -> p m t", m=2)
                s.step(pool.tensor_tensor(qk, qk, c("rt_cos").unsqueeze(1).to_broadcast([P, 2, T]), ALU.mult).then_inc(pool_done, 1))
                pool.wait_ge(dve_done, at("dve", f"rt_sin{u}"))
                pool.wait_ge(pool_done, s.n)
                s.step(pool.tensor_tensor(RQK[:, u, :], RQK[:, u, :], RROT[:, u % 2, :], ALU.add).then_inc(pool_done, 1), f"rt_cos{u}")
            for t in range(2):
                for n in range(RW_LEVELS):
                    for q in range(2):
                        pool.wait_ge(dve_done, at("dve", f"rw_ma{t * 8 + 4 * q + 3}"))
                        if n:
                            pool.wait_ge(pe_done, at("pe", f"rw_x{t}_{n - 1}_{q}"))
                            pool.wait_ge(dve_done, at("dve", f"rw_t{t}_0_{q}"))
                        elif t:
                            pool.wait_ge(pe_done, at("pe", f"rw_x0_{RW_LEVELS - 1}_{q}"))
                        level = c("rw_level")[:, n * P:(n + 1) * P].unsqueeze(1).to_broadcast([P, 4, P])
                        s.step(pool.tensor_tensor(AL[:, 4 * q:4 * q + 4, :], MA[:, 4 * q:4 * q + 4, 0, :], level, ALU.mult).then_inc(pool_done, 1),
                               f"rw_al{t}_{n}_{q}")
            add_x("m0")
            if upto < 5:
                return
            add_x("x0")
            add_x("f1")
            s.step(pool.memset(SU[:, :, 0:2], 0.0).then_inc(pool_done, 1), "su_pad")
            add_x("f2")
            add_x("m1")
            add_x("x1")
            add_x("f3")


INPUTS = ("c", "c_ctx", "x", "ctx", "mem_2")


def prepare(inputs):
    a = {k: np.asarray(x) for k, x in inputs.items()}
    return {
        "const": constant_arrays(),
        "vec": vector_columns(a),
        "xs": np.ascontiguousarray(np.concatenate([feature_major(a["ctx"]), feature_major(a["x"])], 2)),
        "mem": feature_major(a["mem_2"]),
        "weights": weight_stream(a),
    }


def make(bacc, arrays, upto=99):
    plan = {}
    for _ in range(2):
        nc = bacc.Bacc("TRN2", target_bir_lowering=False, num_devices=1)
        ins = [nc.dram_tensor(n, arrays[n].shape, F32, kind="ExternalInput").ap() for n in arrays]
        out = nc.dram_tensor("y", (P, KT, T), F32, kind="ExternalOutput").ap()
        build(nc, *ins, out, plan, upto)
    return nc, plan


def kernel(**inputs):
    import concourse.bacc as bacc
    from concourse.bass_utils import run_bass_kernel_spmd as run

    arrays = prepare(inputs)
    nc, _ = make(bacc, arrays)
    y = run(nc, [arrays], core_ids=[0]).results[0]["y"]
    return np.ascontiguousarray(y.transpose(2, 1, 0)).reshape(1, T, D)
```

```python
from contextlib import ExitStack, contextmanager

import numpy as np

import concourse.bass as bass
from concourse import mybir

F32 = mybir.dt.float32
F32R = mybir.dt.float32r
ACT = mybir.ActivationFunctionType
ALU = mybir.AluOpType
AX = mybir.AxisListType.X

P = 128
T = 256
D = 1024
KT = D // P
RING = 4
HALVES = 3
TURN = 12
FF1_TILES = 4096 // P
FF2_TILES = 2816 // P
M0_PANELS = 30
M1_PANELS = 17
TAPS = 31
PAD = TAPS // 2
CHUNK = 512
CHUNK_TILES = CHUNK // P
CHUNK_PANELS = KT // 2
FIRST_CHUNKS = 4
MOD_CHUNKS = 24
SEG = T + 2 * PAD
RW_C = 64
RW_LEVELS = 6
TOPK = 64
NEG = -1.0e30
TAKEN = -3.0e38
EPS = 1e-6

VECTORS = (
    [("c", 16), ("b_mod", 96), ("norm1", 16), ("norm2", 16), ("dw", TAPS * KT), ("dw_b", KT), ("ln_g", KT),
     ("ln_b", KT), ("gqa_q", 1), ("gqa_k", 1), ("norm_g", 128), ("mem_g", KT), ("rw_mu", 14), ("w0", 4), ("a0", 4),
     ("k_k", 4), ("k_a", 4), ("r_k", 4), ("rw_g", 4), ("rw_b", 4), ("rt_g", 4), ("rt_b", 4), ("dsa_q", 2),
     ("dsa_kv", 1), ("sc_w", 12), ("sc_b", 4)])
CONSTS = [("ident", 128), ("ones", 128), ("blk", 128), ("gqa_rot", 128), ("rt_rot", 128), ("gqa_cos", 512),
          ("gqa_sin", 512), ("rt_cos", 256), ("rt_sin", 256), ("rt_decay", 1024), ("rw_mask", 512),
          ("rw_level", 128 * RW_LEVELS), ("causal", 384), ("eps", 4)]


def columns(table):
    at, n = {}, 0
    for name, width in table:
        at[name] = (n, width)
        n += width
    return at, n


VEC_AT, VEC_N = columns(VECTORS)
CON_AT, CON_N = columns(CONSTS)


def constant_arrays():
    f = np.float32
    p = np.arange(P)
    c = {"ident": np.eye(P, dtype=f), "ones": np.ones((P, P), f)}
    c["blk"] = (p[:, None] // 64 == p[None, :] // 64).astype(f)

    def rotation(half):
        m = np.zeros((P, P), f)
        for i in range(P):
            first = i % (2 * half) < half
            m[i + half if first else i - half, i] = -1.0 if first else 1.0
        return m

    c["gqa_rot"], c["rt_rot"] = rotation(16), rotation(64)
    pos = np.arange(T)
    inv = (f(10000.0) ** (-np.arange(16, dtype=f) / f(16))).astype(f)
    ang = np.zeros((64, T), f)
    for i in range(64):
        where = (pos // 64 if i < 32 else pos % 64).astype(f)
        ang[i] = where * inv[i % 16]
    ang = np.concatenate([ang, ang])
    c["gqa_cos"] = np.concatenate([np.ones((P, T), f), np.cos(ang)], 1)
    c["gqa_sin"] = np.concatenate([np.zeros((P, T), f), np.sin(ang)], 1)
    inv = (f(10000.0) ** (-np.arange(64, dtype=f) / f(64))).astype(f)
    ang = (pos.astype(f)[None, :] * inv[:, None]).astype(f)
    ang = np.concatenate([ang, ang])
    c["rt_cos"], c["rt_sin"] = np.cos(ang), np.sin(ang)
    rel = pos[None, :] - p[:, None]
    gammas = [np.log1p(-(2.0 ** (-5.0 - h))) for h in range(4)]
    c["rt_decay"] = np.concatenate(
        [np.where(rel >= 0, np.exp(np.maximum(rel, 0) * g), 0.0) * 128 ** -0.5 for g in gammas], 1)
    same = p[:, None] // RW_C == p[None, :] // RW_C
    strict = (same & (p[:, None] < p[None, :])).astype(f)
    upto = (same & (p[:, None] <= p[None, :])).astype(f)
    c["rw_mask"] = np.concatenate([strict, upto, strict, upto], 1)
    levels = []
    for n in range(RW_LEVELS):
        w = 1 << n
        levels.append((p[:, None] // (2 * w) == p[None, :] // (2 * w))
                      & (p[:, None] // w % 2 == 0) & (p[None, :] // w % 2 == 1))
    c["rw_level"] = np.concatenate(levels, 1)
    s = np.arange(T)
    c["causal"] = np.concatenate([np.where(s[None, :P] <= p[:, None], 0.0, NEG),
                                  np.where(s[None, :] <= P + p[:, None], 0.0, NEG)], 1)
    c["eps"] = np.tile(np.array([EPS, 64e-5, 0.0, 1.0]), (P, 1))
    return np.ascontiguousarray(np.concatenate([c[n].astype(f) for n, _ in CONSTS], 1))


def k_panels(w):
    n = w.shape[1] // P
    return w.reshape(KT, P, n, P).transpose(2, 1, 0, 3).reshape(n, P, D)


def column_panels(w):
    n = w.shape[1] // CHUNK
    return w.reshape(KT // 2, 2, P, n, CHUNK).transpose(3, 0, 2, 1, 4).reshape(-1, P, D)


def row_panels(w):
    return w.reshape(-1, P, D)


def weight_stream(a):
    out = []

    def add(*panels):
        out.extend(np.asarray(x).reshape(-1, P, D) for x in panels)

    mod = np.concatenate([column_panels(a["w_mod"][0]), column_panels(a["w_mod"][1])])
    add(mod[:FIRST_CHUNKS * CHUNK_PANELS])
    pw1 = k_panels(a["conv_w_pw1"][0])
    add(np.stack([pw1[:KT], pw1[KT:]], 1))
    add(mod[FIRST_CHUNKS * CHUNK_PANELS:])
    add(k_panels(a["conv_w_pw2"][0]))

    def mlp(layer):
        up, down = k_panels(a["w_ff1"][layer]), row_panels(a["w_ff2"][layer])
        add(up[0:1], np.stack([up[1:], down[:-1]], 1), down[-1:])

    mlp(0)
    mlp(0)
    qkv = a["gqa_w_qkv"][0]
    keys = qkv[:, 1024:1280].reshape(D, 4, 1, 64)
    add(k_panels(np.concatenate([keys, keys], 2).reshape(D, 512)))
    add(k_panels(qkv[:, 1280:1536]), k_panels(qkv[:, :1024]))
    add(k_panels(a["gqa_w_o"][0]))
    mlp(1)

    def ffn(layer, which):
        gate, up = (k_panels(a[n][layer, which]) for n in ("ffn_w_gate_2", "ffn_w_up_2"))
        down = row_panels(a["ffn_w_down_2"][layer, which])
        add(gate[0:1], up[0:1], np.stack([gate[1:], up[1:], down[:-1]], 1), down[-1:])

    def xattn(layer):
        add(k_panels(a["xa_wk_2"][layer]), k_panels(a["xa_wv_2"][layer]), k_panels(a["xa_wq_2"][layer]))
        add(row_panels(a["xa_wo_2"][layer]))

    ffn(0, 0)
    ev = k_panels(a["ev_w_in_2"][0])
    add(ev[14:], ev[:14])
    pair = np.concatenate([a["rw_w2_2"][0], a["rw_a2_2"][0]], 0)
    add(np.concatenate([pair, a["rw_g2_2"][0]], 1))
    add(k_panels(a["ev_w_out_2"][0]))
    xattn(0)
    ffn(0, 1)
    ffn(1, 0)
    od = a["od_w_in_2"][0]
    k_idx = od[:, 384:448]
    none = np.zeros((D, 120), np.float32)
    add(k_panels(np.concatenate([od[:, :384], k_idx, k_idx, od[:, 448:456], none, od[:, 456:]], 1)))
    q_rows = lambda w: w[0].reshape(2, P, 512).transpose(1, 0, 2).reshape(P, D)
    uk = a["dsa_w_uk_2"][0].reshape(4, P, P).transpose(1, 0, 2).reshape(P, 512)
    uv = a["dsa_w_uv_2"][0].transpose(1, 0, 2).reshape(P, 512)
    add(q_rows(a["dsa_w_uq_2"]), q_rows(a["dsa_w_qi_2"]), np.concatenate([uk, uv], 1))
    add(k_panels(a["od_w_out_2"][0]))
    xattn(1)
    ffn(1, 1)
    return np.concatenate(out)


def cols(v):
    return np.asarray(v, np.float32).reshape(-1, P).T


def vector_columns(a):
    two = lambda v: np.concatenate([v[0], v[0]])
    v = {
        "c": np.stack([cols(a["c_ctx"]), cols(a["c"])], 2).reshape(P, 16),
        "b_mod": cols(a["b_mod"]), "norm1": cols(a["norm1_g"]), "norm2": cols(a["norm2_g"]),
        "dw": cols(a["conv_w_dw"]), "dw_b": cols(a["conv_b_dw"]), "ln_g": cols(a["conv_ln_g"]),
        "ln_b": cols(a["conv_ln_b"]), "gqa_q": cols(two(a["gqa_q_norm"])), "gqa_k": cols(two(a["gqa_k_norm"])),
        "norm_g": cols(a["norm_g_2"]), "mem_g": cols(a["mem_norm_g_2"]), "rw_mu": cols(a["rw_mu_2"]),
        "w0": cols(a["rw_w0_2"]), "a0": cols(a["rw_a0_2"]), "k_k": cols(a["rw_k_k_2"]), "k_a": cols(a["rw_k_a_2"]),
        "r_k": cols(a["rw_r_k_2"]), "rw_g": cols(a["rw_ln_g_2"]), "rw_b": cols(a["rw_ln_b_2"]),
        "rt_g": cols(a["rt_gn_g_2"]), "rt_b": cols(a["rt_gn_b_2"]), "dsa_q": cols(a["dsa_q_norm_g_2"]),
        "dsa_kv": cols(a["dsa_kv_norm_g_2"]), "sc_w": cols(a["sc_conv_w_2"]), "sc_b": cols(a["sc_conv_b_2"]),
    }
    return np.ascontiguousarray(np.concatenate([v[n] for n, _ in VECTORS], 1))


def feature_major(x):
    return np.ascontiguousarray(np.asarray(x).reshape(T, KT, P).transpose(2, 1, 0))


class Steps:

    def __init__(self, key, eng, plan):
        self.key, self.eng, self.plan, self.n = key, eng, plan, 0

    def step(self, ins, name=None):
        self.n += 1
        if name is not None:
            self.plan[self.key, name] = self.n

    def base(self, name):
        self.plan[self.key, name] = self.n

    @contextmanager
    def loop(self, turns):
        start = self.n
        with self.eng.Fori(0, turns) as i:
            yield i
        self.n = start + (self.n - start) * turns


def build(nc, const, vec, xs, mem, weights, out, plan):
    with ExitStack() as ctx:
        def sb(name, *shape, dt=F32):
            return ctx.enter_context(nc.sbuf_tensor(name, [P, *shape], dt))

        def sem(name):
            return ctx.enter_context(nc.semaphore(name))

        ring = sb("ring", RING, D)
        WS = sb("WS", HALVES, 2, D, dt=F32R)
        HS2 = sb("HS2", 2, KT, T, dt=F32R)
        HTS = sb("HTS", 2, 2, T, dt=F32R)
        con = sb("con", CON_N)
        vecs = sb("vecs", VEC_N)
        X = sb("X", KT, 2 * T)
        H = sb("H", KT, 2 * T)
        RS = sb("RS", 2, 2 * T)
        MOD = sb("MOD", 96, 2)
        GS = sb("GS", 4, KT, 2)
        SC = sb("SC", 16)
        small = sb("small", 64)
        with ExitStack() as convolution:
            convolution.enter_context(nc.sbuf_tensor("below", [P, 11264], F32))
            CH = convolution.enter_context(nc.sbuf_tensor("CH", [P, 2, KT, 2 * T], F32R))
        arena = sb("arena", 22528)
        ps = ctx.enter_context(nc.psum_tensor("ps", [P, 8, 512], F32))

        full = [sem(f"panel_full{s}") for s in range(RING)]
        panels_done = sem("panels_done")
        uppers_ready = sem("uppers_ready")
        splits_used = sem("splits_used")
        pe_done, act_done, dve_done, pool_done = (sem(f"{k}_done") for k in ("pe", "act", "dve", "pool"))
        sems = {"pe": pe_done, "act": act_done, "dve": dve_done, "pool": pool_done, "panel": panels_done,
                "split": splits_used}

        def at(key, name):
            return plan.get((key, name), 1)

        def after(key, name):
            return sems[key], at(key, name)

        inputs_in = [sem(f"{n}_in") for n in ("con", "vec", "x", "mem")]
        out_stored = sem("out_stored")

        def c(name):
            start, width = CON_AT[name]
            return con[:, start:start + width]

        def v(name, i=0, n=1):
            start, _ = VEC_AT[name]
            return vecs[:, start + i:start + i + n]

        def area(at, *shape):
            n = int(np.prod(shape))
            assert at + n <= 22528, (at, shape)
            ap = arena[:, at:at + n]
            if len(shape) == 2:
                ap = ap.rearrange("p (a b) -> p a b", a=shape[0])
            if len(shape) == 3:
                ap = ap.rearrange("p (a b c) -> p a b c", a=shape[0], b=shape[1])
            return ap

        def looped(tiles, per):
            return (tiles - 3) // (TURN // per)

        def after_up(t, kinds):
            return kinds - 1 if t == 0 else (kinds + 1) * t + kinds - 2

        ident, ones, blk = c("ident"), c("ones"), c("blk")
        eps6, eps_rw = c("eps")[:, 0:1], c("eps")[:, 1:2]
        LAT = slice(T, 2 * T)
        ACC = lambda k: ps[:, 4 + k // 2, (k % 2) * T:(k % 2 + 1) * T]

        U = area(0, KT, 2, SEG)
        CV = area(4608, KT, 2 * T)
        SG = area(8704, 2, 2 * T)
        ROWS = area(9728, 3, CHUNK)
        HS = area(0, 2, T)
        HT = area(512, 2, T)
        KQ = area(0, 8, 2 * T)
        GV = area(4096, 4, 2 * P)
        GO = area(5120, KT, T)
        SQ = area(7168, 2, 2 * T)
        ROT = area(8192, 2, 2 * T)
        KQR = area(9216, 2, 2 * T)
        PR = area(10240, 3, 2 * T)
        PT = area(11776, 2, 2 * T)
        SBI = area(12800, 2, T)
        AS = area(13312, 64, 4)

        Y = area(0, KT, T)
        MEMN = X[:, :, 0:T]
        TMP = H[:, :, 0:T]
        HG = sb("HG", 4, KT)
        XK, XV, XQ, XO = area(0, 4, T), area(1024, 2, 512), area(2048, 4, T), area(3072, 4, T)
        RQK, RROT = area(2048, 4, 512), area(4096, 2, 512)
        RV, RG, RO, RP = area(5120, 2, 512), area(6144, 4, T), area(7168, 4, T), area(8192, 2, 512)
        GSQ, GRR = area(9216, 2, 512), area(10240, 2, 512)
        RAW, P2 = area(14848, 2, 2, 260), area(11264, 14, T)
        LW, LC, EP, EN, EX, RESET = (area(16384 + 1024 * n, 1024) for n in range(6))
        AA, KK, KP = (area(8192 + 1024 * n, 1024) for n in range(3))
        RWG, BON = H[:, 0:4, 0:T], H[:, 4:8, 0:T]
        AR = area(2048, 4, 2, T)
        BF, KF = area(4096, 4, T), area(5120, 4, T)
        BC, KC = area(6144, 4, T), area(7168, 4, T)
        AT, BT, KTM, VT = area(8192, 2, 512), area(9216, 2, 512), area(10240, 2, 512), area(14848, 2, 512)
        PC = small[:, 16:32].rearrange("p (m c) -> p m c", m=4)
        MR, MA = area(16384, 16, 2, P), area(20480, 8, 2, P)
        TI, TT = area(6144, 8, P), area(7168, 8, P)
        XB = lambda h: H[:, h // 2, T + (h % 2) * P:T + (h % 2 + 1) * P]
        AL, W1, TV, TAT = area(11264, 8, P), area(12288, 512), area(12800, 2, 512), area(13824, 4, T)
        SK, SKP = area(6144, 4, 4, 64), area(7168, 4, 64)
        UB, YR = area(4096, 2, 8, 64), area(5120, 4, T)
        WSQ, WRR = area(20480, 2, 512), area(21504, 2, 512)
        CQ, CKV, KI, WI = area(2048, 2, T), area(2560, T), area(2816, T), area(3072, 2, 8)
        SU, GB = area(3104, 4, 260), area(4160, 4, T)
        DQ, QI, QL, CKT = area(5184, 4, T), area(6208, 4, T), area(7232, 8, T), area(9280, 2, P)
        RL, SCO, WK, BI, OL = area(9536, 2, T), area(13568, 2, T), area(14080, 2, T), area(14592, 2, T), area(15104, 8, T)
        TOP = small[:, 32:48].rearrange("p (t e) -> p t e", t=2)
        SHH = area(17152, 4, T)
        SQD = area(18176, 3, T)

        lo_of = lambda h: 64 * (h % 2)
        GQA_UNITS = [(h, t, 4) for h in range(16) for t in range(2)]
        XA_UNITS = [(h, t, 2) for h in range(4) for t in range(2)]
        DSA_UNITS = [(h, t, t + 1) for h in range(8) for t in range(2)]

        block = ctx.enter_context(nc.Block())

        @block.sync
        def _(sp):
            total = plan.get(("panel", "total"), RING)
            for n in range(min(RING, total)):
                sp.dma_start(ring[:, n, :], weights[n]).then_inc(full[n], 16)
            turns = total // RING
            if turns > 1:
                with sp.Fori(1, turns) as i:
                    for s in range(RING):
                        sp.wait_ge(panels_done, RING * i + (s + 1 - RING))
                        sp.dma_start(ring[:, s, :], weights[RING * i + s]).then_inc(full[s], 16)
            for n in range(max(turns, 1) * RING, total):
                sp.wait_ge(panels_done, n + 1 - RING)
                sp.dma_start(ring[:, n % RING, :], weights[n]).then_inc(full[n % RING], 16)
            sp.wait_ge(panels_done, total)

        @block.tensor
        def _(pe):
            s = Steps("pe", pe, plan)
            panels = [0]

            def panel(i=None, back=0):
                n = panels[0]
                panels[0] += 1
                slot, value = n % RING, 16 * (n // RING + 1)
                pe.wait_ge(full[slot], value if i is None else 16 * (TURN // RING) * i + value)
                return ring[:, slot, :]

            def used(ins, name=None):
                ins.then_inc(panels_done, 1)
                if name is not None:
                    plan["panel", name] = panels[0]

            def turns(n):
                panels[0] += (n - 1) * TURN

            def feature_tile(dst, rhs, w, per_k=None, first=True, name=None):
                for k in range(KT):
                    if per_k:
                        pe.wait_ge(sems[per_k[0]], at(per_k[0], per_k[1] + f"{k}"))
                    ins = pe.matmul(dst, w[:, k * P:(k + 1) * P], rhs(k), start=(k == 0), stop=(k == KT - 1))
                used(ins, name)

            def column_sums(bank, src, tiles, name, what=ones, wait=None):
                for k in range(tiles):
                    if wait:
                        pe.wait_ge(sems[wait[0]], at(wait[0], wait[1] + f"{k}"))
                    ins = pe.matmul(bank, what, src(k), start=(k == 0), stop=(k == tiles - 1))
                s.step(ins.then_inc(pe_done, 1), name)

            splits = [0]

            def split_panel(i=None):
                slot = splits[0] % HALVES
                panels[0] += 1
                splits[0] += 1
                pe.wait_ge(panels_done, panels[0] if i is None else panels[0] + i * TURN)
                return WS[:, slot, 0, :], WS[:, slot, 1, :]

            def three_products(dst, w, cut, upper, lower, first, last):
                pe.matmul(dst, w[0][:, cut], upper, start=first, stop=False, skip_group_check=True)
                pe.matmul(dst, w[0][:, cut], lower, start=False, stop=False, skip_group_check=True)
                return pe.matmul(dst, w[1][:, cut], upper, start=False, stop=last, skip_group_check=True)

            def first_two(dsts, starts, tag, halves=lambda half, k: HS2[:, half, k, :]):
                ws = split_panel(), split_panel()
                for k in range(KT):
                    cut = slice(k * P, (k + 1) * P)
                    pe.wait_ge(act_done, at("act", f"{tag}_u{k}"))
                    for dst, w, start in zip(dsts, ws, starts):
                        pe.matmul(dst, w[0][:, cut], halves(0, k), start=(start and k == 0), stop=False, skip_group_check=True)
                        pe.matmul(dst, w[1][:, cut], halves(0, k), start=False, stop=False, skip_group_check=True)
                for k in range(KT):
                    pe.wait_ge(dve_done, at("dve", f"{tag}_l{k}"))
                    for dst, w in zip(dsts, ws):
                        ins = pe.matmul(dst, w[0][:, k * P:(k + 1) * P], halves(1, k), start=False, stop=(k == KT - 1),
                                        skip_group_check=True)
                        if k == KT - 1:
                            ins.then_inc(splits_used, 1)

            def split_section(tag):
                plan["panel", tag], plan["split", tag] = panels[0], splits[0]

            def split_tile(dst, name, first=True, halves=lambda half, k: HS2[:, half, k, :]):
                w = split_panel()
                for k in range(KT):
                    ins = three_products(dst, w, slice(k * P, (k + 1) * P), halves(0, k), halves(1, k),
                                         first and k == 0, k == KT - 1)
                ins.then_inc(splits_used, 1)
                plan["split", name] = splits[0]

            def hidden_loop(tag, tiles, kinds):
                plan["panel", tag], plan["split", tag] = panels[0], splits[0]
                d0 = at("dve", tag)
                per = kinds + 1
                body = TURN // per

                def up(t, i=None):
                    if i is not None or t >= 2:
                        value = d0 + 3 * (t - 2) + 1
                        pe.wait_ge(dve_done, value if i is None else value + i * 3 * body)
                    for q in range(kinds):
                        w = split_panel(i)
                        for k in range(KT):
                            ins = three_products(ps[:, t % 2, q * T:(q + 1) * T], w, slice(k * P, (k + 1) * P),
                                                 HS2[:, 0, k, :], HS2[:, 1, k, :], k == 0 and q == 0, k == KT - 1)
                        ins.then_inc(splits_used, 1)

                def down(t, i=None):
                    value = d0 + 3 * t + 3
                    pe.wait_ge(dve_done, value if i is None else value + i * 3 * body)
                    w = split_panel(i)
                    for k in range(KT):
                        ins = three_products(ACC(k), w, slice(k * P, (k + 1) * P), HTS[:, t % 2, 0, :],
                                             HTS[:, t % 2, 1, :], i is None and t == 0 and k % 2 == 0, t == tiles - 1)
                    ins.then_inc(splits_used, 1)

                n = looped(tiles, per)
                if kinds == 1:
                    first_two((ps[:, 0, 0:T], ps[:, 1, 0:T]), (True, True), tag)
                else:
                    first_two((ps[:, 0, 0:T], ps[:, 0, T:2 * T]), (True, False), tag)
                    up(1)
                plan["split", tag + ".up1"] = splits[0]
                pe.wait_ge(dve_done, at("dve", tag + ".acc_free"))
                down(0)
                with pe.Fori(0, n) as i:
                    for b in range(body):
                        up(2 + b, i)
                        down(1 + b, i)
                turns(n)
                splits[0] += (n - 1) * TURN
                for t in range(2 + n * body, tiles):
                    up(t)
                    plan["split", tag + ".last_up"] = splits[0]
                    down(t - 1)
                down(tiles - 1)
                plan["split", tag + ".last"] = splits[0]

            for q in range(2):
                pe.wait_ge(inputs_in[q], 16)

            def mod_rows(n, i=None):
                for q in range(CHUNK_PANELS):
                    w = panel(i)
                    for k in range(2):
                        c0 = 2 * (2 * q + k)
                        ins = pe.matmul(ps[0:2, 4 + n % 3, :], SC[:, c0:c0 + 2], w[:, k * CHUNK:(k + 1) * CHUNK],
                                        start=(q + k == 0), stop=(q == CHUNK_PANELS - 1 and k == 1))
                    used(ins, f"mod_rows{n}")

            def mod_turned(n, i=None):
                copied = at("act", f"mod_row{n}")
                pe.wait_ge(act_done, copied if i is None else copied + 3 * i)
                for m in range(CHUNK_TILES):
                    col = 2 * (CHUNK_TILES * n + m)
                    dst = ps[:, 7, col:col + 2] if i is None else ps[:, 7, bass.ds(2 * CHUNK_TILES * 3 * i + col, 2)]
                    ins = pe.matmul(dst, ROWS[0:2, n % 3, m * P:(m + 1) * P], ident[0:2, 0:2], start=True, stop=True)
                s.step(ins.then_inc(pe_done, 1), f"mod_turned{n}")

            def norm_sums(tag, t0, width):
                column_sums(ps[:, 2, 0:width], lambda k: H[:, k, t0:t0 + width], KT, tag + "sum",
                            wait=("act", tag + "sq"))

            pe.wait_ge(act_done, at("act", "silu_c"))
            mod_rows(0)
            for n in range(1, FIRST_CHUNKS):
                mod_rows(n)
                mod_turned(n - 1)
            mod_turned(FIRST_CHUNKS - 1)
            norm_sums("n0", 0, 2 * T)

            conv_halves = lambda half, k: CH[:, half, k, :]
            split_section("pw1")
            for j in range(KT):
                if j >= 2:
                    pe.wait_ge(dve_done, at("dve", f"glu{j - 2}"))
                else:
                    pe.wait_ge(act_done, at("act", "n0rms"))
                if j == 0:
                    first_two((ps[:, 0, :], ps[:, 1, :]), (True, True), "pw1", conv_halves)
                    plan["split", "pw1_0_1"] = splits[0]
                    continue
                for q in range(2):
                    split_tile(ps[:, 2 * (j % 2) + q, :], f"pw1_{j}_{q}", True, conv_halves)
            mod_turns = (MOD_CHUNKS - FIRST_CHUNKS) // 3
            with s.loop(mod_turns) as i:
                for n in range(FIRST_CHUNKS, FIRST_CHUNKS + 3):
                    mod_rows(n, i)
                    if n > FIRST_CHUNKS:
                        mod_turned(n - 1, i)
                mod_turned(FIRST_CHUNKS + 2, i)
            turns(mod_turns)
            for n in range(FIRST_CHUNKS + 3 * mod_turns, MOD_CHUNKS):
                mod_rows(n)
                mod_turned(n)
            column_sums(ps[:, 0, :], lambda k: CV[:, k, :], KT, "ln_mean", wait=("dve", "conv"))
            column_sums(ps[:, 2, :], lambda k: H[:, k, :], KT, "ln_var", wait=("act", "ln_sq"))
            split_section("pw2")
            first_two((ps[:, 0, :], ps[:, 1, :]), (True, True), "pw2", conv_halves)
            plan["split", "pw2_0"], plan["split", "pw2_1"] = splits[0], splits[0]
            for j in range(2, KT):
                pe.wait_ge(dve_done, at("dve", f"pw2_{j - 2}"))
                split_tile(ps[:, j % 2, :], f"pw2_{j}", True, conv_halves)
            norm_sums("n1", 0, 2 * T)
            hidden_loop("mlp0c", FF1_TILES, 1)
            hidden_loop("mlp0l", FF1_TILES, 1)

            norm_sums("n2", 0, 2 * T)
            def kq_rotated(u):
                if u < 8:
                    pe.wait_ge(act_done, at("act", f"kq_sq{u}"))
                    if u >= 2:
                        pe.wait_ge(act_done, at("act", f"kq_rms{u - 2}"))
                    else:
                        pe.wait_ge(act_done, at("act", "n2rms"))
                    s.step(pe.matmul(ps[:, 2 + u % 2, :], blk, SQ[:, u % 2, :], start=True, stop=True).then_inc(pe_done, 1), f"kq_sum{u}")
                if u >= 2:
                    w = u - 2
                    pe.wait_ge(dve_done, at("dve", f"kq_norm{w}"))
                    if w >= 2:
                        pe.wait_ge(dve_done, at("dve", f"kq_sin{w - 2}"))
                    s.step(pe.matmul(ps[:, 6 + w % 2, :], c("gqa_rot"), KQ[:, w, :], start=True, stop=True).then_inc(pe_done, 1), f"kq_rot{w}")

            for u in range(4):
                if u >= 2:
                    pe.wait_ge(act_done, at("act", f"kq_raw{u - 2}"))
                    kq_rotated(u - 2)
                feature_tile(ps[:, u % 2, :], lambda k: H[:, k, :], panel(), ("act", "n2h") if u == 0 else None,
                             name=f"kq{u}")
            for q in range(2):
                w = panel()
                for t in range(4):
                    for k in range(KT):
                        ins = pe.matmul(ps[:, 4 + q, t * P:(t + 1) * P], H[:, k, t * P:(t + 1) * P],
                                        w[:, k * P:(k + 1) * P], start=(k == 0 and t == 0), stop=(k == KT - 1),
                                        skip_group_check=True)
                used(ins, f"gv{q}")
                plan["panel", "gqa_w"] = panels[0]
                kq_rotated(q + 2)
            for u in range(4, 8):
                pe.wait_ge(act_done, at("act", f"kq_raw{u - 2}"))
                for q in range(2):
                    w = panel()
                    for k in range(KT):
                        ins = pe.matmul(ps[:, u % 2, q * T:(q + 1) * T], w[:, k * P:(k + 1) * P], H[:, k, LAT],
                                        start=(k == 0 and q == 0), stop=(k == KT - 1), skip_group_check=True)
                    used(ins, f"kq{u}")
                if u >= 5:
                    kq_rotated(u - 1)
            for u in range(7, 10):
                kq_rotated(u)

            def attention(tag, units, score, value, out_of):
                for u in range(len(units) + 3):
                    if u < len(units):
                        if u >= 4:
                            pe.wait_ge(*(after("dve", f"{tag}_bias{u - 4}") if tag == "dsa" else after("act", f"{tag}_exp{u - 4}")))
                        a, b = score(u)
                        s.step(pe.matmul(ps[:, u % 4, 0:units[u][2] * P], a, b, start=True, stop=True).then_inc(pe_done, 1), f"{tag}_s{u}")
                    w = u - 2
                    if 0 <= w < len(units):
                        pe.wait_ge(dve_done, at("dve", f"{tag}_p{w}"))
                        if w >= 2:
                            pe.wait_ge(act_done, at("act", f"{tag}_pt{w - 2}"))
                        nl = units[w][2]
                        for l in range(nl):
                            ins = pe.transpose(ps[:, 4 + w % 2, l * P:(l + 1) * P],
                                               PR[:, w % 3, l * P:(l + 1) * P], ident)
                        s.step(ins.then_inc(pe_done, 1), f"{tag}_t{w}")
                    w = u - 3
                    if w >= 0:
                        if w >= 4 and w % 2 == 0:
                            pe.wait_ge(dve_done, at("dve", f"{tag}_o{w - 3}"))
                        pe.wait_ge(act_done, at("act", f"{tag}_pt{w}"))
                        nl = units[w][2]
                        for l in range(nl):
                            ins = pe.matmul(out_of(w), value(w, l), PT[:, w % 2, l * P:(l + 1) * P],
                                            start=(l == 0), stop=(l == nl - 1), skip_group_check=True)
                        s.step(ins.then_inc(pe_done, 1), f"{tag}_pv{w}")

            def gqa_score(u):
                h, t, _ = GQA_UNITS[u]
                lo = 64 * (h % 2)
                q = KQ[lo:lo + 64, 4 + h // 4, (h // 2 % 2) * T + t * P:(h // 2 % 2) * T + t * P + P]
                return q, KQ[lo:lo + 64, h // 4, :]

            def gqa_value(u, l):
                h = GQA_UNITS[u][0]
                g = h // 4
                return GV[:, l, g * 64:(g + 1) * 64]

            def gqa_out(u):
                h, t, _ = GQA_UNITS[u]
                lo = 64 * (h % 2)
                return ps[lo:lo + 64, 6 + h % 2, t * P:(t + 1) * P]

            pe.wait_ge(pool_done, at("pool", "kq_cos7"))
            pe.wait_ge(act_done, at("act", "gv1"))
            attention("gqa", GQA_UNITS, gqa_score, gqa_value, gqa_out)
            for j in range(KT):
                if j >= 2:
                    pe.wait_ge(dve_done, at("dve", f"wo_{j - 2}"))
                else:
                    pe.wait_ge(dve_done, at("dve", "gqa_o31"))
                feature_tile(ps[:, j % 2, 0:T], lambda k: GO[:, k, :], panel(), name=f"wo_{j}")
            norm_sums("n3", T, T)
            hidden_loop("mlp1", FF1_TILES, 1)

            HL = lambda k: H[:, k, LAT]

            def row_products(tag, tiles, src, wait):
                for r in range(tiles):
                    w = panel()
                    pe.wait_ge(sems[wait[0]], at(wait[0], wait[1](r)))
                    for k in range(KT):
                        ins = pe.matmul(ACC(k), w[:, k * P:(k + 1) * P], src(r), start=(r == 0 and k % 2 == 0),
                                        stop=(r == tiles - 1), skip_group_check=True)
                    used(ins, f"{tag}_out{r}")

            def out_tiles(tag, wait):
                for j in range(KT):
                    w = panel()
                    for k in range(KT):
                        if j == 0:
                            pe.wait_ge(*after(*wait(k)))
                        ins = pe.matmul(ACC(j), w[:, k * P:(k + 1) * P], Y[:, k, :], start=(k == 0 and j % 2 == 0),
                                        stop=(k == KT - 1), skip_group_check=True)
                    used(ins, f"{tag}_out{j}")

            def sums_post(tag):
                column_sums(ps[:, 2, 0:T], HL, KT, tag + "sum", wait=("act", tag + "sq"))

            def pair(bank, name, first=None):
                if first:
                    first_two((ps[:, bank, 0:T], ps[:, bank, T:2 * T]), (True, False), first)
                    plan["split", name] = splits[0]
                    return
                for q in range(2):
                    split_tile(ps[:, bank, q * T:(q + 1) * T], name, q == 0)

            def split_token_major(bank, width, name):
                w = split_panel()
                for t in range(2):
                    dst = ps[:, bank, t * width:(t + 1) * width]
                    for k in range(KT):
                        x = [HS2[:, half, k, t * P:(t + 1) * P] for half in range(2)]
                        cut = slice(k * P, k * P + width)
                        pe.matmul(dst, x[0], w[0][:, cut], start=(k == 0 and t == 0), stop=False, skip_group_check=True)
                        pe.matmul(dst, x[1], w[0][:, cut], start=False, stop=False, skip_group_check=True)
                        ins = pe.matmul(dst, x[0], w[1][:, cut], start=False, stop=(k == KT - 1), skip_group_check=True)
                ins.then_inc(splits_used, 1)
                plan["split", name] = splits[0]

            def token_major(bank, src, name):
                w = panel()
                for t in range(2):
                    for k in range(KT):
                        ins = pe.matmul(ps[:, bank, t * P:(t + 1) * P], src(k, t), w[:, k * P:(k + 1) * P],
                                        start=(k == 0 and t == 0), stop=(k == KT - 1), skip_group_check=True)
                used(ins, name)

            def ffn(tag):
                sums_post(tag + "a")
                hidden_loop(tag, FF2_TILES, 2)
                sums_post(tag + "b")

            def xattn(tag):
                for h in range(4):
                    if h >= 2:
                        pe.wait_ge(act_done, at("act", f"{tag}_k{h - 2}"))
                    w = panel()
                    for k in range(KT):
                        ins = pe.matmul(ps[:, h % 2, 0:T], w[:, k * P:(k + 1) * P], MEMN[:, k, :], start=(k == 0),
                                        stop=(k == KT - 1))
                    used(ins, f"{tag}_k{h}")
                for q in range(4):
                    pe.wait_ge(act_done, at("act", f"{tag}_k{q + 2}" if q < 2 else f"{tag}_v{q - 2}"))
                    token_major(q % 2, lambda k, t: MEMN[:, k, t * P:(t + 1) * P], f"{tag}_v{q}")
                sums_post(tag + "a")
                for h in range(4):
                    pe.wait_ge(act_done, at("act", f"{tag}_v{h + 2}" if h < 2 else f"{tag}_q{h - 2}"))
                    feature_tile(ps[:, h % 2, 0:T], HL, panel(), ("dve", tag + "ah") if h == 0 else None, name=f"{tag}_q{h}")
                pe.wait_ge(act_done, at("act", f"{tag}_q3"))
                attention(tag, XA_UNITS,
                          lambda u: (XQ[:, u // 2, (u % 2) * P:(u % 2 + 1) * P], XK[:, u // 2, :]),
                          lambda u, l: XV[:, l, (u // 2) * P:(u // 2 + 1) * P],
                          lambda u: ps[:, 6 + u // 2 % 2, (u % 2) * P:(u % 2 + 1) * P])
                row_products(tag, 4, lambda r: XO[:, r, :], ("dve", lambda r: f"{tag}_o7"))
                sums_post(tag + "b")

            def group_norm(tag, buf, what, sq, ready):
                for q in range(2):
                    pe.wait_ge(*after(*ready(q)))
                    s.step(pe.matmul(ps[:, q, :], what, buf[:, 2 * q:2 * q + 2, :], start=True, stop=True).then_inc(pe_done, 1), f"{tag}_mean{q}")
                for q in range(2):
                    pe.wait_ge(act_done, at("act", f"{tag}_sq{q}"))
                    s.step(pe.matmul(ps[:, 2 + q, :], what, sq[:, q, :], start=True, stop=True).then_inc(pe_done, 1), f"{tag}_var{q}")

            column_sums(ps[:, 2, 0:T], lambda k: H[:, k, 0:T], KT, "memsum", wait=("act", "memsq"))
            ffn("f0")

            sums_post("m0a")
            split_section("m0")
            for u in range(4):
                if u >= 2:
                    pe.wait_ge(act_done, at("act", f"rt_raw{u - 2}"))
                pair(u % 2, f"rt_qk{u}", "m0" if u == 0 else None)
            for q in range(4):
                if q >= 2:
                    pe.wait_ge(act_done, at("act", f"rt_v{q - 2}"))
                else:
                    pe.wait_ge(dve_done, at("dve", "m0_acc_free"))
                split_token_major(4 + q % 2, P, f"rt_v{q}")
            for u in range(2):
                pe.wait_ge(act_done, at("act", f"rt_raw{u + 2}"))
                pair(u % 2, f"rt_g{u}")
            for u in range(7):
                pe.wait_ge(act_done, at("act", f"rt_g{u}" if u < 2 else f"rw_raw{u - 2}"))
                pair(u % 2, f"rw_p{u}")
            for u in range(4):
                if u < 2:
                    pe.wait_ge(act_done, at("act", "m0arms"))
                else:
                    pe.wait_ge(dve_done, at("dve", f"rt_sin{u - 2}"))
                s.step(pe.matmul(ps[:, 2 + u % 2, :], c("rt_rot"), RQK[:, u, :], start=True, stop=True).then_inc(pe_done, 1), f"rt_rot{u}")
            for h in range(4):
                q, k = RQK[:, h // 2, (h % 2) * T:(h % 2 + 1) * T], RQK[:, 2 + h // 2, (h % 2) * T:(h % 2 + 1) * T]
                if h == 0:
                    pe.wait_ge(pool_done, at("pool", "rt_cos3"))
                    pe.wait_ge(act_done, at("act", "rt_v3"))
                elif h >= 2:
                    pe.wait_ge(dve_done, at("dve", f"rt_p{h - 2}"))
                pe.matmul(ps[:, 4 + h % 2, 0:T], k[:, 0:P], q, start=True, stop=True, skip_group_check=True)
                s.step(pe.matmul(ps[:, 4 + h % 2, T:T + P], k[:, P:T], q[:, P:T], start=False, stop=True,
                                 skip_group_check=True).then_inc(pe_done, 1), f"rt_s{h}")
            for h in range(4):
                pe.wait_ge(dve_done, at("dve", f"rt_p{h}"))
                if h >= 2:
                    pe.wait_ge(act_done, at("act", f"rt_o{h - 2}"))
                pe.matmul(ps[:, 6 + h % 2, 0:T], RV[:, 0, h * P:(h + 1) * P], RP[:, h % 2, 0:T], start=True, stop=False,
                          skip_group_check=True)
                s.step(pe.matmul(ps[:, 6 + h % 2, P:T], RV[:, 1, h * P:(h + 1) * P], RP[:, h % 2, T:T + P], start=False,
                                 stop=True, skip_group_check=True).then_inc(pe_done, 1), f"rt_pv{h}")
            pe.wait_ge(act_done, at("act", "rw_raw6"))
            pe.wait_ge(dve_done, at("dve", "rt_sin3"))
            group_norm("rt", RO, ones, GSQ, lambda q: ("act", f"rt_o{2 * q + 1}"))

            w = panel()
            pe.wait_ge(act_done, at("act", "rw_tanh"))
            pe.wait_ge(dve_done, at("dve", "rt_gn"))
            for m in range(4):
                for rows, bank, out_cols in ((slice(0, 64), 0, m), (slice(64, P), 2, m)):
                    pe.matmul(ps[:, bank + m // 2, (m % 2) * T:(m % 2 + 1) * T], w[rows, m * P:(m + 1) * P],
                              P2[rows, 12, :], start=(m % 2 == 0), stop=True, skip_group_check=True)
            for m in range(4):
                ins = pe.matmul(ps[:, 4 + m // 2, (m % 2) * T:(m % 2 + 1) * T], w[:, 512 + m * P:512 + (m + 1) * P],
                                P2[:, 13, :], start=(m % 2 == 0), stop=True, skip_group_check=True)
            used(ins, "rw_low")
            for q in range(2):
                pe.wait_ge(dve_done, at("dve", "rw_kk2"))
                s.step(pe.matmul(ps[:, 6 + q, :], blk, EX[:, q * 512:(q + 1) * 512], start=True, stop=True).then_inc(pe_done, 1), f"rw_kksum{q}")
            for q in range(2):
                pe.wait_ge(act_done, at("act", "rw_g"))
                pe.wait_ge(dve_done, at("dve", "rw_rk"))
                s.step(pe.matmul(ps[:, 4 + q, :], blk, LW[:, q * 512:(q + 1) * 512], start=True, stop=True).then_inc(pe_done, 1), f"rw_bon{q}")
            n = 0
            for name, src, ready in (("v", P2[:, 8:12, :], "rw_p2"), ("a", AR[:, :, 0, :], "rw_ahat"),
                                     ("b", BC, "rw_bc"), ("k", KC, "rw_kc")):
                pe.wait_ge(dve_done, at("dve", ready))
                for t in range(2):
                    if n == 0:
                        pe.wait_ge(act_done, at("act", "rw_sig"))
                    if n >= 2:
                        pe.wait_ge(act_done, at("act", f"rw_tm{n - 2}"))
                    for m in range(4):
                        ins = pe.transpose(ps[:, n % 2, m * P:(m + 1) * P], src[:, m, t * P:(t + 1) * P], ident)
                    s.step(ins.then_inc(pe_done, 1), f"rw_tm{n}")
                    n += 1
            pe.wait_ge(act_done, at("act", "rw_tm7"))
            pe.wait_ge(dve_done, at("dve", "rw_bonus"))
            pe.wait_ge(dve_done, at("dve", "rw_kkn"))
            for t in range(2):
                for h in range(8):
                    u, m, lo = t * 8 + h, h // 2, lo_of(h)
                    bank = 4 + h % 4
                    if u >= 4:
                        pe.wait_ge(dve_done, at("dve", f"rw_mm{u - 4}"))
                    ar = AR[lo:lo + 64, m, :, t * P:(t + 1) * P]
                    pe.matmul(ps[:, bank, 0:T].rearrange("p (x t) -> p x t", x=2), BF[lo:lo + 64, m, t * P:(t + 1) * P], ar,
                              start=True, stop=True, skip_group_check=True)
                    s.step(pe.matmul(ps[:, bank, T:2 * T].rearrange("p (x t) -> p x t", x=2),
                                     KF[lo:lo + 64, m, t * P:(t + 1) * P], ar, start=False, stop=True,
                                     skip_group_check=True).then_inc(pe_done, 1), f"rw_mm{u}")
                for n in range(RW_LEVELS):
                    for q in range(2):
                        pe.wait_ge(pool_done, at("pool", f"rw_al{t}_{n}_{q}"))
                        if n:
                            pe.wait_ge(dve_done, at("dve", f"rw_t{t}_{n - 1}_{q}"))
                        elif q == 0:
                            pe.wait_ge(dve_done, at("dve", f"rw_mm{t * 8 + 7}"))
                        for h in range(4 * q, 4 * q + 4):
                            ins = pe.matmul(ps[:, 3 * q, (h % 4) * P:(h % 4 + 1) * P], AL[:, h, :],
                                            TI[:, h, :] if n else ident, start=True, stop=True, skip_group_check=True)
                        s.step(ins.then_inc(pe_done, 1), f"rw_x{t}_{n}_{q}")
                    if n == 0:
                        continue
                    for q in range(2):
                        pe.wait_ge(act_done, at("act", f"rw_x{t}_{n}_{q}"))
                        if n < RW_LEVELS - 1:
                            for h in range(4 * q, 4 * q + 4):
                                ins = pe.matmul(ps[:, 3 * q + 1, (h % 4) * P:(h % 4 + 1) * P], TT[:, h, :], XB(h),
                                                start=True, stop=True, skip_group_check=True)
                            s.step(ins.then_inc(pe_done, 1), f"rw_dt{t}_{n}_{q}")
                        for h in range(4 * q, 4 * q + 4):
                            ins = pe.matmul(ps[:, 3 * q + 2, (h % 4) * P:(h % 4 + 1) * P], XB(h), TT[:, h, :],
                                            start=True, stop=True, skip_group_check=True)
                        s.step(ins.then_inc(pe_done, 1), f"rw_dtt{t}_{n}_{q}")
                for h in range(8):
                    ins = pe.matmul(ps[:, 6, h * 64:(h + 1) * 64], MA[:, h, 1, :], VT[:, t, h * 64:(h + 1) * 64],
                                    start=True, stop=True, skip_group_check=True)
                s.step(ins.then_inc(pe_done, 1), f"rw_w1_{t}")
                pe.wait_ge(act_done, at("act", f"rw_w1_{t}"))
                pe.wait_ge(dve_done, at("dve", f"rw_t{t}_{RW_LEVELS - 1}_1"))
                for h in range(8):
                    ins = pe.matmul(ps[:, 7, h * 64:(h + 1) * 64], TT[:, h, :], W1[:, h * 64:(h + 1) * 64],
                                    start=True, stop=True, skip_group_check=True)
                s.step(ins.then_inc(pe_done, 1), f"rw_tv{t}")
                for h in range(8):
                    lo = lo_of(h)
                    ins = pe.matmul(ps[lo:lo + 64, 1, (h // 2) * P:(h // 2 + 1) * P], AT[:, t, h * 64:(h + 1) * 64],
                                    TT[:, h, :], start=True, stop=True, skip_group_check=True)
                s.step(ins.then_inc(pe_done, 1), f"rw_ta{t}")
                pe.wait_ge(act_done, at("act", f"rw_tv{t}"))
            for ch in range(4):
                t, lo = ch // 2, 64 * (ch % 2)
                if ch:
                    pe.wait_ge(act_done, at("act", "rw_ta1"))
                    pe.wait_ge(dve_done, at("dve", f"rw_s{ch}"))
                    for h in range(8):
                        kl = lo_of(h)
                        ins = pe.matmul(ps[lo:lo + 64, 2 + h % 2, (h // 2) * 64:(h // 2 + 1) * 64],
                                        TAT[kl:kl + 64, h // 2, ch * 64:(ch + 1) * 64], SK[kl:kl + 64, ch, h // 2, :],
                                        start=True, stop=True, skip_group_check=True)
                    s.step(ins.then_inc(pe_done, 1), f"rw_u{ch}")
                pe.wait_ge(dve_done, at("dve", f"rw_u{ch}"))
                if ch < 3:
                    for h in range(8):
                        kl = lo_of(h)
                        dst = ps[kl:kl + 64, 4 + ch % 2, (h // 2) * 64:(h // 2 + 1) * 64]
                        pe.matmul(dst, BT[lo:lo + 64, t, h * 64:(h + 1) * 64], UB[lo:lo + 64, t, h, :], start=True,
                                  stop=False, skip_group_check=True)
                        ins = pe.matmul(dst, KTM[lo:lo + 64, t, h * 64:(h + 1) * 64], VT[lo:lo + 64, t, h * 64:(h + 1) * 64],
                                        start=False, stop=True, skip_group_check=True)
                    s.step(ins.then_inc(pe_done, 1), f"rw_s{ch + 1}")
                if ch % 2 == 0:
                    continue
                if t:
                    pe.wait_ge(dve_done, at("dve", "rw_y0"))
                for h in range(8):
                    u, m, kl = t * 8 + h, h // 2, lo_of(h)
                    bank = 6 + h % 2
                    dst = lambda a, b: ps[kl:kl + 64, bank, m * P + a:m * P + b]
                    pe.matmul(dst(0, P), VT[:, t, h * 64:(h + 1) * 64], MR[:, u, 1, :], start=True, stop=False,
                              skip_group_check=True)
                    ins = pe.matmul(dst(0, P), UB[:, t, h, :], MR[:, u, 0, :], start=False, stop=(t == 0),
                                    skip_group_check=True)
                    for cc in (2 * t, 2 * t + 1):
                        if cc:
                            a = 64 * (cc % 2)
                            ins = pe.matmul(dst(a, a + 64), SK[kl:kl + 64, cc, m, :],
                                            AR[kl:kl + 64, m, 1, cc * 64:(cc + 1) * 64], start=False, stop=True,
                                            skip_group_check=True)
                s.step(ins.then_inc(pe_done, 1), f"rw_y{t}")
            pe.wait_ge(dve_done, at("dve", "rw_u3"))
            group_norm("rw", YR, blk, WSQ, lambda q: ("dve", "rw_y1"))
            out_tiles("m0", lambda k: ("dve", f"yb{k - 4}" if k >= 4 else f"ya{k}"))
            sums_post("m0b")
            xattn("x0")
            ffn("f1")
            ffn("f2")

            sums_post("m1a")
            split_section("m1")
            pair(0, "ds_cq", "m1")
            split_tile(ps[:, 1, 0:T], "ds_ckv")
            split_tile(ps[:, 1, T:2 * T], "ds_ki", False)
            pe.wait_ge(act_done, at("act", "m1arms"))
            split_token_major(3, 8, "ds_w")
            pe.wait_ge(dve_done, at("dve", "m1_acc_free"))
            for u in range(6):
                if u >= 2:
                    pe.wait_ge(act_done, at("act", f"sc_raw{u - 2}"))
                pair(4 + u % 2, f"sc_p{u}")
            for q in range(2):
                pe.wait_ge(act_done, at("act", f"ds_sq{q}"))
                ins = pe.matmul(ps[:, 2, 0:T], ones, SQD[:, q, :], start=(q == 0), stop=(q == 1), skip_group_check=True)
            s.step(ins.then_inc(pe_done, 1), "ds_cqsum")
            pe.wait_ge(act_done, at("act", "ds_sq2"))
            pe.wait_ge(act_done, at("act", "ds_w"))
            s.step(pe.matmul(ps[:, 3, 0:T], ones, SQD[:, 2, :], start=True, stop=True).then_inc(pe_done, 1), "ds_kvsum")
            for name, dst in (("ds_q", 0), ("ds_qi", 6)):
                w = panel()
                pe.wait_ge(dve_done, at("dve", "ds_cqn"))
                pe.wait_ge(act_done, at("act", "ds_ki"))
                for m in range(4):
                    for r in range(2):
                        ins = pe.matmul(ps[:, dst + m // 2, (m % 2) * T:(m % 2 + 1) * T],
                                        w[:, r * 512 + m * P:r * 512 + (m + 1) * P], CQ[:, r, :],
                                        start=(r == 0 and m % 2 == 0), stop=(r == 1), skip_group_check=True)
                used(ins, name)
            pe.wait_ge(dve_done, at("dve", "ds_ckvn"))
            pe.wait_ge(act_done, at("act", "sc_raw5"))
            for t in range(2):
                ins = pe.transpose(ps[:, 4, t * P:(t + 1) * P], CKV[:, t * P:(t + 1) * P], ident)
            s.step(ins.then_inc(pe_done, 1), "ds_ckt")
            pe.wait_ge(act_done, at("act", "ds_qi"))
            for u in range(16):
                h, t = u // 2, u % 2
                lo = lo_of(h)
                if u >= 4:
                    pe.wait_ge(act_done, at("act", f"ds_rl{u - 4}"))
                bank = 4 + (h % 2) * 2 + t
                if u == 0:
                    pe.wait_ge(act_done, at("act", "ds_ckt"))
                s.step(pe.matmul(ps[:, bank, 0:(t + 1) * P], QI[lo:lo + 64, h // 2, t * P:(t + 1) * P],
                                 KI[lo:lo + 64, 0:(t + 1) * P], start=True, stop=True).then_inc(pe_done, 1), f"ds_l{u}")
            uk = panel()
            pe.wait_ge(act_done, at("act", "ds_q"))
            for h in range(8):
                lo = lo_of(h)
                if h < 2:
                    pe.wait_ge(dve_done, at("dve", "ds_ckvn"))
                else:
                    pe.wait_ge(act_done, at("act", f"ds_ql{h - 2}"))
                s.step(pe.matmul(ps[:, 2 + h % 2, 0:T], uk[lo:lo + 64, (h // 2) * P:(h // 2 + 1) * P],
                                 DQ[lo:lo + 64, h // 2, :], start=True, stop=True).then_inc(pe_done, 1), f"ds_ql{h}")
            pe.wait_ge(act_done, at("act", "ds_ql7"))
            attention("dsa", DSA_UNITS,
                      lambda u: (QL[:, u // 2, (u % 2) * P:(u % 2 + 1) * P], CKV[:, 0:(u % 2 + 1) * P]),
                      lambda u, l: CKT[:, l, :],
                      lambda u: ps[:, 6 + u // 2 % 2, (u % 2) * P:(u % 2 + 1) * P])
            pe.wait_ge(dve_done, at("dve", "dsa_o15"))
            for h in range(8):
                lo = lo_of(h)
                ins = pe.matmul(ps[lo:lo + 64, h // 4, (h // 2 % 2) * T:(h // 2 % 2 + 1) * T],
                                uk[:, 512 + h * 64:512 + (h + 1) * 64], OL[:, h, :], start=True, stop=True,
                                skip_group_check=True)
            used(ins, "ds_uv")
            out_tiles("m1", lambda k: ("dve", f"yd{k - 4}") if k >= 4 else ("act", f"yc{k // 2}"))
            sums_post("m1b")
            xattn("x1")
            ffn("f3")
            plan["panel", "total"] = panels[0]

        @block.scalar
        def _(act):
            s = Steps("act", act, plan)
            act.dma_start(con[:, :], const).then_inc(inputs_in[0], 16)
            act.dma_start(vecs[:, :], vec).then_inc(inputs_in[1], 16)
            act.dma_start(X[:, :, :], xs).then_inc(inputs_in[2], 16)

            def squares(tag, src, dst, tiles, wait=None, before=None):
                act.activation(small[:, 1:2], eps6, ACT.Sqrt)
                for k in range(tiles):
                    if before:
                        before(k)
                    if wait:
                        act.wait_ge(sems[wait[0]], at(wait[0], wait[1].format(k)))
                    s.step(act.activation(dst(k), src(k), ACT.Square).then_inc(act_done, 1), f"{tag}sq{k}")

            def rms(tag, width, n, eps=eps6):
                act.wait_ge(pe_done, at("pe", tag + "sum"))
                s.step(act.activation(RS[:, 0, 0:width], ps[:, 2, 0:width], ACT.Sqrt, bias=eps, scale=1.0 / n).then_inc(act_done, 1),
                       tag + "rms")

            def mod_norm(tag, layer, which, segs, wait, last, shift=True, square=True, before=None):
                t0, t1 = min(segs) * T, (max(segs) + 1) * T
                if last:
                    act.wait_ge(*after(*last))
                if square:
                    squares(tag, lambda k: X[:, k, t0:t1], lambda k: H[:, k, t0:t1], KT, wait, before)
                rms(tag, t1 - t0, D)
                for k in range(KT if shift else 0):
                    for g in segs:
                        act.wait_ge(dve_done, at("dve", f"{tag}g{k}_{g}"))
                        m = layer * 48 + 24 * which + k
                        ins = act.activation(H[:, k, g * T:(g + 1) * T], H[:, k, g * T:(g + 1) * T], ACT.Identity,
                                             bias=MOD[:, m, g:g + 1])
                        s.step(ins.then_inc(act_done, 1), f"{tag}h{k}" if g == segs[-1] else None)

            def upper(tag, n, i=None):
                panel, split = at("panel", tag) + n, at("split", tag) + n
                value = 16 * (panel // RING + 1)
                act.wait_ge(full[panel % RING], value if i is None else value + i * 16 * (TURN // RING))
                if i is not None or split >= HALVES:
                    used = split - HALVES + 1
                    act.wait_ge(splits_used, used if i is None else used + i * TURN)
                act.copy(WS[:, split % HALVES, 0, :], ring[:, panel % RING, :]).then_inc(uppers_ready, 1)

            def uppers(tag, first, last):
                for n in range(first, last):
                    upper(tag, n)

            def first_uppers(tag):
                for n in range(HALVES):
                    upper(tag, n)

            def input_uppers(tag, src, wait, free, bias=None):
                if free:
                    act.wait_ge(splits_used, at("split", free))
                for k in range(KT):
                    act.wait_ge(dve_done, at("dve", wait.format(k)))
                    if bias:
                        ins = act.activation(HS2[:, 0, k, :], src(k), ACT.Identity, bias=bias(k))
                    else:
                        ins = act.copy(HS2[:, 0, k, :], src(k))
                    s.step(ins.then_inc(act_done, 1), f"{tag}_u{k}")

            def hidden_act(tag, tiles, kinds, func):
                s.base(tag)
                q0, d0 = at("split", tag), at("dve", tag)
                per = kinds + 1
                body = TURN // per

                def step_(t, i=None):
                    used = q0 + after_up(t, kinds) + 1
                    act.wait_ge(splits_used, used if i is None else used + i * TURN)
                    if i is not None or t >= 2:
                        read = d0 + 3 * (t - 2) + 1
                        act.wait_ge(dve_done, read if i is None else read + i * 3 * body)
                    s.step(act.activation(HS[:, t % 2, :], ps[:, t % 2, 0:T], func).then_inc(act_done, 1))
                    for n in range(after_up(t, kinds) + HALVES, after_up(t + 1, kinds) + HALVES):
                        if n < per * tiles:
                            upper(tag, n, i)

                for n in range(HALVES, after_up(0, kinds) + HALVES):
                    upper(tag, n)
                n = looped(tiles, per)
                step_(0)
                step_(1)
                with s.loop(n) as i:
                    for b in range(body):
                        step_(2 + b, i)
                for t in range(2 + n * body, tiles):
                    step_(t)

            def mod_rows(n, i=None):
                done = at("panel", f"mod_rows{n}")
                act.wait_ge(panels_done, done if i is None else done + TURN * i)
                s.step(act.copy(ROWS[0:2, n % 3, :], ps[0:2, 4 + n % 3, :]).then_inc(act_done, 1), f"mod_row{n}")

            act.wait_ge(inputs_in[1], 16)
            s.step(act.activation(SC[:, :], v("c", 0, 16), ACT.Silu).then_inc(act_done, 1), "silu_c")
            act.wait_ge(inputs_in[0], 16)
            act.wait_ge(inputs_in[2], 16)
            squares("n0", lambda k: X[:, k, :], lambda k: H[:, k, :], KT)
            for n in range(FIRST_CHUNKS):
                mod_rows(n)
            first_uppers("pw1")
            mod_norm("n0", 0, 0, (0, 1), None, None, shift=False, square=False)
            for k in range(KT):
                for g in range(2):
                    act.wait_ge(dve_done, at("dve", f"n0g{k}_{g}"))
                    s.step(act.activation(CH[:, 0, k, g * T:(g + 1) * T], H[:, k, g * T:(g + 1) * T], ACT.Identity,
                                          bias=MOD[:, k, g:g + 1]).then_inc(act_done, 1), f"pw1_u{k}_{g}")
                plan["act", f"pw1_u{k}"] = s.n
            for j in range(KT):
                uppers("pw1", 2 * j + 3, min(2 * j + 5, 2 * KT))
                act.wait_ge(splits_used, at("split", f"pw1_{j}_1"))
                if j >= 2:
                    act.wait_ge(dve_done, at("dve", f"glu{j - 2}"))
                s.step(act.activation(SG[:, j % 2, :], ps[:, 2 * (j % 2) + 1, :], ACT.Sigmoid).then_inc(act_done, 1), f"sig{j}")
            mod_turns = (MOD_CHUNKS - FIRST_CHUNKS) // 3
            with s.loop(mod_turns) as i:
                for n in range(FIRST_CHUNKS, FIRST_CHUNKS + 3):
                    mod_rows(n, i)
            for n in range(FIRST_CHUNKS + 3 * mod_turns, MOD_CHUNKS):
                mod_rows(n)
            squares("ln_", lambda k: CV[:, k, :], lambda k: H[:, k, :], KT, ("dve", "ln_c{}"))
            act.wait_ge(pe_done, at("pe", "ln_var"))
            s.step(act.activation(RS[:, 0, :], ps[:, 2, :], ACT.Sqrt, bias=eps6, scale=1.0 / D).then_inc(act_done, 1), "ln_rms")
            first_uppers("pw2")
            for k in range(KT):
                act.wait_ge(dve_done, at("dve", f"ln_n{k}"))
                s.step(act.activation(H[:, k, :], CV[:, k, :], ACT.Silu, bias=v("ln_b", k), scale=v("ln_g", k)).then_inc(act_done, 1),
                       f"ln_h{k}")
                act.wait_ge(act_done, s.n)
                s.step(act.copy(CH[:, 0, k, :], H[:, k, :]).then_inc(act_done, 1), f"pw2_u{k}")
            next_upper = lambda k: upper("pw2", k + HALVES) if k + HALVES < KT else upper("mlp0c", k + HALVES - KT)
            mod_norm("n1", 0, 1, (0, 1), ("dve", "pw2_{}"), None, shift=False, before=next_upper)
            mlp_shift = lambda layer, g: (lambda k: MOD[:, layer * 48 + 24 + k, g:g + 1])
            input_uppers("mlp0c", lambda k: H[:, k, 0:T], "n1g{}_0", None, mlp_shift(0, 0))
            hidden_act("mlp0c", FF1_TILES, 1, ACT.Relu)
            input_uppers("mlp0l", lambda k: H[:, k, LAT], "n1g{}_1", "mlp0c.last_up", mlp_shift(0, 1))
            first_uppers("mlp0l")
            hidden_act("mlp0l", FF1_TILES, 1, ACT.Relu)
            mod_norm("n2", 1, 0, (0, 1), ("dve", "mlp0l_x{}"), ("split", "mlp0l.last"))
            def kq_rms(u):
                act.wait_ge(pe_done, at("pe", f"kq_sum{u}"))
                if u >= 2:
                    act.wait_ge(dve_done, at("dve", f"kq_norm{u - 2}"))
                s.step(act.activation(KQR[:, u % 2, :], ps[:, 2 + u % 2, :], ACT.Sqrt, bias=eps6, scale=1.0 / 64).then_inc(act_done, 1),
                       f"kq_rms{u}")

            for u in range(8):
                act.wait_ge(panels_done, at("panel", f"kq{u}"))
                s.step(act.copy(KQ[:, u, :], ps[:, u % 2, :]).then_inc(act_done, 1), f"kq_raw{u}")
                if u >= 2:
                    act.wait_ge(pe_done, at("pe", f"kq_sum{u - 2}"))
                act.wait_ge(act_done, s.n)
                s.step(act.activation(SQ[:, u % 2, :], KQ[:, u, :], ACT.Square).then_inc(act_done, 1), f"kq_sq{u}")
                if u >= 2:
                    kq_rms(u - 2)
                if u == 3:
                    for q in range(2):
                        act.wait_ge(panels_done, at("panel", f"gv{q}"))
                        s.step(act.copy(GV[:, :, q * P:(q + 1) * P], ps[:, 4 + q, :].rearrange("p (t c) -> p t c", t=4)).then_inc(act_done, 1),
                               f"gv{q}")
            kq_rms(6)
            kq_rms(7)

            def attention(tag, units, scale):
                for u in range(len(units) + 1):
                    if u < len(units):
                        L = units[u][2] * P
                        act.wait_ge(dve_done, at("dve", f"{tag}_max{u}"))
                        if u >= 3:
                            act.wait_ge(pe_done, at("pe", f"{tag}_t{u - 3}"))
                        src = SBI[:, u % 2, 0:L] if tag == "dsa" else ps[:, u % 4, 0:L]
                        s.step(act.activation(PR[:, u % 3, 0:L], src, ACT.Exp, bias=AS[:, u % 64, 0:1], scale=scale,
                                              accum_out=AS[:, u % 64, 1:2]).then_inc(act_done, 1), f"{tag}_exp{u}")
                    if u >= 2:
                        pt(tag, units, u - 2)
                pt(tag, units, len(units) - 1)

            def pt(tag, units, w):
                L = units[w][2] * P
                act.wait_ge(pe_done, at("pe", f"{tag}_t{w}"))
                if w >= 2:
                    act.wait_ge(pe_done, at("pe", f"{tag}_pv{w - 2}"))
                s.step(act.copy(PT[:, w % 2, 0:L], ps[:, 4 + w % 2, 0:L]).then_inc(act_done, 1), f"{tag}_pt{w}")

            attention("gqa", GQA_UNITS, 64 ** -0.5)
            first_uppers("mlp1")
            mod_norm("n3", 1, 1, (1,), ("dve", "wo_{}"), ("panel", "wo_7"), shift=False)
            input_uppers("mlp1", lambda k: H[:, k, LAT], "n3g{}_1", None, mlp_shift(1, 1))
            hidden_act("mlp1", FF1_TILES, 1, ACT.Relu)

            HL = lambda k: H[:, k, LAT]
            XL = lambda k: X[:, k, LAT]

            def plain_norm(tag, wait, last):
                if last:
                    act.wait_ge(*after(*last))
                squares(tag + "a", XL, HL, KT, wait)
                rms(tag + "a", T, D)

            def post_norm(tag, *last):
                act.wait_ge(*after(*last))
                squares(tag + "b", ACC, HL, KT)
                rms(tag + "b", T, D)

            def evacuate(name, key, dst, src, func=ACT.Copy, **kw):
                act.wait_ge(sems[key], at(key, name))
                s.step(act.activation(dst, src, func, **kw).then_inc(act_done, 1), name)

            def ffn(tag, wait, last):
                first_uppers(tag)
                plain_norm(tag, wait, last)
                input_uppers(tag, HL, tag + "ah{}", None)
                hidden_act(tag, FF2_TILES, 2, ACT.Silu)
                post_norm(tag, "split", tag + ".last")

            def xattn(tag, wait, last_panel):
                for h in range(4):
                    evacuate(f"{tag}_k{h}", "panel", XK[:, h, :], ps[:, h % 2, 0:T])
                for q in range(4):
                    evacuate(f"{tag}_v{q}", "panel", XV[:, :, q * P:(q + 1) * P],
                             ps[:, q % 2, 0:T].rearrange("p (t c) -> p t c", t=2))
                plain_norm(tag, wait, last_panel)
                for h in range(4):
                    evacuate(f"{tag}_q{h}", "panel", XQ[:, h, :], ps[:, h % 2, 0:T])
                attention(tag, XA_UNITS, P ** -0.5)
                post_norm(tag, "panel", f"{tag}_out3")

            def group_norm(tag, buf, sq, rr, n, eps):
                for q in range(2):
                    act.wait_ge(dve_done, at("dve", f"{tag}_cen{q}"))
                    s.step(act.activation(sq[:, q, :], buf[:, 2 * q:2 * q + 2, :], ACT.Square).then_inc(act_done, 1), f"{tag}_sq{q}")
                for q in range(2):
                    act.wait_ge(pe_done, at("pe", f"{tag}_var{q}"))
                    s.step(act.activation(rr[:, q, :], ps[:, 2 + q, :], ACT.Sqrt, bias=eps, scale=1.0 / n).then_inc(act_done, 1), f"{tag}_rms{q}")

            act.wait_ge(dve_done, at("dve", "n2g7_1"))
            act.dma_start(MEMN, mem).then_inc(inputs_in[3], 16)
            act.wait_ge(inputs_in[3], 16)
            act.wait_ge(panels_done, at("panel", "gqa_w"))
            squares("mem", lambda k: MEMN[:, k, :], lambda k: H[:, k, 0:T], KT)
            rms("mem", T, D)
            act.wait_ge(dve_done, at("dve", "mem_n"))
            ffn("f0", ("dve", "mlp1_x{}"), ("split", "mlp1.last"))
            first_uppers("m0")
            plain_norm("m0", ("pool", "f0_x{}"), None)
            input_uppers("m0", HL, "m0ah{}", None)
            for u in range(4):
                uppers("m0", 2 * u + 3, 2 * u + 5)
                evacuate(f"rt_qk{u}", "split", RQK[:, u, :], ps[:, u % 2, :])
                plan["act", f"rt_raw{u}"] = s.n
            for q in range(4):
                uppers("m0", 11 + q, 12 + q)
                evacuate(f"rt_v{q}", "split", RV[:, :, q * P:(q + 1) * P],
                         ps[:, 4 + q % 2, 0:T].rearrange("p (t c) -> p t c", t=2))
            for u in range(2):
                uppers("m0", 15 + 2 * u, 17 + 2 * u)
                evacuate(f"rt_g{u}", "split", RG[:, 2 * u:2 * u + 2, :], ps[:, u % 2, :].rearrange("p (m t) -> p m t", m=2),
                         ACT.Silu)
            act.wait_ge(pool_done, at("pool", "raw_pad"))
            for u in range(7):
                uppers("m0", 19 + 2 * u, min(21 + 2 * u, M0_PANELS))
                act.wait_ge(splits_used, at("split", f"rw_p{u}"))
                if u >= 2:
                    act.wait_ge(dve_done, at("dve", f"rw_shift{u - 2}"))
                s.step(act.copy(RAW[:, u % 2, :, 1:T + 1], ps[:, u % 2, :].rearrange("p (m t) -> p m t", m=2)).then_inc(act_done, 1), f"rw_raw{u}")
            for h in range(4):
                evacuate(f"rt_pv{h}", "pe", RO[:, h, :], ps[:, 6 + h % 2, 0:T])
                plan["act", f"rt_o{h}"] = s.n
            act.wait_ge(dve_done, at("dve", "rw_shift6"))
            s.step(act.activation(P2[0:64, 12, :], P2[0:64, 12, :], ACT.Tanh).then_inc(act_done, 1))
            s.step(act.activation(P2[:, 13, :], P2[:, 13, :], ACT.Sigmoid).then_inc(act_done, 1), "rw_tanh")
            group_norm("rt", RO, GSQ, GRR, P, eps6)
            act.wait_ge(panels_done, at("panel", "rw_low"))
            for m in range(4):
                s.step(act.activation(LW[:, m * T:(m + 1) * T], ps[:, m // 2, (m % 2) * T:(m % 2 + 1) * T], ACT.Sigmoid,
                                      bias=v("w0", m)).then_inc(act_done, 1))
                s.step(act.activation(AA[:, m * T:(m + 1) * T], ps[:, 2 + m // 2, (m % 2) * T:(m % 2 + 1) * T],
                                      ACT.Sigmoid, bias=v("a0", m)).then_inc(act_done, 1), "rw_sig")
            for q in range(2):
                s.step(act.copy(RWG[:, 2 * q:2 * q + 2, :], ps[:, 4 + q, :].rearrange("p (m t) -> p m t", m=2)).then_inc(act_done, 1), "rw_g")
            for q in range(2):
                act.wait_ge(pe_done, at("pe", f"rw_kksum{q}"))
                s.step(act.activation(EX[:, q * 512:(q + 1) * 512], ps[:, 6 + q, :], ACT.Sqrt).then_inc(act_done, 1), f"rw_kkroot")
            act.wait_ge(dve_done, at("dve", "rw_scan"))
            s.step(act.activation(EP, LC, ACT.Exp).then_inc(act_done, 1), "rw_ep")
            s.step(act.activation(EN, LC, ACT.Exp, scale=-1.0).then_inc(act_done, 1), "rw_en")
            act.wait_ge(dve_done, at("dve", "rw_excl"))
            s.step(act.activation(EX, EX, ACT.Exp).then_inc(act_done, 1), "rw_ex")
            n = 0
            for dst in (VT, AT, BT, KTM):
                for t in range(2):
                    evacuate(f"rw_tm{n}", "pe", dst[:, t, :], ps[:, n % 2, :])
                    n += 1
            for t in range(2):
                for n in range(1, RW_LEVELS):
                    for q in range(2):
                        act.wait_ge(pe_done, at("pe", f"rw_x{t}_{n}_{q}"))
                        s.step(act.copy(H[:, 2 * q:2 * q + 2, LAT], ps[:, 3 * q, :].rearrange("p (a b) -> p a b", a=2)).then_inc(act_done, 1),
                               f"rw_x{t}_{n}_{q}")
                evacuate(f"rw_w1_{t}", "pe", W1, ps[:, 6, :])
                evacuate(f"rw_tv{t}", "pe", TV[:, t, :], ps[:, 7, :])
                evacuate(f"rw_ta{t}", "pe", TAT[:, :, t * P:(t + 1) * P], ps[:, 1, :].rearrange("p (m t) -> p m t", m=4))
            group_norm("rw", YR, WSQ, WRR, 64, eps_rw)
            act.wait_ge(panels_done, at("panel", "m0_out7"))
            squares("m0b", ACC, HL, KT)
            rms("m0b", T, D)
            xattn("x0", ("pool", "m0_x{}"), None)
            ffn("f1", ("pool", "x0_x{}"), None)
            ffn("f2", ("pool", "f1_x{}"), None)
            first_uppers("m1")
            plain_norm("m1", ("pool", "f2_x{}"), None)
            input_uppers("m1", HL, "m1ah{}", None)
            uppers("m1", 3, 5)
            act.wait_ge(splits_used, at("split", "ds_cq"))
            s.step(act.copy(CQ, ps[:, 0, :].rearrange("p (m t) -> p m t", m=2)).then_inc(act_done, 1), "ds_cq")
            uppers("m1", 5, 7)
            act.wait_ge(splits_used, at("split", "ds_ki"))
            s.step(act.copy(CKV, ps[:, 1, 0:T]).then_inc(act_done, 1), "ds_ckv")
            s.step(act.copy(KI, ps[:, 1, T:2 * T]).then_inc(act_done, 1), "ds_ki")
            uppers("m1", 7, 8)
            act.wait_ge(splits_used, at("split", "ds_w"))
            s.step(act.activation(WI, ps[:, 3, 0:16].rearrange("p (t h) -> p t h", t=2), ACT.Copy, scale=512 ** -0.5).then_inc(act_done, 1), "ds_w")
            act.wait_ge(act_done, s.n)
            for q in range(2):
                s.step(act.activation(SQD[:, q, :], CQ[:, q, :], ACT.Square).then_inc(act_done, 1), f"ds_sq{q}")
            s.step(act.activation(SQD[:, 2, :], CKV, ACT.Square).then_inc(act_done, 1), "ds_sq2")
            for u in range(6):
                dst = (SHH[:, 2 * u:2 * u + 2, :] if u < 2 else GB[:, 2 * u - 4:2 * u - 2, :] if u < 4 else
                       SU[:, 2 * u - 8:2 * u - 6, 2:T + 2])
                uppers("m1", 8 + 2 * u, min(10 + 2 * u, M1_PANELS))
                act.wait_ge(splits_used, at("split", f"sc_p{u}"))
                if u == 4:
                    act.wait_ge(pool_done, at("pool", "su_pad"))
                s.step(act.copy(dst, ps[:, 4 + u % 2, :].rearrange("p (m t) -> p m t", m=2)).then_inc(act_done, 1), f"sc_raw{u}")
            act.wait_ge(pe_done, at("pe", "ds_cqsum"))
            s.step(act.activation(RS[:, 0, 0:T], ps[:, 2, 0:T], ACT.Sqrt, bias=eps6, scale=1.0 / 256).then_inc(act_done, 1), "ds_cqrms")
            act.wait_ge(pe_done, at("pe", "ds_kvsum"))
            s.step(act.activation(RS[:, 1, 0:T], ps[:, 3, 0:T], ACT.Sqrt, bias=eps6, scale=1.0 / 128).then_inc(act_done, 1), "ds_kvrms")
            act.wait_ge(panels_done, at("panel", "ds_q"))
            for q in range(2):
                s.step(act.copy(DQ[:, 2 * q:2 * q + 2, :], ps[:, q, :].rearrange("p (m t) -> p m t", m=2)).then_inc(act_done, 1), "ds_q")
            act.wait_ge(panels_done, at("panel", "ds_qi"))
            for q in range(2):
                s.step(act.copy(QI[:, 2 * q:2 * q + 2, :], ps[:, 6 + q, :].rearrange("p (m t) -> p m t", m=2)).then_inc(act_done, 1), "ds_qi")
            evacuate("ds_ckt", "pe", CKT, ps[:, 4, 0:T].rearrange("p (l c) -> p l c", l=2))
            for u in range(16):
                h, t = u // 2, u % 2
                act.wait_ge(pe_done, at("pe", f"ds_l{u}"))
                if u >= 2:
                    act.wait_ge(dve_done, at("dve", f"ds_sc{u - 2}"))
                s.step(act.activation(RL[:, u % 2, 0:(t + 1) * P], ps[:, 4 + (h % 2) * 2 + t, 0:(t + 1) * P], ACT.Relu).then_inc(act_done, 1), f"ds_rl{u}")
            for h in range(8):
                evacuate(f"ds_ql{h}", "pe", QL[:, h, :], ps[:, 2 + h % 2, 0:T])
            attention("dsa", DSA_UNITS, 64 ** -0.5)
            act.wait_ge(panels_done, at("panel", "ds_uv"))
            for q in range(2):
                s.step(act.copy(Y[:, 2 * q:2 * q + 2, :], ps[:, q, :].rearrange("p (m t) -> p m t", m=2)).then_inc(act_done, 1), f"yc{q}")
            post_norm("m1", "panel", "m1_out7")
            xattn("x1", ("pool", "m1_x{}"), None)
            ffn("f3", ("pool", "x1_x{}"), None)
            act.wait_ge(pool_done, at("pool", "f3_x7"))
            act.dma_start(out, X[:, :, LAT]).then_inc(out_stored, 16)
            act.wait_ge(out_stored, 16)

        @block.vector
        def _(dve):
            s = Steps("dve", dve, plan)
            mod = lambda layer, which, k, g: MOD[:, layer * 48 + which * 8 + k, g:g + 1]

            def gain_shift(n, layer, gain, which):
                sc = MOD[:, layer * 48 + which * 8:layer * 48 + which * 8 + 8, :]
                s.step(dve.scalar_tensor_tensor(out=GS[:, n, :, :], in0=sc, scalar=1.0,
                                                in1=gain.unsqueeze(2).to_broadcast([P, KT, 2]),
                                                op0=ALU.add, op1=ALU.mult).then_inc(dve_done, 1))

            def invert(tag, width):
                dve.wait_ge(act_done, at("act", tag + "rms"))
                s.step(dve.reciprocal(RS[:, 0, 0:width], RS[:, 0, 0:width]).then_inc(dve_done, 1), tag + "inv")
                dve.wait_ge(dve_done, s.n)

            def mod_norm(tag, n, segs):
                t0 = min(segs) * T
                invert(tag, len(segs) * T)
                for k in range(KT):
                    for g in segs:
                        s.step(dve.scalar_tensor_tensor(
                            out=H[:, k, g * T:(g + 1) * T], in0=X[:, k, g * T:(g + 1) * T],
                            scalar=GS[:, n, k, g:g + 1], in1=RS[:, 0, g * T - t0:(g + 1) * T - t0],
                            op0=ALU.mult, op1=ALU.mult).then_inc(dve_done, 1), f"{tag}g{k}_{g}")

            def lower(tag, n, i=None):
                panel, split = at("panel", tag) + n, at("split", tag) + n
                dve.wait_ge(uppers_ready, split + 1 if i is None else split + 1 + i * TURN)
                dve.tensor_tensor(WS[:, split % HALVES, 1, :], ring[:, panel % RING, :],
                                  WS[:, split % HALVES, 0, :].bitcast(F32), ALU.subtract).then_inc(panels_done, 1)

            def first_lowers(tag):
                dve.wait_ge(panels_done, at("panel", tag))
                for n in range(HALVES):
                    lower(tag, n)

            def lowers(tag, first, last):
                for n in range(first, last):
                    lower(tag, n)

            def input_lowers(tag, src, bias=None):
                for k in range(KT):
                    dve.wait_ge(act_done, at("act", f"{tag}_u{k}"))
                    high = HS2[:, 0, k, :].bitcast(F32)
                    if bias:
                        ins = dve.scalar_tensor_tensor(out=HS2[:, 1, k, :], in0=src(k), scalar=bias(k), in1=high,
                                                       op0=ALU.add, op1=ALU.subtract)
                    else:
                        ins = dve.tensor_tensor(HS2[:, 1, k, :], src(k), high, ALU.subtract)
                    s.step(ins.then_inc(dve_done, 1), f"{tag}_l{k}")

            def hidden_dve(tag, tiles, kinds):
                s.base(tag)
                a0, d0, q0 = at("act", tag), s.n, at("split", tag)
                per = kinds + 1
                body = TURN // per

                def step_(t, i=None):
                    held = range(after_up(t, kinds) + HALVES, after_up(t + 1, kinds) + HALVES)
                    held = [n for n in held if n < per * tiles]
                    if held:
                        lower(tag, held[0], i)
                    dve.wait_ge(act_done, a0 + t + 1 if i is None else a0 + t + 1 + i * body)
                    step = lambda n: d0 + 3 * t + n if i is None else d0 + 3 * t + n + i * 3 * body
                    if i is not None or t >= 2:
                        used = q0 + per * (t - 1) + kinds
                        dve.wait_ge(splits_used, used if i is None else used + i * TURN)
                    other = ps[:, t % 2, (kinds - 1) * T:kinds * T]
                    s.step(dve.tensor_tensor(HT[:, t % 2, :], HS[:, t % 2, :], other, ALU.mult).then_inc(dve_done, 1))
                    dve.wait_ge(dve_done, step(1))
                    s.step(dve.tensor_copy(HTS[:, t % 2, 0, :], HT[:, t % 2, :]).then_inc(dve_done, 1))
                    dve.wait_ge(dve_done, step(2))
                    s.step(dve.tensor_tensor(HTS[:, t % 2, 1, :], HT[:, t % 2, :], HTS[:, t % 2, 0, :].bitcast(F32),
                                             ALU.subtract).then_inc(dve_done, 1))
                    for n in held[1:]:
                        lower(tag, n, i)

                for n in range(HALVES, after_up(0, kinds) + HALVES):
                    lower(tag, n)
                n = looped(tiles, per)
                step_(0)
                step_(1)
                with s.loop(n) as i:
                    for b in range(body):
                        step_(2 + b, i)
                for t in range(2 + n * body, tiles):
                    step_(t)

            def gated_add(src, gate, k, g, name):
                s.step(dve.scalar_tensor_tensor(out=X[:, k, g * T:(g + 1) * T], in0=src, scalar=gate,
                                                in1=X[:, k, g * T:(g + 1) * T], op0=ALU.mult, op1=ALU.add).then_inc(dve_done, 1), name)

            dve.wait_ge(inputs_in[1], 16)
            dve.wait_ge(pe_done, at("pe", f"mod_turned{FIRST_CHUNKS - 1}"))
            s.step(dve.tensor_tensor(MOD[:, 0:16, :], ps[:, 7, 0:32].rearrange("p (m g) -> p m g", g=2),
                                     v("b_mod", 0, 16).unsqueeze(2).to_broadcast([P, 16, 2]), ALU.add).then_inc(dve_done, 1), "mod_first")
            dve.wait_ge(dve_done, s.n)
            gain_shift(0, 0, v("norm1", 0, 8), 1)
            dve.wait_ge(inputs_in[2], 16)
            first_lowers("pw1")
            mod_norm("n0", 0, (0, 1))
            for k in range(KT):
                for g in range(2):
                    part = slice(g * T, (g + 1) * T)
                    dve.wait_ge(act_done, at("act", f"pw1_u{k}_{g}"))
                    s.step(dve.scalar_tensor_tensor(out=CH[:, 1, k, part], in0=H[:, k, part], scalar=mod(0, 0, k, g),
                                                    in1=CH[:, 0, k, part].bitcast(F32), op0=ALU.add,
                                                    op1=ALU.subtract).then_inc(dve_done, 1), f"pw1_l{k}")
            dve.wait_ge(pool_done, at("pool", "pad"))
            for j in range(KT):
                lowers("pw1", 2 * j + 3, min(2 * j + 5, 2 * KT))
                dve.wait_ge(act_done, at("act", f"sig{j}"))
                s.step(dve.tensor_tensor(U[:, j, :, PAD:PAD + T],
                                         ps[:, 2 * (j % 2), :].rearrange("p (g t) -> p g t", g=2),
                                         SG[:, j % 2, :].rearrange("p (g t) -> p g t", g=2), ALU.mult).then_inc(dve_done, 1), f"glu{j}")
            cv = lambda j: CV[:, j, :].rearrange("p (g t) -> p g t", g=2)
            for j0 in range(0, KT, 2):
                for tap in range(TAPS):
                    for j in (j0, j0 + 1):
                        src = U[:, j, :, tap:tap + T]
                        w = v("dw", tap * KT + j)
                        dve.wait_ge(dve_done, s.n - 1)
                        if tap == 0:
                            ins = dve.tensor_scalar(cv(j), src, w, v("dw_b", j), ALU.mult, ALU.add)
                        else:
                            ins = dve.scalar_tensor_tensor(out=cv(j), in0=src, scalar=w, in1=cv(j),
                                                           op0=ALU.mult, op1=ALU.add)
                        s.step(ins.then_inc(dve_done, 1), f"conv{j}" if tap == TAPS - 1 else None)
            dve.wait_ge(pe_done, at("pe", "ln_mean"))
            s.step(dve.tensor_scalar(RS[:, 1, :], ps[:, 0, :], 1.0 / D, None, ALU.mult).then_inc(dve_done, 1))
            dve.wait_ge(dve_done, s.n)
            for k in range(KT):
                s.step(dve.tensor_tensor(CV[:, k, :], CV[:, k, :], RS[:, 1, :], ALU.subtract).then_inc(dve_done, 1), f"ln_c{k}")
            first_lowers("pw2")
            dve.wait_ge(act_done, at("act", "ln_rms"))
            s.step(dve.reciprocal(RS[:, 0, :], RS[:, 0, :]).then_inc(dve_done, 1))
            dve.wait_ge(dve_done, s.n)
            for k in range(KT):
                s.step(dve.tensor_tensor(CV[:, k, :], CV[:, k, :], RS[:, 0, :], ALU.mult).then_inc(dve_done, 1), f"ln_n{k}")
            for k in range(KT):
                dve.wait_ge(act_done, at("act", f"pw2_u{k}"))
                s.step(dve.tensor_tensor(CH[:, 1, k, :], H[:, k, :], CH[:, 0, k, :].bitcast(F32),
                                         ALU.subtract).then_inc(dve_done, 1), f"pw2_l{k}")
            dve.wait_ge(pe_done, at("pe", f"mod_turned{MOD_CHUNKS - 1}"))
            s.step(dve.tensor_tensor(MOD[:, 16:96, :], ps[:, 7, 32:192].rearrange("p (m g) -> p m g", g=2),
                                     v("b_mod", 16, 80).unsqueeze(2).to_broadcast([P, 80, 2]), ALU.add).then_inc(dve_done, 1), "mod_rest")
            dve.wait_ge(dve_done, s.n)
            gain_shift(1, 0, v("norm2", 0, 8), 4)
            gain_shift(2, 1, v("norm1", 8, 8), 1)
            gain_shift(3, 1, v("norm2", 8, 8), 4)
            for j in range(KT):
                if j + HALVES < KT:
                    lower("pw2", j + HALVES)
                else:
                    lower("mlp0c", j + HALVES - KT)
                dve.wait_ge(splits_used, at("split", f"pw2_{j}"))
                gated_add(ps[:, j % 2, 0:T], mod(0, 2, j, 0), j, 0, None)
                gated_add(ps[:, j % 2, T:2 * T], mod(0, 2, j, 1), j, 1, f"pw2_{j}")
            mod_norm("n1", 1, (0, 1))
            s.base("mlp0c.acc_free")
            input_lowers("mlp0c", lambda k: H[:, k, 0:T], lambda k: mod(0, 3, k, 0))
            hidden_dve("mlp0c", FF1_TILES, 1)
            input_lowers("mlp0l", lambda k: H[:, k, LAT], lambda k: mod(0, 3, k, 1))
            first_lowers("mlp0l")
            dve.wait_ge(splits_used, at("split", "mlp0c.last"))
            for k in range(KT):
                gated_add(ACC(k), mod(0, 5, k, 0), k, 0, f"mlp0c_x{k}")
            s.base("mlp0l.acc_free")
            hidden_dve("mlp0l", FF1_TILES, 1)
            dve.wait_ge(splits_used, at("split", "mlp0l.last"))
            for k in range(KT):
                gated_add(ACC(k), mod(0, 5, k, 1), k, 1, f"mlp0l_x{k}")
            mod_norm("n2", 2, (0, 1))
            for u in range(10):
                if u < 8:
                    dve.wait_ge(act_done, at("act", f"kq_rms{u}"))
                    s.step(dve.reciprocal(KQR[:, u % 2, :], KQR[:, u % 2, :]).then_inc(dve_done, 1))
                    dve.wait_ge(dve_done, s.n)
                    s.step(dve.scalar_tensor_tensor(out=KQ[:, u, :], in0=KQ[:, u, :], scalar=v("gqa_k" if u < 4 else "gqa_q"),
                                                    in1=KQR[:, u % 2, :], op0=ALU.mult, op1=ALU.mult).then_inc(dve_done, 1), f"kq_norm{u}")
                w = u - 2
                if w >= 0:
                    dve.wait_ge(pe_done, at("pe", f"kq_rot{w}"))
                    if w >= 2:
                        dve.wait_ge(pool_done, at("pool", f"kq_cos{w - 2}"))
                    for half in range(2):
                        sin = c("gqa_sin")[:, half * T:(half + 1) * T] if w < 4 else c("gqa_sin")[:, T:2 * T]
                        ins = dve.tensor_tensor(ROT[:, w % 2, half * T:(half + 1) * T], ps[:, 6 + w % 2, half * T:(half + 1) * T],
                                                sin, ALU.mult)
                        s.step(ins.then_inc(dve_done, 1), f"kq_sin{w}" if half else None)

            def attention(tag, units, scale, out_src, out_dst, bias=None):
                for u in range(len(units) + 3):
                    if u < len(units):
                        L = units[u][2] * P
                        dve.wait_ge(pe_done, at("pe", f"{tag}_s{u}"))
                        if bias is not None:
                            if u >= 2:
                                dve.wait_ge(act_done, at("act", f"{tag}_exp{u - 2}"))
                            s.step(dve.tensor_tensor(SBI[:, u % 2, 0:L], ps[:, u % 4, 0:L], bias(u), ALU.add).then_inc(dve_done, 1), f"{tag}_bias{u}")
                            dve.wait_ge(dve_done, s.n)
                            src = SBI[:, u % 2, 0:L]
                        else:
                            src = ps[:, u % 4, 0:L]
                        s.step(dve.reduce_max(AS[:, u % 64, 2:3], src, AX).then_inc(dve_done, 1))
                        dve.wait_ge(dve_done, s.n)
                        s.step(dve.tensor_scalar(AS[:, u % 64, 0:1], AS[:, u % 64, 2:3], -scale, None, ALU.mult).then_inc(dve_done, 1),
                               f"{tag}_max{u}")
                    if 1 <= u <= len(units):
                        w = u - 1
                        L = units[w][2] * P
                        dve.wait_ge(act_done, at("act", f"{tag}_exp{w}"))
                        s.step(dve.reciprocal(AS[:, w % 64, 3:4], AS[:, w % 64, 1:2]).then_inc(dve_done, 1))
                        dve.wait_ge(dve_done, s.n)
                        s.step(dve.tensor_scalar(PR[:, w % 3, 0:L], PR[:, w % 3, 0:L], AS[:, w % 64, 3:4], None,
                                                 ALU.mult).then_inc(dve_done, 1), f"{tag}_p{w}")
                    w = u - 3
                    if w >= 0 and w % 2:
                        dve.wait_ge(pe_done, at("pe", f"{tag}_pv{w}"))
                        s.step(dve.tensor_copy(out_dst(w), out_src(w)).then_inc(dve_done, 1), f"{tag}_o{w}")

            def head_rows(w):
                lo = lo_of(GQA_UNITS[w][0])
                return slice(lo, lo + 64)

            attention("gqa", GQA_UNITS, 64 ** -0.5, lambda w: ps[head_rows(w), 6 + w // 2 % 2, 0:T],
                      lambda w: GO[head_rows(w), w // 4, :])
            for j in range(KT):
                dve.wait_ge(panels_done, at("panel", f"wo_{j}"))
                gated_add(ps[:, j % 2, 0:T], mod(1, 2, j, 1), j, 1, f"wo_{j}")
            first_lowers("mlp1")
            mod_norm("n3", 3, (1,))
            s.base("mlp1.acc_free")
            input_lowers("mlp1", lambda k: H[:, k, LAT], lambda k: mod(1, 3, k, 1))
            hidden_dve("mlp1", FF1_TILES, 1)
            dve.wait_ge(splits_used, at("split", "mlp1.last"))
            for k in range(KT):
                gated_add(ACC(k), mod(1, 5, k, 1), k, 1, f"mlp1_x{k}")

            def plain_norm(tag, which):
                invert(tag + "a", T)
                for k in range(KT):
                    s.step(dve.scalar_tensor_tensor(out=H[:, k, LAT], in0=X[:, k, LAT], scalar=v("norm_g", which * 8 + k),
                                                    in1=RS[:, 0, 0:T], op0=ALU.mult, op1=ALU.mult).then_inc(dve_done, 1), f"{tag}ah{k}")

            def post_norm(tag, gain):
                invert(tag + "b", T)
                for k in range(KT):
                    s.step(dve.scalar_tensor_tensor(out=TMP[:, k, :], in0=ACC(k), scalar=gain(k), in1=RS[:, 0, 0:T],
                                                    op0=ALU.mult, op1=ALU.mult).then_inc(dve_done, 1), f"{tag}_t{k}")

            def ffn(tag, layer, first, half):
                first_lowers(tag)
                plain_norm(tag, layer * 8 + first)
                s.base(tag + ".acc_free")
                input_lowers(tag, lambda k: H[:, k, LAT])
                hidden_dve(tag, FF2_TILES, 2)
                post_norm(tag, lambda k: HG[:, half, k:k + 1])

            def xattn(tag, layer):
                plain_norm(tag, layer * 8 + 4)
                attention(tag, XA_UNITS, P ** -0.5, lambda w: ps[:, 6 + w // 2 % 2, 0:T], lambda w: XO[:, w // 2, :])
                post_norm(tag, lambda k: v("norm_g", (layer * 8 + 5) * 8 + k))

            def group_norm(tag, buf, rr, n, gain, shift):
                for q in range(2):
                    dve.wait_ge(pe_done, at("pe", f"{tag}_mean{q}"))
                    pairs = buf[:, 2 * q:2 * q + 2, :]
                    s.step(dve.scalar_tensor_tensor(out=pairs, in0=ps[:, q, :].rearrange("p (m t) -> p m t", m=2),
                                                    scalar=-1.0 / n, in1=pairs, op0=ALU.mult, op1=ALU.add).then_inc(dve_done, 1), f"{tag}_cen{q}")
                for q in range(2):
                    dve.wait_ge(act_done, at("act", f"{tag}_rms{q}"))
                    pairs = buf[:, 2 * q:2 * q + 2, :]
                    s.step(dve.reciprocal(rr[:, q, :], rr[:, q, :]).then_inc(dve_done, 1))
                    dve.wait_ge(dve_done, s.n)
                    s.step(dve.tensor_tensor(pairs, pairs, rr[:, q, :].rearrange("p (m t) -> p m t", m=2), ALU.mult).then_inc(dve_done, 1))
                    dve.wait_ge(dve_done, s.n)
                    for m in (2 * q, 2 * q + 1):
                        s.step(dve.tensor_scalar(buf[:, m, :], buf[:, m, :], v(gain, m), v(shift, m), ALU.mult, ALU.add).then_inc(dve_done, 1))
                dve.wait_ge(dve_done, s.n)

            for n, which in enumerate((1, 7, 9, 15)):
                s.step(dve.tensor_scalar(HG[:, n, :], v("norm_g", which * 8, 8), 0.5, None, ALU.mult).then_inc(dve_done, 1))
            invert("mem", T)
            for k in range(KT):
                s.step(dve.scalar_tensor_tensor(out=MEMN[:, k, :], in0=MEMN[:, k, :], scalar=v("mem_g", k),
                                                in1=RS[:, 0, 0:T], op0=ALU.mult, op1=ALU.mult).then_inc(dve_done, 1), "mem_n")
            ffn("f0", 0, 0, 0)
            first_lowers("m0")
            plain_norm("m0", 2)
            s.base("m0_acc_free")
            input_lowers("m0", lambda k: H[:, k, LAT])
            lowers("m0", HALVES, 19)
            for u in range(7):
                lowers("m0", 19 + 2 * u, min(21 + 2 * u, M0_PANELS))
                dve.wait_ge(act_done, at("act", f"rw_raw{u}"))
                now = RAW[:, u % 2, :, 1:T + 1]
                s.step(dve.tensor_tensor(P2[:, 2 * u:2 * u + 2, :], RAW[:, u % 2, :, 0:T], now, ALU.subtract).then_inc(dve_done, 1))
                dve.wait_ge(dve_done, s.n)
                for m in range(2):
                    p2 = P2[:, 2 * u + m, :]
                    s.step(dve.scalar_tensor_tensor(out=p2, in0=p2, scalar=v("rw_mu", 2 * u + m), in1=now[:, m, :],
                                                    op0=ALU.mult, op1=ALU.add).then_inc(dve_done, 1), f"rw_shift{u}")
            plan["dve", "rw_p2"] = s.n
            for u in range(4):
                dve.wait_ge(pe_done, at("pe", f"rt_rot{u}"))
                if u >= 2:
                    dve.wait_ge(pool_done, at("pool", f"rt_cos{u - 2}"))
                s.step(dve.tensor_tensor(RROT[:, u % 2, :].rearrange("p (m t) -> p m t", m=2),
                                         ps[:, 2 + u % 2, :].rearrange("p (m t) -> p m t", m=2),
                                         c("rt_sin").unsqueeze(1).to_broadcast([P, 2, T]), ALU.mult).then_inc(dve_done, 1), f"rt_sin{u}")
            for h in range(4):
                dve.wait_ge(pe_done, at("pe", f"rt_s{h}"))
                if h >= 2:
                    dve.wait_ge(pe_done, at("pe", f"rt_pv{h - 2}"))
                decay = c("rt_decay")[:, h * T:(h + 1) * T]
                s.step(dve.tensor_tensor(RP[:, h % 2, 0:T], ps[:, 4 + h % 2, 0:T], decay, ALU.mult).then_inc(dve_done, 1))
                s.step(dve.tensor_tensor(RP[:, h % 2, T:T + P], ps[:, 4 + h % 2, T:T + P], decay[:, 0:P], ALU.mult).then_inc(dve_done, 1), f"rt_p{h}")
            group_norm("rt", RO, GRR, P, "rt_g", "rt_b")
            dve.wait_ge(act_done, at("act", "rt_g1"))
            for m in range(4):
                s.step(dve.tensor_tensor(Y[:, 4 + m, :], RO[:, m, :], RG[:, m, :], ALU.mult).then_inc(dve_done, 1), f"yb{m}")
            plan["dve", "rt_gn"] = s.n
            dve.wait_ge(dve_done, s.n)
            r4, k4, v4 = P2[:, 0:4, :], P2[:, 4:8, :], P2[:, 8:12, :]
            four = lambda ap: ap.rearrange("p (m t) -> p m t", m=4)
            for m in range(4):
                s.step(dve.tensor_scalar(KK[:, m * T:(m + 1) * T], P2[:, 4 + m, :], v("k_k", m), None, ALU.mult).then_inc(dve_done, 1))
            dve.wait_ge(dve_done, s.n)
            s.step(dve.tensor_tensor(EX, KK, KK, ALU.mult).then_inc(dve_done, 1), "rw_kk2")
            dve.wait_ge(act_done, at("act", "rw_sig"))
            for m in range(4):
                s.step(dve.tensor_scalar(KP[:, m * T:(m + 1) * T], AA[:, m * T:(m + 1) * T], 1.0, v("k_a", m),
                                         ALU.subtract, ALU.mult).then_inc(dve_done, 1))
            dve.wait_ge(dve_done, s.n)
            s.step(dve.scalar_tensor_tensor(out=four(KP), in0=four(KP), scalar=1.0, in1=k4, op0=ALU.add, op1=ALU.mult).then_inc(dve_done, 1))
            s.step(dve.tensor_scalar(EN, LW, -float(np.exp(-0.5)), None, ALU.mult).then_inc(dve_done, 1))
            dve.wait_ge(pool_done, at("pool", "reset"))
            dve.wait_ge(dve_done, s.n)
            s.step(dve.tensor_tensor_scan(LC, RESET, EN, 0.0, ALU.mult, ALU.add).then_inc(dve_done, 1), "rw_scan0")
            dve.wait_ge(dve_done, s.n)
            s.step(dve.tensor_tensor(four(LW), r4, four(KP), ALU.mult).then_inc(dve_done, 1))
            dve.wait_ge(dve_done, s.n)
            for m in range(4):
                s.step(dve.tensor_scalar(LW[:, m * T:(m + 1) * T], LW[:, m * T:(m + 1) * T], v("r_k", m), None, ALU.mult).then_inc(dve_done, 1), "rw_rk")
            dve.wait_ge(act_done, at("act", "rw_kkroot"))
            s.step(dve.tensor_scalar(EX, EX, 1e-12, None, ALU.max).then_inc(dve_done, 1))
            dve.wait_ge(dve_done, s.n)
            s.step(dve.reciprocal(EX, EX).then_inc(dve_done, 1))
            dve.wait_ge(dve_done, s.n)
            s.step(dve.tensor_tensor(KK, KK, EX, ALU.mult).then_inc(dve_done, 1), "rw_kkn")
            dve.wait_ge(dve_done, s.n)
            s.step(dve.tensor_tensor(EX, LC, EN, ALU.subtract).then_inc(dve_done, 1), "rw_excl")
            plan["dve", "rw_scan"] = s.n
            s.step(dve.tensor_tensor(AA, AA, KK, ALU.mult).then_inc(dve_done, 1))
            for q in range(2):
                dve.wait_ge(pe_done, at("pe", f"rw_bon{q}"))
                s.step(dve.tensor_tensor(BON[:, 2 * q:2 * q + 2, :], ps[:, 4 + q, :].rearrange("p (m t) -> p m t", m=2),
                                         P2[:, 8 + 2 * q:10 + 2 * q, :], ALU.mult).then_inc(dve_done, 1), "rw_bonus")
            dve.wait_ge(act_done, at("act", "rw_ep"))
            dve.wait_ge(pe_done, at("pe", "rt_mean1"))
            s.step(dve.tensor_tensor(AR[:, :, 1, :], r4, four(EP), ALU.mult).then_inc(dve_done, 1), "rw_rhat")
            s.step(dve.tensor_copy(PC, four(EP).rearrange("p m (c t) -> p m c t", c=4)[:, :, :, RW_C - 1]).then_inc(dve_done, 1), "rw_pc")
            dve.wait_ge(act_done, at("act", "rw_en"))
            dve.wait_ge(dve_done, s.n)
            s.step(dve.tensor_tensor(BF, four(AA), four(EN), ALU.mult).then_inc(dve_done, 1))
            s.step(dve.tensor_tensor(KF, four(KP), four(EN), ALU.mult).then_inc(dve_done, 1))
            dve.wait_ge(act_done, at("act", "rw_ex"))
            s.step(dve.scalar_tensor_tensor(out=AR[:, :, 0, :], in0=four(KK), scalar=-1.0, in1=four(EX), op0=ALU.mult,
                                            op1=ALU.mult).then_inc(dve_done, 1), "rw_ahat")
            dve.wait_ge(dve_done, s.n)
            for src, dst, name in ((BF, BC, "rw_bc"), (KF, KC, "rw_kc")):
                for m in range(4):
                    s.step(dve.tensor_tensor(dst[:, m, :].rearrange("p (c t) -> p c t", c=4),
                                             src[:, m, :].rearrange("p (c t) -> p c t", c=4),
                                             PC[:, m, :].unsqueeze(2).to_broadcast([P, 4, RW_C]), ALU.mult).then_inc(dve_done, 1), name)
            masks = c("rw_mask").rearrange("p (x y t) -> p x y t", x=2, y=2)
            for t in range(2):
                for h in range(8):
                    u = t * 8 + h
                    dve.wait_ge(pe_done, at("pe", f"rw_mm{u}"))
                    if h == 0 and t:
                        dve.wait_ge(pe_done, at("pe", "rw_w1_0"))
                        dve.wait_ge(pool_done, at("pool", f"rw_al0_{RW_LEVELS - 1}_1"))
                    got = ps[:, 4 + h % 4, :].rearrange("p (x y t) -> p x y t", x=2, y=2)
                    s.step(dve.tensor_tensor(MA[:, h, :, :], got[:, :, 0, :], masks[:, :, 0, :], ALU.mult).then_inc(dve_done, 1), f"rw_ma{u}")
                    s.step(dve.tensor_tensor(MR[:, u, :, :], got[:, :, 1, :], masks[:, :, 1, :], ALU.mult).then_inc(dve_done, 1), f"rw_mm{u}")
                for n in range(RW_LEVELS):
                    for q in range(2):
                        hs = slice(4 * q, 4 * q + 4)
                        eye = ident.unsqueeze(1).to_broadcast([P, 4, P])
                        bank = lambda b: ps[:, 3 * q + b, :].rearrange("p (h t) -> p h t", h=4)
                        if n == 0:
                            dve.wait_ge(pe_done, at("pe", f"rw_x{t}_{n}_{q}"))
                            if t and q == 0:
                                dve.wait_ge(pe_done, at("pe", "rw_ta0"))
                            s.step(dve.tensor_tensor(TI[:, hs, :], bank(0), eye, ALU.add).then_inc(dve_done, 1))
                            s.step(dve.tensor_tensor(TT[:, hs, :], AL[:, hs, :], eye, ALU.add).then_inc(dve_done, 1), f"rw_t{t}_{n}_{q}")
                            continue
                        if n < RW_LEVELS - 1:
                            dve.wait_ge(pe_done, at("pe", f"rw_dt{t}_{n}_{q}"))
                            dve.wait_ge(dve_done, s.n)
                            s.step(dve.tensor_tensor(TI[:, hs, :], TI[:, hs, :], bank(1), ALU.add).then_inc(dve_done, 1))
                        dve.wait_ge(pe_done, at("pe", f"rw_dtt{t}_{n}_{q}"))
                        dve.wait_ge(dve_done, s.n)
                        s.step(dve.tensor_tensor(TT[:, hs, :], TT[:, hs, :], bank(2), ALU.add).then_inc(dve_done, 1), f"rw_t{t}_{n}_{q}")
            s.step(dve.memset(SK[:, 0, :, :], 0.0).then_inc(dve_done, 1))
            for ch in range(4):
                t, lo = ch // 2, 64 * (ch % 2)
                rows = slice(lo, lo + 64)
                ub, tv = (ap.rearrange("p (m x) v -> p x m v", x=2) for ap in
                          (UB[rows, t, :, :], TV[rows, t, :].rearrange("p (h v) -> p h v", h=8)))
                if ch == 0:
                    dve.wait_ge(act_done, at("act", "rw_ta1"))
                    s.step(dve.tensor_copy(ub[:, 0, :, :], tv[:, 0, :, :]).then_inc(dve_done, 1))
                    s.step(dve.tensor_copy(ub[:, 1, :, :], tv[:, 1, :, :]).then_inc(dve_done, 1), "rw_u0")
                else:
                    dve.wait_ge(pe_done, at("pe", f"rw_u{ch}"))
                    for x in range(2):
                        s.step(dve.tensor_tensor(ub[:, x, :, :], ps[rows, 2 + x, 0:T].rearrange("p (m v) -> p m v", m=4),
                                                 tv[:, x, :, :], ALU.add).then_inc(dve_done, 1), f"rw_u{ch}")
                if ch < 3:
                    dve.wait_ge(dve_done, s.n)
                    s.step(dve.tensor_tensor(SKP, SK[:, ch, :, :], PC[:, :, ch:ch + 1].to_broadcast([P, 4, 64]), ALU.mult).then_inc(dve_done, 1))
                    dve.wait_ge(pe_done, at("pe", f"rw_s{ch + 1}"))
                    dve.wait_ge(dve_done, s.n)
                    s.step(dve.tensor_tensor(SK[:, ch + 1, :, :], ps[:, 4 + ch % 2, 0:T].rearrange("p (m v) -> p m v", m=4),
                                             SKP, ALU.add).then_inc(dve_done, 1), f"rw_s{ch + 1}")
                if ch % 2:
                    dve.wait_ge(pe_done, at("pe", f"rw_y{t}"))
                    for x in range(2):
                        half = slice(64 * x, 64 * x + 64)
                        s.step(dve.tensor_copy(YR[half, :, t * P:(t + 1) * P],
                                               ps[half, 6 + x, :].rearrange("p (m t) -> p m t", m=4)).then_inc(dve_done, 1), f"rw_y{t}")
            dve.wait_ge(dve_done, s.n)
            group_norm("rw", YR, WRR, 64, "rw_g", "rw_b")
            dve.wait_ge(act_done, at("act", "rw_g"))
            s.step(dve.tensor_tensor(YR, YR, BON, ALU.add).then_inc(dve_done, 1))
            dve.wait_ge(dve_done, s.n)
            for m in range(4):
                s.step(dve.tensor_tensor(Y[:, m, :], YR[:, m, :], RWG[:, m, :], ALU.mult).then_inc(dve_done, 1), f"ya{m}")
            dve.wait_ge(dve_done, s.n)
            post_norm("m0", lambda k: v("norm_g", 3 * 8 + k))
            xattn("x0", 0)
            ffn("f1", 0, 6, 1)
            ffn("f2", 1, 0, 2)
            first_lowers("m1")
            plain_norm("m1", 10)
            s.base("m1_acc_free")
            input_lowers("m1", lambda k: H[:, k, LAT])
            lowers("m1", HALVES, M1_PANELS)
            dve.wait_ge(act_done, at("act", "ds_kvrms"))
            s.step(dve.reciprocal(RS[:, :, 0:T], RS[:, :, 0:T]).then_inc(dve_done, 1))
            dve.wait_ge(dve_done, s.n)
            for q in range(2):
                s.step(dve.scalar_tensor_tensor(out=CQ[:, q, :], in0=CQ[:, q, :], scalar=v("dsa_q", q), in1=RS[:, 0, 0:T],
                                                op0=ALU.mult, op1=ALU.mult).then_inc(dve_done, 1), "ds_cqn")
            s.step(dve.scalar_tensor_tensor(out=CKV, in0=CKV, scalar=v("dsa_kv"), in1=RS[:, 1, 0:T], op0=ALU.mult,
                                            op1=ALU.mult).then_inc(dve_done, 1), "ds_ckvn")
            for u in range(16):
                h, t = u // 2, u % 2
                L = (t + 1) * P
                dve.wait_ge(act_done, at("act", f"ds_rl{u}"))
                if h == 0:
                    ins = dve.tensor_scalar(SCO[:, t, 0:L], RL[:, u % 2, 0:L], WI[:, t, h:h + 1], None, ALU.mult)
                else:
                    dve.wait_ge(dve_done, s.n - 1)
                    ins = dve.scalar_tensor_tensor(out=SCO[:, t, 0:L], in0=RL[:, u % 2, 0:L], scalar=WI[:, t, h:h + 1],
                                                   in1=SCO[:, t, 0:L], op0=ALU.mult, op1=ALU.add)
                s.step(ins.then_inc(dve_done, 1), f"ds_sc{u}")
            dve.wait_ge(dve_done, s.n)
            mask = [c("causal")[:, 0:P], c("causal")[:, P:3 * P]]
            for t in range(2):
                L = (t + 1) * P
                s.step(dve.tensor_tensor(WK[:, t, 0:L], SCO[:, t, 0:L], mask[t], ALU.add).then_inc(dve_done, 1))
            for n in range(TOPK // 8):
                for t in range(2):
                    dve.wait_ge(dve_done, s.n - 1)
                    s.step(dve.max(TOP[:, t, :], WK[:, t, 0:(t + 1) * P]).then_inc(dve_done, 1))
                for t in range(2):
                    dve.wait_ge(dve_done, s.n - 1)
                    row = WK[:, t, 0:(t + 1) * P]
                    s.step(dve.match_replace(row, TOP[:, t, :], row, TAKEN).then_inc(dve_done, 1))
            dve.wait_ge(dve_done, s.n)
            for t in range(2):
                L = (t + 1) * P
                s.step(dve.tensor_scalar(BI[:, t, 0:L], WK[:, t, 0:L], TAKEN, NEG, ALU.not_equal, ALU.mult).then_inc(dve_done, 1))
                dve.wait_ge(dve_done, s.n)
                s.step(dve.tensor_tensor(BI[:, t, 0:L], BI[:, t, 0:L], mask[t], ALU.add).then_inc(dve_done, 1))
            dve.wait_ge(dve_done, s.n)
            attention("dsa", DSA_UNITS, 64 ** -0.5, lambda w: ps[:, 6 + w // 2 % 2, 0:T], lambda w: OL[:, w // 2, :],
                      bias=lambda u: BI[:, u % 2, 0:(u % 2 + 1) * P])
            dve.wait_ge(act_done, at("act", "sc_raw5"))
            s.step(dve.tensor_tensor(SU[:, :, 2:T + 2], SU[:, :, 2:T + 2], SHH, ALU.mult).then_inc(dve_done, 1))
            dve.wait_ge(dve_done, s.n)
            for m in range(4):
                y = Y[:, 4 + m, :]
                s.step(dve.tensor_scalar(y, SU[:, m, 0:T], v("sc_w", m), v("sc_b", m), ALU.mult, ALU.add).then_inc(dve_done, 1))
                for tap in (1, 2):
                    dve.wait_ge(dve_done, s.n)
                    s.step(dve.scalar_tensor_tensor(out=y, in0=SU[:, m, tap:tap + T], scalar=v("sc_w", 4 * tap + m), in1=y,
                                                    op0=ALU.mult, op1=ALU.add).then_inc(dve_done, 1))
                dve.wait_ge(dve_done, s.n)
                s.step(dve.tensor_tensor(y, y, GB[:, m, :], ALU.mult).then_inc(dve_done, 1), f"yd{m}")
            post_norm("m1", lambda k: v("norm_g", 11 * 8 + k))
            xattn("x1", 1)
            ffn("f3", 1, 6, 3)

        @block.gpsimd
        def _(pool):
            s = Steps("pool", pool, plan)
            s.step(pool.memset(U[:, :, :, :], 0.0).then_inc(pool_done, 1), "pad")
            pool.wait_ge(inputs_in[0], 16)
            for u in range(8):
                pool.wait_ge(pe_done, at("pe", f"kq_rot{u}"))
                for half in range(2):
                    cos = c("gqa_cos")[:, half * T:(half + 1) * T] if u < 4 else c("gqa_cos")[:, T:2 * T]
                    q = KQ[:, u, half * T:(half + 1) * T]
                    s.step(pool.tensor_tensor(q, q, cos, ALU.mult).then_inc(pool_done, 1))
                pool.wait_ge(dve_done, at("dve", f"kq_sin{u}"))
                pool.wait_ge(pool_done, s.n)
                s.step(pool.tensor_tensor(KQ[:, u, :], KQ[:, u, :], ROT[:, u % 2, :], ALU.add).then_inc(pool_done, 1), f"kq_cos{u}")

            def add_x(tag):
                for k in range(KT):
                    pool.wait_ge(dve_done, at("dve", f"{tag}_t{k}"))
                    s.step(pool.tensor_tensor(X[:, k, LAT], X[:, k, LAT], TMP[:, k, :], ALU.add).then_inc(pool_done, 1), f"{tag}_x{k}")

            add_x("f0")
            s.step(pool.memset(RAW[:, :, :, :], 0.0).then_inc(pool_done, 1), "raw_pad")
            s.step(pool.memset(RESET, 1.0).then_inc(pool_done, 1))
            pool.wait_ge(pool_done, s.n)
            s.step(pool.memset(RESET.rearrange("p (c t) -> p c t", t=RW_C)[:, :, 0:1], 0.0).then_inc(pool_done, 1), "reset")
            for u in range(4):
                pool.wait_ge(pe_done, at("pe", f"rt_rot{u}"))
                qk = RQK[:, u, :].rearrange("p (m t) -> p m t", m=2)
                s.step(pool.tensor_tensor(qk, qk, c("rt_cos").unsqueeze(1).to_broadcast([P, 2, T]), ALU.mult).then_inc(pool_done, 1))
                pool.wait_ge(dve_done, at("dve", f"rt_sin{u}"))
                pool.wait_ge(pool_done, s.n)
                s.step(pool.tensor_tensor(RQK[:, u, :], RQK[:, u, :], RROT[:, u % 2, :], ALU.add).then_inc(pool_done, 1), f"rt_cos{u}")
            for t in range(2):
                for n in range(RW_LEVELS):
                    for q in range(2):
                        pool.wait_ge(dve_done, at("dve", f"rw_ma{t * 8 + 4 * q + 3}"))
                        if n:
                            pool.wait_ge(pe_done, at("pe", f"rw_x{t}_{n - 1}_{q}"))
                            pool.wait_ge(dve_done, at("dve", f"rw_t{t}_0_{q}"))
                        elif t:
                            pool.wait_ge(pe_done, at("pe", f"rw_x0_{RW_LEVELS - 1}_{q}"))
                        level = c("rw_level")[:, n * P:(n + 1) * P].unsqueeze(1).to_broadcast([P, 4, P])
                        s.step(pool.tensor_tensor(AL[:, 4 * q:4 * q + 4, :], MA[:, 4 * q:4 * q + 4, 0, :], level, ALU.mult).then_inc(pool_done, 1),
                               f"rw_al{t}_{n}_{q}")
            add_x("m0")
            add_x("x0")
            add_x("f1")
            s.step(pool.memset(SU[:, :, 0:2], 0.0).then_inc(pool_done, 1), "su_pad")
            add_x("f2")
            add_x("m1")
            add_x("x1")
            add_x("f3")


INPUTS = ("c", "c_ctx", "x", "ctx", "mem_2")


def prepare(inputs):
    a = {k: np.asarray(x) for k, x in inputs.items()}
    return {
        "const": constant_arrays(),
        "vec": vector_columns(a),
        "xs": np.ascontiguousarray(np.concatenate([feature_major(a["ctx"]), feature_major(a["x"])], 2)),
        "mem": feature_major(a["mem_2"]),
        "weights": weight_stream(a),
    }


def make(bacc, arrays):
    plan = {}
    for _ in range(2):
        nc = bacc.Bacc("TRN2", target_bir_lowering=False, num_devices=1)
        ins = [nc.dram_tensor(n, arrays[n].shape, F32, kind="ExternalInput").ap() for n in arrays]
        out = nc.dram_tensor("y", (P, KT, T), F32, kind="ExternalOutput").ap()
        build(nc, *ins, out, plan)
    return nc, plan


def kernel(**inputs):
    import concourse.bacc as bacc
    from concourse.bass_utils import run_bass_kernel_spmd as run

    arrays = prepare(inputs)
    nc, _ = make(bacc, arrays)
    y = run(nc, [arrays], core_ids=[0]).results[0]["y"]
    return np.ascontiguousarray(y.transpose(2, 1, 0)).reshape(1, T, D)
```
